# Optimizing a Trainium2 kernel written in Bass

```python
import jax, jax.numpy as jnp
from jax import lax
import numpy as np

D_MODEL = 1024
BATCH = 1
SEQ = 128
DEPTH = 1
DEC_BATCH = 1
DEC_SEQ = 1024
PAST_LEN = 128

GRID_W = 64
EPS = 1e-6
NEG_INF = -1e30
NA_HEADS = 6
NA_DIM = 64
NA_WIDTH = NA_HEADS * NA_DIM
NA_ROWS = 8
NA_COLS = 16
NA_QBLOCK = 16
NA_KBLOCK = 32
RPB_ROWS = 2 * NA_ROWS - 1
RPB_COLS = 2 * NA_COLS - 1
CTX_QBLOCK = 128
ML_HEADS = 4
ML_DIM = 96
ML_WIDTH = ML_HEADS * ML_DIM
ML_CHUNK = 64
ML_FORGET_BIAS = 3.0
POOL_WINDOWS = (2, 4, 8, 16)
POOL_GROUPS = 4
POOL_DIM = 64
POOL_WIDTH = POOL_GROUPS * POOL_DIM
MIX_WIDTH = NA_WIDTH + ML_WIDTH + POOL_WIDTH
N_GATE_COLS = 4 * ML_HEADS
IN_COLS = 3 * NA_WIDTH + 4 * ML_WIDTH + N_GATE_COLS + POOL_WIDTH
N_EXPERTS = 16
N_EXPERT_GROUPS = 4
EXPERTS_PER_GROUP = N_EXPERTS // N_EXPERT_GROUPS
TOP_K = 2
D_EXPERT = 512
ADA_DIM = 6 * D_MODEL

kernel_name = 'hybrid_na_mlstm_pool_moe_diffusion_step'

def _in_split_points():
    sizes = [NA_WIDTH] * 3 + [ML_WIDTH] * 4 + [N_GATE_COLS]
    pts, acc = [], 0
    for s in sizes:
        acc += s
        pts.append(acc)
    return pts

def rms_norm(x, g):
    xf = x.astype(jnp.float32)
    y = xf * lax.rsqrt(jnp.mean(xf * xf, axis=-1, keepdims=True) + EPS) * g.astype(jnp.float32)
    return y.astype(x.dtype)

def context_attention(q, k, v):
    B, S, H, d = q.shape
    nb = S // CTX_QBLOCK
    qb = q.reshape(B, nb, CTX_QBLOCK, H, d).transpose(1, 0, 2, 3, 4)

    def one_block(qi):
        s = jnp.einsum('bqhd,bkhd->bhqk', qi, k).astype(jnp.float32) * (d ** -0.5)
        p = jax.nn.softmax(s, axis=-1).astype(v.dtype)
        return jnp.einsum('bhqk,bkhd->bqhd', p, v)

    o = lax.map(one_block, qb)
    return o.transpose(1, 0, 2, 3, 4).reshape(B, S, H, d)

def neighborhood_attention(q, k, v, ck, cv, rpb):
    B, T, H, d = q.shape
    rows = T // GRID_W
    kr = min(NA_ROWS, rows)
    nj = GRID_W // NA_QBLOCK
    r = np.arange(rows)
    row_start = np.clip(r - kr // 2, 0, rows - kr)
    row_idx = row_start[:, None] + np.arange(kr)
    cols = np.arange(GRID_W)
    col_start = np.clip(cols - NA_COLS // 2, 0, GRID_W - NA_COLS)
    blk_start = np.minimum(col_start[::NA_QBLOCK], GRID_W - NA_KBLOCK)
    col_idx = blk_start[:, None] + np.arange(NA_KBLOCK)
    qcol = cols.reshape(nj, NA_QBLOCK)
    cs = col_start.reshape(nj, NA_QBLOCK)
    in_win = (col_idx[:, None, :] >= cs[:, :, None]) & (col_idx[:, None, :] < cs[:, :, None] + NA_COLS)
    dr = row_idx - r[:, None] + NA_ROWS - 1
    dc = np.clip(col_idx[:, None, :] - qcol[:, :, None] + NA_COLS - 1, 0, RPB_COLS - 1)
    bias = rpb.astype(jnp.float32)[:, dr[:, None, None, :, None], dc[None, :, :, None, :]]
    bias = jnp.where(in_win[None, None, :, :, None, :], bias, NEG_INF)
    bias = bias.transpose(1, 2, 0, 3, 4, 5).reshape(rows, nj, H, NA_QBLOCK, kr * NA_KBLOCK)
    ridx = row_idx[:, None, :, None]
    cidx = col_idx[None, :, None, :]
    kgrid = k.reshape(B, rows, GRID_W, H, d)
    vgrid = v.reshape(B, rows, GRID_W, H, d)
    kg = kgrid[:, ridx, cidx].reshape(B, rows, nj, kr * NA_KBLOCK, H, d)
    vg = vgrid[:, ridx, cidx].reshape(B, rows, nj, kr * NA_KBLOCK, H, d)
    qg = q.reshape(B, rows, nj, NA_QBLOCK, H, d)
    scale = d ** -0.5
    s_loc = jnp.einsum('brjqhd,brjkhd->brjhqk', qg, kg).astype(jnp.float32) * scale + bias[None]
    s_ctx = jnp.einsum('brjqhd,bphd->brjhqp', qg, ck).astype(jnp.float32) * scale
    n_loc = s_loc.shape[-1]
    p = jax.nn.softmax(jnp.concatenate([s_loc, s_ctx], axis=-1), axis=-1).astype(v.dtype)
    o = (jnp.einsum('brjhqk,brjkhd->brjqhd', p[..., :n_loc], vg)
         + jnp.einsum('brjhqp,bphd->brjqhd', p[..., n_loc:], cv))
    return o.reshape(B, T, H, d)

def mlstm_chunkwise(q, k, v, i_pre, f_pre, C0, n0, m0):
    B, T, H, d = q.shape
    L = ML_CHUNK
    nc = T // L
    f32 = jnp.float32

    def chunks(a):
        return a.astype(f32).reshape(B, nc, L, H, d).transpose(1, 0, 3, 2, 4)

    def gchunks(a):
        return a.astype(f32).reshape(B, nc, L, H).transpose(1, 0, 3, 2)

    qc = chunks(q) * (d ** -0.5)
    kc, vc = chunks(k), chunks(v)
    log_i = gchunks(i_pre)
    log_f = jax.nn.log_sigmoid(gchunks(f_pre))
    causal = jnp.asarray(np.tril(np.ones((L, L), dtype=bool)))

    def step(carry, xs):
        C, n, m = carry
        qt, kt, vt, li, lf = xs
        b = jnp.cumsum(lf, axis=-1)
        dmat = jnp.where(causal, b[..., :, None] - b[..., None, :] + li[..., None, :], -jnp.inf)
        inter = b + m[..., None]
        m_t = jnp.maximum(inter, jnp.max(dmat, axis=-1))
        w_intra = jnp.exp(dmat - m_t[..., None])
        w_inter = jnp.exp(inter - m_t)
        s = jnp.einsum('bhtd,bhsd->bhts', qt, kt) * w_intra
        num = w_inter[..., None] * jnp.einsum('bhtd,bhde->bhte', qt, C) + jnp.einsum('bhts,bhse->bhte', s, vt)
        den = w_inter * jnp.einsum('bhtd,bhd->bht', qt, n) + jnp.sum(s, axis=-1)
        h = num / jnp.maximum(jnp.abs(den), jnp.exp(-m_t))[..., None]
        b_end = b[..., -1]
        g = b_end[..., None] - b + li
        m_new = jnp.maximum(b_end + m, jnp.max(g, axis=-1))
        decay = jnp.exp(b_end + m - m_new)
        kw = kt * jnp.exp(g - m_new[..., None])[..., None]
        C_new = decay[..., None, None] * C + jnp.einsum('bhsd,bhse->bhde', kw, vt)
        n_new = decay[..., None] * n + jnp.sum(kw, axis=2)
        return (C_new, n_new, m_new), h

    (C, n, m), hs = lax.scan(step, (C0.astype(f32), n0.astype(f32), m0.astype(f32)),
                             (qc, kc, vc, log_i, log_f))
    h = hs.transpose(1, 0, 3, 2, 4).reshape(B, T, H, d)
    return h, (C, n, m)

def mlstm_bidirectional(q, k, v, gates, state):
    C0, n0, m0 = state
    flip = lambda a: jnp.flip(a, axis=1)
    h_f, (Cf, nf, mf) = mlstm_chunkwise(q, k, v, gates[:, :, 0], gates[:, :, 1], C0[:, 0], n0[:, 0], m0[:, 0])
    h_b, (Cb, nb, mb) = mlstm_chunkwise(flip(q), flip(k), flip(v), flip(gates[:, :, 2]), flip(gates[:, :, 3]),
                                        C0[:, 1], n0[:, 1], m0[:, 1])
    h = h_f + flip(h_b)
    return h, (jnp.stack([Cf, Cb], axis=1), jnp.stack([nf, nb], axis=1), jnp.stack([mf, mb], axis=1))

def multiscale_pool(u, w_pool, pool_scale):
    B, T, _ = u.shape
    uf = u.astype(jnp.float32).reshape(B, T, POOL_GROUPS, POOL_DIM)
    csum = jnp.concatenate([jnp.zeros((B, 1, POOL_GROUPS, POOL_DIM), jnp.float32), jnp.cumsum(uf, axis=1)], axis=1)
    t = np.arange(T)
    outs = []
    for g, w in enumerate(POOL_WINDOWS):
        lo = np.clip(t - w // 2, 0, T)
        hi = np.clip(t - w // 2 + w, 0, T)
        cnt = (hi - lo).astype(np.float32)
        mean = (csum[:, hi, g] - csum[:, lo, g]) / cnt[None, :, None]
        outs.append(mean - uf[:, :, g])
    pooled = jnp.stack(outs, axis=2)
    y = jnp.einsum('btgc,gce->btge', pooled, w_pool.astype(jnp.float32)).reshape(B, T, POOL_WIDTH)
    return (y * pool_scale.astype(jnp.float32)).astype(u.dtype)

def grouped_moe(h, w_router, b_router, w_gate, w_up, w_down):
    shp = h.shape
    x = h.reshape(-1, shp[-1])
    scores = jax.nn.sigmoid(x.astype(jnp.float32) @ w_router.astype(jnp.float32))
    sel = scores + b_router.astype(jnp.float32)
    grp = sel.reshape(-1, N_EXPERT_GROUPS, EXPERTS_PER_GROUP)
    grp_score = jnp.sum(lax.top_k(grp, TOP_K)[0], axis=-1)
    gidx = jnp.argmax(grp_score, axis=-1)
    in_grp = (jnp.arange(N_EXPERTS) // EXPERTS_PER_GROUP)[None, :] == gidx[:, None]
    _, top_idx = lax.top_k(jnp.where(in_grp, sel, -jnp.inf), TOP_K)
    top_s = jnp.take_along_axis(scores, top_idx, axis=-1)
    gates = top_s / jnp.sum(top_s, axis=-1, keepdims=True)
    combine = jnp.sum(jax.nn.one_hot(top_idx, N_EXPERTS, dtype=jnp.float32) * gates[..., None], axis=1)
    hid = jax.nn.silu(jnp.einsum('nd,edf->nef', x, w_gate)) * jnp.einsum('nd,edf->nef', x, w_up)
    hid = hid * combine[..., None].astype(hid.dtype)
    out = jnp.einsum('nef,efd->nd', hid, w_down)
    return out.reshape(shp).astype(h.dtype)

def trunk_layer(x, mod, norm1, w_in, b_in, rpb, ml_norm, w_pool, pool_scale, w_out,
                norm2, w_router, b_router, w_gate, w_up, w_down, ctx_kv, ml_state):
    B, T, _ = x.shape
    sh1, sc1, g1, sh2, sc2, g2 = jnp.split(mod, 6, axis=-1)
    h = rms_norm(x, norm1) * (1 + sc1) + sh1
    proj = h @ w_in + b_in
    qa, ka, va, qb, kb, vb, ob, gts, pin = jnp.split(proj, _in_split_points(), axis=-1)
    qa = qa.reshape(B, T, NA_HEADS, NA_DIM)
    ka = ka.reshape(B, T, NA_HEADS, NA_DIM)
    va = va.reshape(B, T, NA_HEADS, NA_DIM)
    if ctx_kv is None:
        out_a = context_attention(qa, ka, va)
    else:
        out_a = neighborhood_attention(qa, ka, va, ctx_kv[0], ctx_kv[1], rpb)
    qb = qb.reshape(B, T, ML_HEADS, ML_DIM)
    kb = kb.reshape(B, T, ML_HEADS, ML_DIM)
    vb = vb.reshape(B, T, ML_HEADS, ML_DIM)
    hb, new_ml = mlstm_bidirectional(qb, kb, vb, gts.reshape(B, T, 4, ML_HEADS), ml_state)
    hb = hb * lax.rsqrt(jnp.mean(hb * hb, axis=-1, keepdims=True) + EPS) * ml_norm.astype(jnp.float32).reshape(ML_HEADS, ML_DIM)
    out_b = (jax.nn.sigmoid(ob.astype(jnp.float32)) * hb.reshape(B, T, ML_WIDTH)).astype(x.dtype)
    out_c = multiscale_pool(pin, w_pool, pool_scale)
    mixed = jnp.concatenate([out_a.reshape(B, T, NA_WIDTH), out_b, out_c], axis=-1) @ w_out
    x = x + g1 * mixed
    h2 = rms_norm(x, norm2) * (1 + sc2) + sh2
    x = x + g2 * grouped_moe(h2, w_router, b_router, w_gate, w_up, w_down)
    return x, (ka, va), new_ml

def setup_inputs(seed: int = 0) -> dict:
    key = jax.random.key(seed)
    ks = jax.random.split(key, 32)
    nrm = lambda k, shape, s: jax.random.normal(k, shape, jnp.float32) * s
    f_cols = np.concatenate([
        3 * NA_WIDTH + 4 * ML_WIDTH + ML_HEADS + np.arange(ML_HEADS),
        3 * NA_WIDTH + 4 * ML_WIDTH + 3 * ML_HEADS + np.arange(ML_HEADS)])
    b_in = nrm(ks[13], (DEPTH, IN_COLS), 0.02).at[:, f_cols].add(ML_FORGET_BIAS)
    return {
        'x_prompt': nrm(ks[0], (BATCH, SEQ, D_MODEL), 1.0),
        'x_sample': nrm(ks[1], (DEC_BATCH, DEC_SEQ, D_MODEL), 1.0),
        'cache_k_attn': nrm(ks[2], (DEC_BATCH, DEPTH, PAST_LEN, NA_HEADS, NA_DIM), 1.0),
        'cache_v_attn': nrm(ks[3], (DEC_BATCH, DEPTH, PAST_LEN, NA_HEADS, NA_DIM), 1.0),
        'state_mlstm_C': nrm(ks[4], (DEC_BATCH, DEPTH, 2, ML_HEADS, ML_DIM, ML_DIM), 1.0),
        'state_mlstm_n': nrm(ks[5], (DEC_BATCH, DEPTH, 2, ML_HEADS, ML_DIM), 1.0),
        'state_mlstm_m': nrm(ks[6], (DEC_BATCH, DEPTH, 2, ML_HEADS), 1.0),
        'c': nrm(ks[7], (DEC_BATCH, D_MODEL), 1.0),
        'c_ctx': nrm(ks[8], (D_MODEL,), 1.0),
        'w_ada': nrm(ks[9], (DEPTH, D_MODEL, ADA_DIM), 0.5 * D_MODEL ** -0.5),
        'b_ada': nrm(ks[10], (DEPTH, ADA_DIM), 0.02),
        'norm1': 1.0 + nrm(ks[11], (DEPTH, D_MODEL), 0.02),
        'w_in': nrm(ks[12], (DEPTH, D_MODEL, IN_COLS), D_MODEL ** -0.5),
        'b_in': b_in,
        'rpb': nrm(ks[14], (DEPTH, NA_HEADS, RPB_ROWS, RPB_COLS), 0.5),
        'ml_norm': 1.0 + nrm(ks[15], (DEPTH, ML_WIDTH), 0.02),
        'w_pool': nrm(ks[16], (DEPTH, POOL_GROUPS, POOL_DIM, POOL_DIM), POOL_DIM ** -0.5),
        'pool_scale': 1.0 + nrm(ks[17], (DEPTH, POOL_WIDTH), 0.1),
        'w_out': nrm(ks[18], (DEPTH, MIX_WIDTH, D_MODEL), MIX_WIDTH ** -0.5),
        'norm2': 1.0 + nrm(ks[19], (DEPTH, D_MODEL), 0.02),
        'w_router': nrm(ks[20], (D_MODEL, N_EXPERTS), D_MODEL ** -0.5),
        'b_router': nrm(ks[21], (N_EXPERTS,), 0.01),
        'w_gate': nrm(ks[22], (DEPTH, N_EXPERTS, D_MODEL, D_EXPERT), D_MODEL ** -0.5),
        'w_up': nrm(ks[23], (DEPTH, N_EXPERTS, D_MODEL, D_EXPERT), D_MODEL ** -0.5),
        'w_down': nrm(ks[24], (DEPTH, N_EXPERTS, D_EXPERT, D_MODEL), D_EXPERT ** -0.5),
        'final_norm': 1.0 + nrm(ks[25], (D_MODEL,), 0.02),
    }

def reference(x_prompt, x_sample, cache_k_attn, cache_v_attn, state_mlstm_C, state_mlstm_n, state_mlstm_m,
              c, c_ctx, w_ada, b_ada, norm1, w_in, b_in, rpb, ml_norm, w_pool, pool_scale, w_out, norm2,
              w_router, b_router, w_gate, w_up, w_down, final_norm):
    xc = x_prompt
    xs = x_sample
    bc = x_prompt.shape[0]
    zero_state = (jnp.zeros((bc, 2, ML_HEADS, ML_DIM, ML_DIM), jnp.float32),
                  jnp.zeros((bc, 2, ML_HEADS, ML_DIM), jnp.float32),
                  jnp.zeros((bc, 2, ML_HEADS), jnp.float32))
    ks_, vs_, Cs, ns, ms = [], [], [], [], []
    for l in range(DEPTH):
        mod_ctx = jax.nn.silu(c_ctx) @ w_ada[l] + b_ada[l]
        mod_lat = (jax.nn.silu(c) @ w_ada[l] + b_ada[l])[:, None, :]
        lw = (norm1[l], w_in[l], b_in[l], rpb[l], ml_norm[l], w_pool[l], pool_scale[l], w_out[l],
              norm2[l], w_router, b_router, w_gate[l], w_up[l], w_down[l])
        xc, (k_l, v_l), (C_l, n_l, m_l) = trunk_layer(xc, mod_ctx, *lw, None, zero_state)
        ks_.append(k_l)
        vs_.append(v_l)
        Cs.append(C_l)
        ns.append(n_l)
        ms.append(m_l)
        xs, _, _ = trunk_layer(xs, mod_lat, *lw, (cache_k_attn[:, l], cache_v_attn[:, l]),
                               (state_mlstm_C[:, l], state_mlstm_n[:, l], state_mlstm_m[:, l]))
    y_prompt = rms_norm(xc, final_norm)
    y_sample = rms_norm(xs, final_norm)
    dt = x_prompt.dtype
    new_cache_k = jnp.stack(ks_, axis=1).astype(dt)
    new_cache_v = jnp.stack(vs_, axis=1).astype(dt)
    new_state_C = jnp.stack(Cs, axis=1).astype(dt)
    new_state_n = jnp.stack(ns, axis=1).astype(dt)
    new_state_m = jnp.stack(ms, axis=1).astype(dt)
    return (y_prompt, y_sample, new_cache_k, new_cache_v, new_state_C, new_state_n, new_state_m)


_drawn_inputs = setup_inputs


def setup_inputs(seed=0):
    import zlib

    import numpy as np

    out = dict(_drawn_inputs(seed))
    spreads = {}
    factors = {'cache_k_attn': 23.213,
     'state_mlstm_C': 6.973,
     'state_mlstm_n': 8.0,
     'state_mlstm_m': 8.0,
     'rpb': 14.37,
     'ml_norm': 19.632,
     'final_norm': 22.095,
     'pool_scale': 3.65,
     'norm2': 3.091,
     'cache_v_attn': 8.0}
    for name, (base, spread) in spreads.items():
        noise = np.random.default_rng([zlib.crc32(name.encode()), seed]).standard_normal(out[name].shape)
        drawn = base * np.exp(spread * noise) if base else spread * noise
        out[name] = __import__('jax').numpy.asarray(drawn.astype(out[name].dtype))
    for name, factor in factors.items():
        out[name] = (out[name] * factor).astype(out[name].dtype)
    return out
```

```python
from contextlib import ExitStack

import numpy as np

import concourse.bass as bass
from concourse import mybir

F32 = mybir.dt.float32
U32 = mybir.dt.uint32
I32 = mybir.dt.int32
ALU = mybir.AluOpType
ACT = mybir.ActivationFunctionType
AX = mybir.AxisListType

P = 128
D = 1024
KD = D // P
LAT, CTX = 1024, 128
TOK = LAT + CTX
NT = TOK // P
CTX_TILE = NT - 1
EPS = 1e-6
NEG = -1e30
BANK = 512

HEADS, HD = 6, 64
AW = HEADS * HD
GRID_W, ROWS = 64, 16
KROWS, KCOLS = 8, 16
EDGE_SLOTS = 14
INNER_ROWS = 10
TAB_SLOTS = EDGE_SLOTS + INNER_ROWS
RPB_R, RPB_C = 15, 31
PADW = 2 * GRID_W - 1

MH, MD = 4, 96
MW = MH * MD
MA = MD + 1
PG, PD = 4, 64
PW = PG * PD
WINDOWS = (2, 4, 8, 16)
N_GATES = 16
C_QA, C_KA, C_VA = 0, AW, 2 * AW
C_QB = 3 * AW
C_KB, C_VB, C_OB, C_TAIL = C_QB + MW, C_QB + 2 * MW, C_QB + 3 * MW, C_QB + 4 * MW
TAIL = N_GATES + PW

NE, EG, EPG, DF = 16, 4, 4, 512
KF = DF // P
N_SLOT_TILES = 34
SLOTS = N_SLOT_TILES * P


class Steps:

    def __init__(self, engine, sem):
        self.engine, self.sem, self.n = engine, sem, 0

    def add(self, instruction):
        instruction.then_inc(self.sem, 1)
        self.n = self.n + 1
        return instruction

    def settle(self):
        self.engine.wait_ge(self.sem, self.n)

    def link(self, instruction):
        self.add(instruction)
        self.settle()


class Arena:

    def __init__(self, tensor, columns):
        self.tensor, self.columns, self.at, self.high = tensor, columns, 0, 0

    def take(self, shape, rows=P):
        n = int(np.prod(shape))
        a = self.tensor[0:rows, self.at:self.at + n]
        self.at += n
        self.high = max(self.high, self.at)
        assert self.at <= self.columns, (self.at, self.columns)
        if len(shape) == 2:
            a = a.rearrange("p (a b) -> p a b", a=shape[0])
        if len(shape) == 3:
            a = a.rearrange("p (a b c) -> p a b c", a=shape[0], b=shape[1])
        return a


def bc(ap, shape):
    return ap.to_broadcast(list(shape))


def program(nc, x_all, cache_k, cache_v, state_C, state_n, state_m, c_both, w_ada, b_ada, norm1, w_in, b_in,
            rpb_pad, ml_norm, w_pool, pool_scale, w_out, norm2, w_router, b_router, w_gate, w_up, w_down,
            final_norm, k_ident, k_upper, k_sel, k_scanmask, k_reset, k_winmask, k_band, k_tile_ids,
            y_all, out_k, out_v, out_C, out_n, out_m):
    ctx = ExitStack()
    with ctx, nc.allow_non_contiguous_dma(reason="biases, states and modulation inputs as columns"):
        sb = ctx.enter_context(nc.sbuf_tensor("sb", [P, 52992], F32))
        ps = ctx.enter_context(nc.psum_tensor("ps", [P, 8 * BANK], F32))
        ar = Arena(sb, 52992)

        def sem(name):
            return ctx.enter_context(nc.semaphore(name))

        def bank(n, cols=BANK, at=0):
            return ps[:, n * BANK + at:n * BANK + at + cols]

        mod_rows = nc.dram_tensor("mod_rows", [2, 6 * D], F32, kind="Internal").ap()
        rpb_rows = nc.dram_tensor("rpb_rows", [HEADS * RPB_R, GRID_W, PADW], F32, kind="Internal").ap()
        slot_x = nc.dram_tensor("slot_x", [SLOTS, D], F32, kind="Internal").ap()
        slot_y = nc.dram_tensor("slot_y", [SLOTS, D], F32, kind="Internal").ap()

        ident = ar.take([P])
        zero_tile = ar.take([D])
        gate = [ar.take([NT]) for _ in range(2)]
        slot = [ar.take([NT]) for _ in range(2)]
        te = ar.take([N_SLOT_TILES])
        const_ready = sem("const_ready")
        zero_ready = sem("zero_ready")
        slots_zeroed = sem("slots_zeroed")
        out_stored = sem("out_stored")
        stored = [0]

        mark = ar.at
        cc = ar.take([KD, 2])
        ce = ar.take([KD, 2])
        ada = [ar.take([KD, BANK]) for _ in range(3)]
        brow = ar.take([6 * D])
        nrow = ar.take([2, D])
        mrow = ar.take([6 * D])
        c_ready = sem("c_ready")
        silu_exp = sem("silu_exp")
        silu_done = sem("silu_done")
        ada_loaded = [sem(f"ada_loaded{s}") for s in range(3)]
        mod_mm = sem("mod_mm")
        mod_evac = sem("mod_evac")
        mod_ready = sem("mod_ready")
        mod_stored = sem("mod_stored")
        dve_mod = sem("dve_mod")
        MOD_BLOCKS = 6 * D // BANK
        with nc.Block() as block:
            @block.sync
            def _(sp):
                sp.dma_start(ident, k_ident).then_inc(const_ready, 16)
                sp.dma_start(rpb_rows, bass.AP(rpb_pad.tensor, 0, [[PADW, HEADS * RPB_R], [0, GRID_W], [1, PADW]])).then_inc(const_ready, 16)
                for v in range(2):
                    sp.dma_start(cc[:, :, v], c_both[v].rearrange("(k p) -> p k", p=P)).then_inc(c_ready, 16)
                sp.dma_start(brow[0:2], bass.AP(b_ada.tensor, 0, [[0, 2], [1, 6 * D]])).then_inc(c_ready, 16)
                for v, n in enumerate((norm1, norm2)):
                    sp.dma_start(nrow[0:2, v], bass.AP(n.tensor, 0, [[0, 2], [1, D]])).then_inc(c_ready, 16)
                src = w_ada.rearrange("(k p) n -> p k n", p=P)

                def load(i, first):
                    for s in range(3):
                        if not first:
                            sp.wait_ge(mod_mm, 3 * i + s - 2)
                        sp.dma_start(ada[s], src[:, :, bass.ds((3 * i + s) * BANK, BANK)]).then_inc(ada_loaded[s], 16)

                load(0, True)
                with sp.Fori(1, MOD_BLOCKS // 3) as i:
                    load(i, False)
                sp.wait_ge(mod_ready, 2)
                sp.dma_start(mod_rows, mrow[0:2]).then_inc(mod_stored, 16)
                sp.wait_ge(mod_stored, 16)
                sp.wait_ge(const_ready, 32)

            @block.gpsimd
            def _(pool):
                nc.gpsimd.memset(zero_tile, 0.0).then_inc(zero_ready, 1)
                pool.wait_ge(zero_ready, 1)
                for j in range(N_SLOT_TILES):
                    pool.dma_start(slot_x[j * P:(j + 1) * P, :], zero_tile).then_inc(slots_zeroed, 16)

            @block.scalar
            def _(act):
                act.wait_ge(c_ready, 16 * 5)
                nc.scalar.activation(ce, cc, ACT.Exp, scale=-1.0).then_inc(silu_exp, 1)

            @block.vector
            def _(dve):
                st = Steps(dve, dve_mod)
                dve.wait_ge(silu_exp, 1)
                st.link(nc.vector.tensor_scalar(ce, ce, 1.0, None, ALU.add))
                st.link(nc.vector.reciprocal(ce, ce))
                nc.vector.tensor_tensor(cc, cc, ce, ALU.mult).then_inc(silu_done, 1)

                def evac(i):
                    for s in range(3):
                        n = 3 * i + s
                        dve.wait_ge(mod_mm, n + 1)
                        nc.vector.tensor_tensor(mrow[0:2, bass.ds(n * BANK, BANK)], bank(s)[0:2],
                                                brow[0:2, bass.ds(n * BANK, BANK)], ALU.add).then_inc(mod_evac, 1)

                evac(0)
                with dve.Fori(1, MOD_BLOCKS // 3) as i:
                    evac(i)
                dve.wait_ge(mod_evac, MOD_BLOCKS)
                for v, part in enumerate((1, 4)):
                    row = mrow[0:2, part * D:(part + 1) * D]
                    nc.vector.scalar_tensor_tensor(out=row, in0=row, scalar=1.0, in1=nrow[0:2, v],
                                                   op0=ALU.add, op1=ALU.mult).then_inc(mod_ready, 1)

            @block.tensor
            def _(pe):
                pe.wait_ge(silu_done, 1)

                def multiply(i, first):
                    for s in range(3):
                        pe.wait_ge(ada_loaded[s], 16 * (i + 1))
                        if not first:
                            pe.wait_ge(mod_evac, 3 * i + s - 2)
                        for k in range(KD):
                            last = nc.tensor.matmul(bank(s)[0:2], cc[:, k, :], ada[s][:, k, :],
                                                    start=(k == 0), stop=(k == KD - 1))
                        last.then_inc(mod_mm, 1)

                multiply(0, True)
                with pe.Fori(1, MOD_BLOCKS // 3) as i:
                    multiply(i, False)
        ar.at = mark

        def mod_row(part):
            return bass.AP(mod_rows.tensor, part * D, [[0, P], [6 * D, 2], [1, D]])

        def side(t):
            return 1 if t == CTX_TILE else 0

        def norm_stage(tag, x, rows_of, nat, outT, load, router=None):
            mark = ar.at
            scale_row, shift_row = ar.take([2, D]), ar.take([2, D])
            junk = ar.take([D])
            ss, ln, y0, t1 = ar.take([NT]), ar.take([NT]), ar.take([NT]), ar.take([NT])
            ring = nat is None
            if ring:
                two = [ar.take([D]) for _ in range(2)]
            row_loaded, x_loaded = sem(tag + "row_loaded"), sem(tag + "x_loaded")
            squares, mean_ready, guess_ready = sem(tag + "squares"), sem(tag + "mean"), sem(tag + "guess")
            nat_ready, turned, copied = sem(tag + "nat_ready"), sem(tag + "turned"), sem(tag + "copied")
            dve_s, act_s = sem(tag + "dve"), sem(tag + "act")
            nat_of = lambda t: two[t % 2] if ring else nat[:, t, :]
            with nc.Block() as block:
                @block.sync
                def _(sp):
                    for row, part in zip((shift_row, scale_row), rows_of):
                        sp.dma_start(row, mod_row(part)).then_inc(row_loaded, 16)
                    if load is not None:
                        for t in range(NT):
                            sp.dma_start(x[:, t, :], load[t * P:(t + 1) * P, :]).then_inc(x_loaded, 16)

                @block.scalar
                def _(act):
                    st = Steps(act, act_s)
                    for t in range(NT):
                        if load is not None:
                            act.wait_ge(x_loaded, 16 * NT)
                        if t:
                            st.settle()
                        st.add(nc.scalar.activation(junk, x[:, t, :], ACT.Square, accum_out=ss[:, t:t + 1]))
                    st.settle()
                    nc.scalar.activation(junk[:, 0:1], ss[:, 0:1], ACT.Square).then_inc(squares, 1)
                    act.wait_ge(mean_ready, 1)
                    st.link(nc.scalar.activation(ln, ss, ACT.Ln))
                    nc.scalar.activation(y0, ln, ACT.Exp, scale=-0.5).then_inc(guess_ready, 1)
                    for t in range(NT):
                        act.wait_ge(turned, t + 1)
                        for half in range(2):
                            ins = nc.scalar.activation(
                                outT[:, 4 * half:4 * half + 4, t * P:(t + 1) * P],
                                bank(4 * (t % 2) + half).rearrange("p (k t) -> p k t", k=4), ACT.Copy)
                        ins.then_inc(copied, 1)

                @block.vector
                def _(dve):
                    st = Steps(dve, dve_s)
                    dve.wait_ge(squares, 1)
                    nc.vector.tensor_scalar(ss, ss, 1.0 / D, EPS, ALU.mult, ALU.add).then_inc(mean_ready, 1)
                    dve.wait_ge(guess_ready, 1)
                    st.link(nc.vector.tensor_tensor(t1, y0, y0, ALU.mult))
                    st.link(nc.vector.scalar_tensor_tensor(out=t1, in0=t1, scalar=-0.5, in1=ss,
                                                           op0=ALU.mult, op1=ALU.mult))
                    st.link(nc.vector.scalar_tensor_tensor(out=y0, in0=t1, scalar=1.5, in1=y0,
                                                           op0=ALU.add, op1=ALU.mult))
                    dve.wait_ge(row_loaded, 32)
                    for t in range(NT):
                        if ring and t >= 2:
                            dve.wait_ge(turned, t - 1)
                        st.link(nc.vector.scalar_tensor_tensor(
                            out=nat_of(t), in0=x[:, t, :], scalar=y0[:, t:t + 1], in1=scale_row[:, side(t), :],
                            op0=ALU.mult, op1=ALU.mult))
                        nc.vector.tensor_tensor(nat_of(t), nat_of(t), shift_row[:, side(t), :],
                                                ALU.add).then_inc(nat_ready, 1)

                @block.tensor
                def _(pe):
                    for t in range(NT):
                        pe.wait_ge(nat_ready, t + 1)
                        if t >= 2:
                            pe.wait_ge(copied, t - 1)
                        for k in range(KD):
                            last = nc.tensor.transpose(
                                ps[:, (4 * (t % 2)) * BANK + k * P:(4 * (t % 2)) * BANK + (k + 1) * P],
                                nat_of(t)[:, k * P:(k + 1) * P], ident)
                        last.then_inc(turned, 1)
            ar.at = mark

        start_h = ar.at
        hT = ar.take([KD, TOK])
        mark_h = ar.at
        x_res = ar.take([NT, D])
        norm_stage("n1_", x_res, (0, 1), None, hT, x_all)
        ar.at = mark_h

        qbT, kbT = ar.take([MH, TOK]), ar.take([MH, TOK])
        vb = ar.take([NT, MH, MA])
        og = ar.take([NT, MW])
        gi, gf = ar.take([NT, 64]), ar.take([NT, 64])
        after_mlstm_in = ar.at
        pin = ar.take([NT, PW])
        qaT, kaT = ar.take([3, TOK]), ar.take([3, TOK])
        va = ar.take([NT, AW])
        after_proj = ar.at
        wring = [ar.take([KD, AW]) for _ in range(2)]
        bias_a, bias_b = ar.take([6]), ar.take([8])
        bias_row = ar.take([3 * MW + TAIL])
        ofs = {C_VA: 0, C_VB: MW, C_OB: 2 * MW, C_TAIL: 3 * MW}
        groups = [("T", C_QA, AW), ("T", C_KA, AW), ("N", C_VA, AW), ("T", C_QB, MW), ("T", C_KB, MW),
                  ("N", C_VB, MW), ("N", C_OB, MW), ("N", C_TAIL, TAIL)]
        units = []
        for g, (kind, c0, n) in enumerate(groups):
            if kind == "T":
                m = P if c0 < C_VA else MD
                for b in range(n // m):
                    units += [(g, b, m, t0, tn) for t0, tn in ((0, 512), (512, 512), (1024, 128))]
            else:
                units += [(g, t, n, t * P, P) for t in range(NT)]
        last_of = {g: max(i for i, u in enumerate(units) if u[0] == g) for g in range(len(groups))}
        w_loaded = [sem(f"w_loaded{s}") for s in range(2)]
        bias_loaded = sem("bias_loaded")
        proj_mm, proj_evac = sem("proj_mm"), sem("proj_evac")
        dve_proj, sig_exp, sig_in = sem("dve_proj"), sem("sig_exp"), sem("sig_in")
        with nc.Block() as block:
            @block.sync
            def _(sp):
                src = w_in.rearrange("(k p) n -> p k n", p=P)
                sp.dma_start(bias_a, b_in[0:2 * AW].rearrange("(b p) -> p b", p=P)).then_inc(bias_loaded, 16)
                sp.dma_start(bias_b[0:MD], b_in[C_QB:C_QB + 2 * MW].rearrange("(b p) -> p b", p=MD)).then_inc(bias_loaded, 16)
                for c0, at in ofs.items():
                    n = TAIL if c0 == C_TAIL else MW
                    sp.dma_start(bias_row[:, at:at + n], bass.AP(b_in.tensor, c0, [[0, P], [1, n]])).then_inc(bias_loaded, 16)
                for g, (_, c0, n) in enumerate(groups):
                    if g >= 2:
                        sp.wait_ge(proj_mm, last_of[g - 2] + 1)
                    sp.dma_start(wring[g % 2][:, :, 0:n], src[:, :, c0:c0 + n]).then_inc(w_loaded[g % 2], 16)

            @block.tensor
            def _(pe):
                seen = set()
                for i, (g, b, m, t0, tn) in enumerate(units):
                    if g not in seen:
                        seen.add(g)
                        pe.wait_ge(w_loaded[g % 2], 16 * (g // 2 + 1))
                    if i >= 8:
                        pe.wait_ge(proj_evac, i - 7)
                    w = wring[g % 2]
                    for k in range(KD):
                        if groups[g][0] == "T":
                            last = nc.tensor.matmul(bank(i % 8)[0:m, 0:tn], w[:, k, b * m:(b + 1) * m],
                                                    hT[:, k, t0:t0 + tn], start=(k == 0), stop=(k == KD - 1))
                        else:
                            last = nc.tensor.matmul(bank(i % 8)[:, 0:m], hT[:, k, t0:t0 + P], w[:, k, 0:m],
                                                    start=(k == 0), stop=(k == KD - 1))
                    last.then_inc(proj_mm, 1)

            @block.gpsimd
            def _(pool):
                nc.gpsimd.memset(vb, 1.0).then_inc(sig_in, 1)
                nc.gpsimd.memset(gi, 0.0).then_inc(sig_in, 1)
                nc.gpsimd.memset(gf, 0.0).then_inc(sig_in, 1)

            @block.scalar
            def _(act):
                act.wait_ge(proj_evac, last_of[6] + 1)
                nc.scalar.activation(og, og, ACT.Exp, scale=-1.0).then_inc(sig_exp, 1)

            @block.vector
            def _(dve):
                st = Steps(dve, dve_proj)
                dve.wait_ge(bias_loaded, 16 * 6)
                dve.wait_ge(sig_in, 3)
                for i, (g, b, m, t0, tn) in enumerate(units):
                    dve.wait_ge(proj_mm, i + 1)
                    c0 = groups[g][1]
                    p = bank(i % 8)
                    if groups[g][0] == "T":
                        if c0 < C_VA:
                            dst, bias = (qaT if c0 == C_QA else kaT), bias_a[:, (c0 // P) + b:(c0 // P) + b + 1]
                            scale = HD ** -0.5 if c0 == C_QA else 1.0
                        else:
                            col = (0 if c0 == C_QB else MH) + b
                            dst, bias = (qbT if c0 == C_QB else kbT), bias_b[0:MD, col:col + 1]
                            scale = float(MD) ** -0.5 if c0 == C_QB else 1.0
                        ins = nc.vector.tensor_scalar(dst[0:m, b, t0:t0 + tn], p[0:m, 0:tn], bias, scale, ALU.add, ALU.mult)
                    else:
                        row = bias_row[:, ofs[c0]:ofs[c0] + m]
                        if c0 == C_VA:
                            ins = nc.vector.tensor_tensor(va[:, b, :], p[:, 0:m], row, ALU.add)
                        elif c0 == C_VB:
                            ins = nc.vector.tensor_tensor(vb[:, b, :, 0:MD], p[:, 0:m].rearrange("p (h d) -> p h d", h=MH),
                                                          row.rearrange("p (h d) -> p h d", h=MH), ALU.add)
                        elif c0 == C_OB:
                            ins = nc.vector.tensor_tensor(og[:, b, :], p[:, 0:m], row, ALU.add)
                        else:
                            for dst, at in ((gi, 0), (gf, MH)):
                                for way in range(2):
                                    c = at + 2 * MH * way
                                    st.add(nc.vector.tensor_tensor(dst[:, b, 32 * way:32 * way + MH], p[:, c:c + MH],
                                                                   row[:, c:c + MH], ALU.add))
                            ins = nc.vector.tensor_tensor(pin[:, b, :], p[:, N_GATES:TAIL], row[:, N_GATES:TAIL], ALU.add)
                    ins.then_inc(proj_evac, 1)
                dve.wait_ge(sig_exp, 1)
                st.link(nc.vector.tensor_scalar(og, og, 1.0, None, ALU.add))
                st.link(nc.vector.reciprocal(og, og))
        ar.at = start_h
        mix = ar.take([NT, D])
        ar.at = after_proj

        mark = ar.at
        band = ar.take([PG * 6, P])
        wp = ar.take([PG, PD])
        ps_row = ar.take([PW])
        pT = [ar.take([PG, P]) for _ in range(2)]
        pool_in, pool_mm, pool_cp, pool_y, pool_out = (sem("pool_in"), sem("pool_mm"), sem("pool_cp"), sem("pool_y"), sem("pool_out"))

        def band_terms(t):
            if t == CTX_TILE:
                return [(t, 3)]
            terms = [(t, 1 if t == 0 else 2 if t == CTX_TILE - 1 else 0)]
            if t > 0:
                terms.append((t - 1, 4))
            if t < CTX_TILE - 1:
                terms.append((t + 1, 5))
            return terms

        with nc.Block() as block:
            @block.sync
            def _(sp):
                sp.dma_start(band, k_band.rearrange("n s t -> s n t")).then_inc(pool_in, 16)
                sp.dma_start(wp[0:PD], w_pool.rearrange("g c e -> c g e")).then_inc(pool_in, 16)
                sp.dma_start(ps_row, bass.AP(pool_scale.tensor, 0, [[0, P], [1, PW]])).then_inc(pool_in, 16)

            @block.tensor
            def _(pe):
                pe.wait_ge(pool_in, 48)
                for t in range(NT + 1):
                    if t < NT:
                        if t >= 2:
                            pe.wait_ge(pool_cp, t - 1)
                        for g in range(PG):
                            terms = band_terms(t)
                            for n, (s, b) in enumerate(terms):
                                last = nc.tensor.matmul(bank(t % 2)[0:PD, g * P:(g + 1) * P], pin[:, s, g * PD:(g + 1) * PD],
                                                        band[:, g * 6 + b, :], start=(n == 0), stop=(n == len(terms) - 1))
                        last.then_inc(pool_mm, 1)
                    if t >= 1:
                        u = t - 1
                        pe.wait_ge(pool_cp, u + 1)
                        if u >= 2:
                            pe.wait_ge(pool_out, u - 1)
                        for g in range(PG):
                            last = nc.tensor.matmul(bank(2 + u % 2)[:, g * PD:(g + 1) * PD], pT[u % 2][0:PD, g, :],
                                                    wp[0:PD, g, :], start=True, stop=True)
                        last.then_inc(pool_y, 1)

            @block.scalar
            def _(act):
                for t in range(NT):
                    act.wait_ge(pool_mm, t + 1)
                    if t >= 2:
                        act.wait_ge(pool_y, t - 1)
                    nc.scalar.activation(pT[t % 2][0:PD], bank(t % 2)[0:PD].rearrange("p (g t) -> p g t", g=PG),
                                         ACT.Copy).then_inc(pool_cp, 1)

            @block.vector
            def _(dve):
                for t in range(NT):
                    dve.wait_ge(pool_y, t + 1)
                    nc.vector.tensor_tensor(mix[:, t, AW + MW:D], bank(2 + t % 2)[:, 0:PW], ps_row, ALU.mult).then_inc(pool_out, 1)
        ar.at = mark

        mark = ar.at
        ck, ckT, cv = ar.take([AW]), ar.take([3, P]), ar.take([AW])
        kc_nat = ar.take([AW])
        winmask = ar.take([TAB_SLOTS, GRID_W])
        tab = [ar.take([TAB_SLOTS, GRID_W]) for _ in range(2)]
        SW_ = INNER_ROWS * GRID_W + P
        sc = [ar.take([SW_]) for _ in range(2)]
        pr = [ar.take([SW_]) for _ in range(2)]
        pt = [ar.take([SW_ // P, P]) for _ in range(2)]
        stat = ar.take([HEADS * NT, 4])
        LOCALS = {0: (0, 8, 6), 2: (0, 8, 4), 12: (8, 8, 2), 14: (8, 8, 0)}
        att = []
        for h in range(HEADS):
            for t in range(NT):
                if t == CTX_TILE:
                    att.append((h, t, None, 0, 0))
                elif 2 * t in LOCALS:
                    att.append((h, t) + LOCALS[2 * t])
                else:
                    att.append((h, t, 2 * t - 4, INNER_ROWS, EDGE_SLOTS))
        att_in, ck_turned, ck_ready, tab_in, tab_ready = (sem("att_in"), sem("ck_turned"), sem("ck_ready"), [sem("tab_in0"), sem("tab_in1")], sem("tab_ready"))
        s_mm, s_read, negmax, probs, p_turned, p_cp_act, p_cp_dve, pv_mm, att_out = (sem(n) for n in (
            "score_mm", "score_read", "negmax", "probs", "probs_turned", "pt_copied_act", "pt_copied_dve", "pv_mm", "att_out"))
        dve_att = sem("dve_att")
        with nc.Block() as block:
            @block.sync
            def _(sp):
                sp.dma_start(ck, cache_k).then_inc(att_in, 16)
                sp.dma_start(cv, cache_v).then_inc(att_in, 16)
                sp.dma_start(winmask, k_winmask).then_inc(att_in, 16)
                sp.dma_start(out_v, va[:, CTX_TILE, :]).then_inc(out_stored, 16)
                stored[0] += 16
                for h in range(HEADS):
                    if h >= 2:
                        sp.wait_ge(s_read, NT * (h - 1))
                    for half in range(2):
                        for s0, n, dr in ((0, EDGE_SLOTS, 1 - half), (EDGE_SLOTS, INNER_ROWS, 3 - half)):
                            src = bass.AP(rpb_rows.tensor, (h * RPB_R + dr) * GRID_W * PADW + GRID_W - 1,
                                          [[PADW - 1, GRID_W], [GRID_W * PADW, n], [1, GRID_W]])
                            sp.dma_start(tab[h % 2][GRID_W * half:GRID_W * (half + 1), s0:s0 + n, :],
                                         src).then_inc(tab_in[h % 2], 16)
                    if h == 1:
                        sp.wait_ge(ck_ready, 2)
                        sp.dma_start(out_k, kc_nat).then_inc(out_stored, 16)
                        stored[0] += 16

            @block.gpsimd
            def _(pool):
                pool.wait_ge(att_in, 48)
                for h in range(HEADS):
                    pool.wait_ge(tab_in[h % 2], 64 * (h // 2 + 1))
                    nc.gpsimd.tensor_tensor(tab[h % 2], tab[h % 2], winmask, ALU.add).then_inc(tab_ready, 1)

            def keys(n):
                return n[3] * GRID_W

            def dve_copies(n):
                return n - n // NT

            @block.tensor
            def _(pe):
                pe.wait_ge(att_in, 48)
                for j in range(3):
                    last = nc.tensor.transpose(bank(0)[:, j * P:(j + 1) * P], ck[:, j * P:(j + 1) * P], ident)
                for j in range(3):
                    last = nc.tensor.transpose(bank(2)[:, j * P:(j + 1) * P], kaT[:, j, LAT:TOK], ident)
                last.then_inc(ck_turned, 1)
                pe.wait_ge(ck_ready, 2)

                def score(i):
                    h, t, r0, _, _ = att[i]
                    if i >= 2:
                        pe.wait_ge(s_read, i - 1)
                    rows = slice(HD * (h % 2), HD * (h % 2) + HD)
                    q = qaT[rows, h // 2, t * P:(t + 1) * P]
                    base = 2 * (i % 2)
                    if r0 is None:
                        nc.tensor.matmul(bank(base)[:, 0:P], q, kaT[rows, h // 2, LAT:TOK], start=True, stop=True).then_inc(s_mm, 1)
                        return
                    n = keys(att[i])
                    nc.tensor.matmul(bank(base), q, kaT[rows, h // 2, r0 * GRID_W:r0 * GRID_W + BANK], start=True, stop=True)
                    if n > BANK:
                        nc.tensor.matmul(bank(base + 1)[:, 0:P], q, kaT[rows, h // 2, r0 * GRID_W + BANK:r0 * GRID_W + n], start=True, stop=True)
                    nc.tensor.matmul(bank(base + 1)[:, n - BANK:n - BANK + P], q, ckT[rows, h // 2, :], start=True, stop=True).then_inc(s_mm, 1)

                def turn(i):
                    pe.wait_ge(probs, i + 1)
                    if i >= 1:
                        pe.wait_ge(p_cp_act, i)
                        if dve_copies(i):
                            pe.wait_ge(p_cp_dve, dve_copies(i))
                    for j in range(keys(att[i]) // P + 1):
                        last = nc.tensor.transpose(ps[:, 4 * BANK + j * P:4 * BANK + (j + 1) * P],
                                                   pr[i % 2][:, j * P:(j + 1) * P], ident)
                    last.then_inc(p_turned, 1)

                def weigh(i):
                    h, t, r0, _, _ = att[i]
                    pe.wait_ge(p_cp_act, i + 1)
                    pe.wait_ge(p_cp_dve, dve_copies(i + 1))
                    if i >= 2:
                        pe.wait_ge(att_out, i - 1)
                    out = bank(6 + i % 2)[:, 0:HD]
                    cols = slice(h * HD, (h + 1) * HD)
                    n = keys(att[i]) // P
                    for j in range(n):
                        nc.tensor.matmul(out, pt[i % 2][:, j, :], va[:, r0 // 2 + j, cols], start=(j == 0), stop=False)
                    v = va[:, CTX_TILE, cols] if r0 is None else cv[:, cols]
                    nc.tensor.matmul(out, pt[i % 2][:, n, :], v, start=(n == 0), stop=True).then_inc(pv_mm, 1)

                score(0)
                for i in range(len(att)):
                    if i + 1 < len(att):
                        score(i + 1)
                    if i:
                        weigh(i - 1)
                    turn(i)
                weigh(len(att) - 1)

            @block.scalar
            def _(act):
                for i, u in enumerate(att):
                    n = keys(u)
                    act.wait_ge(negmax, i + 1)
                    if i >= 2:
                        act.wait_ge(p_turned, i - 1)
                    nc.scalar.activation(pr[i % 2][:, 0:n + P], sc[i % 2][:, 0:n + P], ACT.Exp, bias=stat[:, i, 1:2],
                                         accum_out=stat[:, i, 2:3]).then_inc(probs, 1)
                    act.wait_ge(p_turned, i + 1)
                    if i >= 2:
                        act.wait_ge(pv_mm, i - 1)
                    c = min(n // P + 1, 4)
                    nc.scalar.activation(pt[i % 2][:, 0:c, :], bank(4)[:, 0:c * P].rearrange("p (j t) -> p j t", j=c), ACT.Copy).then_inc(p_cp_act, 1)

            @block.vector
            def _(dve):
                st = Steps(dve, dve_att)
                dve.wait_ge(ck_turned, 1)
                nc.vector.tensor_copy(ckT, bank(0)[:, 0:3 * P].rearrange("p (j t) -> p j t", j=3)).then_inc(ck_ready, 1)
                nc.vector.tensor_copy(kc_nat, bank(2)[:, 0:3 * P]).then_inc(ck_ready, 1)

                def bias_and_max(i):
                    h, t, r0, nrows, slot = att[i]
                    n = keys(att[i])
                    if i % NT == 0:
                        dve.wait_ge(tab_ready, h + 1)
                    dve.wait_ge(s_mm, i + 1)
                    if i >= 2:
                        dve.wait_ge(probs, i - 1)
                    base = 2 * (i % 2) * BANK
                    m = stat[:, i, 0:1]
                    if n:
                        ins = nc.vector.tensor_tensor_reduce(
                            out=sc[i % 2][:, 0:n], in0=ps[:, base:base + n],
                            in1=tab[h % 2][:, slot:slot + nrows, :].rearrange("p s k -> p (s k)"), scale=1.0, scalar=-3e38,
                            op0=ALU.add, op1=ALU.max, accum_out=stat[:, i, 3:4])
                        st.link(ins)
                        nc.vector.tensor_scalar(sc[i % 2][:, n:n + P], ps[:, base + n:base + n + P], 0.0, stat[:, i, 3:4],
                                                ALU.add, ALU.max, accum_out=m).then_inc(s_read, 1)
                    else:
                        nc.vector.tensor_scalar(sc[i % 2][:, 0:P], ps[:, base:base + P], 0.0, None,
                                                ALU.add, ALU.max, accum_out=m).then_inc(s_read, 1)
                    dve.wait_ge(s_read, i + 1)
                    nc.vector.tensor_scalar(stat[:, i, 1:2], m, -1.0, None, ALU.mult).then_inc(negmax, 1)

                def copy_turned(i):
                    n = keys(att[i]) // P + 1
                    dve.wait_ge(p_turned, i + 1)
                    if i >= 2:
                        dve.wait_ge(pv_mm, i - 1)
                    if n > 4:
                        nc.vector.tensor_copy(pt[i % 2][:, 4:n, :], bank(5)[:, 0:(n - 4) * P].rearrange("p (j t) -> p j t", j=n - 4)).then_inc(p_cp_dve, 1)

                def normalise(i):
                    h, t = att[i][0:2]
                    dve.wait_ge(probs, i + 1)
                    st.link(nc.vector.reciprocal(stat[:, i, 3:4], stat[:, i, 2:3]))
                    dve.wait_ge(pv_mm, i + 1)
                    nc.vector.tensor_scalar(mix[:, t, h * HD:(h + 1) * HD], bank(6 + i % 2)[:, 0:HD], stat[:, i, 3:4], None, ALU.mult).then_inc(att_out, 1)

                bias_and_max(0)
                for i in range(len(att)):
                    if i + 1 < len(att):
                        bias_and_max(i + 1)
                    if i:
                        normalise(i - 1)
                    copy_turned(i)
                normalise(len(att) - 1)
        ar.at = mark

        ar.at = after_mlstm_in
        cols = ar.take([NT, 4, 64])
        decay = ar.take([8, NT])
        selm = ar.take([8, P])
        r1 = ar.take([TOK])
        keep = ar.at
        giT, gfT, bT, mT, reset, w1, w2 = (ar.take([TOK]) for _ in range(7))
        m0, min_, r1e, ewe = ar.take([1]), ar.take([NT]), ar.take([NT]), ar.take([NT])
        g_in, g_turned, g_copied, f_abs, f_exp, a_rdy, e_rdy, ew_turned, dec_mm, ml_gates = (sem(n) for n in (
            "gate_in", "gate_turned", "gate_copied", "f_abs", "f_softplus", "exps_in", "exps_ready", "cols_turned", "decay_mm", "dve_gates"))
        act_g = sem("act_gates")
        FW, BW = slice(0, 32), slice(32, 64)
        with nc.Block() as block:
            @block.sync
            def _(sp):
                sp.dma_start(selm[0:64], k_sel).then_inc(g_in, 16)
                sp.dma_start(reset[0:64], k_reset).then_inc(g_in, 16)
                sp.wait_ge(ml_gates, 1)
                for way in range(2):
                    sp.dma_start(m0[32 * way:32 * way + MH], state_m[way, :, None]).then_inc(g_in, 16)
                sp.wait_ge(ml_gates, 8)
                sp.dma_start(out_m[0, :, None], mT[0:MH, TOK - 1:TOK]).then_inc(out_stored, 16)
                sp.dma_start(out_m[1, :, None], mT[32:32 + MH, LAT:LAT + 1]).then_inc(out_stored, 16)
                stored[0] += 32
                sp.wait_ge(out_stored, stored[0])

            @block.tensor
            def _(pe):
                for t in range(NT):
                    nc.tensor.transpose(ps[0:64, t * P:(t + 1) * P], gi[:, t, :], ident)
                    last = nc.tensor.transpose(ps[0:64, 4 * BANK + t * P:4 * BANK + (t + 1) * P], gf[:, t, :], ident)
                last.then_inc(g_turned, 1)
                pe.wait_ge(e_rdy, 3)
                pe.wait_ge(a_rdy, 2)
                pe.wait_ge(g_in, 64)
                for t in range(NT):
                    for n, src in enumerate((giT, w1, gfT, w2)):
                        last = nc.tensor.transpose(ps[:, (4 * t + n) * 64:(4 * t + n + 1) * 64], src[0:64, t * P:(t + 1) * P], ident[0:64, 0:64])
                last.then_inc(ew_turned, 1)
                for r in range(8):
                    last = nc.tensor.matmul(bank(6)[:, r * NT:(r + 1) * NT], selm[0:64, r, :], ewe[0:64], start=True, stop=True)
                last.then_inc(dec_mm, 1)

            @block.scalar
            def _(act):
                st = Steps(act, act_g)
                act.wait_ge(f_abs, 1)
                st.link(nc.scalar.activation(w1[0:64], w1[0:64], ACT.Exp, scale=-1.0))
                nc.scalar.activation(w1[0:64], w1[0:64], ACT.Ln, bias=1.0).then_inc(f_exp, 1)
                act.wait_ge(a_rdy, 1)
                nc.scalar.activation(w1[0:64], w1[0:64], ACT.Exp).then_inc(e_rdy, 1)
                nc.scalar.activation(w2[0:64], w2[0:64], ACT.Exp).then_inc(e_rdy, 1)
                nc.scalar.activation(gfT[0:64], mT[0:64], ACT.Exp, scale=-1.0).then_inc(e_rdy, 1)

            @block.vector
            def _(dve):
                st = Steps(dve, ml_gates)
                st.add(nc.vector.memset(m0[0:64], 0.0))
                dve.wait_ge(g_turned, 1)
                nc.vector.tensor_copy(giT[0:64], ps[0:64, 0:TOK]).then_inc(g_copied, 1)
                nc.vector.tensor_copy(gfT[0:64], ps[0:64, 4 * BANK:4 * BANK + TOK]).then_inc(g_copied, 1)
                dve.wait_ge(g_copied, 2)
                nc.vector.scalar_tensor_tensor(out=w1[0:64], in0=gfT[0:64], scalar=-1.0, in1=gfT[0:64], op0=ALU.mult, op1=ALU.max).then_inc(f_abs, 1)
                dve.wait_ge(f_exp, 1)
                st.link(nc.vector.scalar_tensor_tensor(out=gfT[0:64], in0=gfT[0:64], scalar=0.0, in1=w1[0:64], op0=ALU.min, op1=ALU.subtract))
                dve.wait_ge(g_in, 64)
                st.add(nc.vector.tensor_tensor_scan(bT[FW], reset[FW], gfT[FW], 0.0, ALU.mult, ALU.add))
                st.add(nc.vector.tensor_tensor_scan(bT[BW][:, ::-1], reset[BW][:, ::-1], gfT[BW][:, ::-1], 0.0, ALU.mult, ALU.add))
                for seg, init in ((slice(0, LAT), True), (slice(LAT, TOK), False)):
                    for rows, way in ((FW, 0), (BW, 1)):
                        o, a, b = (x[rows, seg] for x in (mT, gfT, giT))
                        if way:
                            o, a, b = (x[:, ::-1] for x in (o, a, b))
                        st.add(nc.vector.tensor_tensor_scan(o, a, b, m0[rows, 0:1] if init else 0.0, ALU.add, ALU.max))
                st.settle()
                st.add(nc.vector.tensor_tensor(r1[0:64], bT[0:64], mT[0:64], ALU.subtract))
                st.add(nc.vector.memset(min_[0:64], 0.0))
                st.link(nc.vector.tensor_tensor(giT[0:64], giT[0:64], bT[0:64], ALU.subtract))
                v3 = lambda x, rows: x[rows].rearrange("p (c t) -> p c t", c=NT)
                st.add(nc.vector.tensor_copy(min_[FW, 0:1], m0[FW]))
                st.add(nc.vector.tensor_copy(min_[FW, 1:8], v3(mT, FW)[:, 0:7, P - 1]))
                st.add(nc.vector.tensor_copy(min_[BW, 7:8], m0[BW]))
                st.add(nc.vector.tensor_copy(min_[BW, 0:7], v3(mT, BW)[:, 1:8, 0]))
                st.add(nc.vector.tensor_copy(r1e[FW], v3(r1, FW)[:, :, P - 1]))
                st.link(nc.vector.tensor_copy(r1e[BW], v3(r1, BW)[:, :, 0]))
                A = slice(0, 64)
                st.add(nc.vector.tensor_tensor(v3(w1, A), v3(r1, A), bc(min_[A, :, None], (64, NT, P)), ALU.add))
                st.settle()
                nc.vector.tensor_tensor(v3(w2, A), v3(giT, A), bc(r1e[A, :, None], (64, NT, P)), ALU.add).then_inc(a_rdy, 1)
                dve.wait_ge(e_rdy, 3)
                st.add(nc.vector.tensor_copy(ewe[FW], v3(w1, FW)[:, :, P - 1]))
                st.settle()
                nc.vector.tensor_copy(ewe[BW], v3(w1, BW)[:, :, 0]).then_inc(a_rdy, 1)
                dve.wait_ge(ew_turned, 1)
                st.add(nc.vector.tensor_copy(cols, ps[:, 0:NT * 256].rearrange("p (t n r) -> p t n r", t=NT, n=4)))
                dve.wait_ge(dec_mm, 1)
                st.add(nc.vector.tensor_copy(decay, bank(6)[:, 0:8 * NT].rearrange("p (r t) -> p r t", r=8)))
        ar.at = keep

        sw = ar.take([8, NT, P])
        knat = ar.take([NT, MW])
        keep_s = ar.at
        scanmask = ar.take([2, P])
        am = [ar.take([NT, P]) for _ in range(2)]
        ew = [ar.take([NT, P]) for _ in range(2)]
        sm_in, am_rdy, bc_mm, ew_add, ew_exp, sw_rdy, kn_turned, kn_cp = (sem(n) for n in (
            "scanmask_in", "a_masked", "weights_mm", "weights_added", "weights_exp", "sw_ready", "k_turned", "k_copied"))

        def a_col(t, way, h0=0, n=1):
            return cols[:, t, 0, 32 * way + h0:32 * way + h0 + n]

        with nc.Block() as block:
            @block.sync
            def _(sp):
                sp.dma_start(scanmask, k_scanmask.rearrange("w s t -> s w t")).then_inc(sm_in, 16)

            @block.gpsimd
            def _(pool):
                pool.wait_ge(sm_in, 16)
                for r in range(8):
                    way, h = divmod(r, 4)
                    if r >= 2:
                        pool.wait_ge(ew_add, r - 1)
                    nc.gpsimd.tensor_tensor(am[r % 2], bc(scanmask[:, way:way + 1, :], (P, NT, P)),
                                            bc(cols[:, :, 0, 32 * way + h:32 * way + h + 1], (P, NT, P)), ALU.add).then_inc(am_rdy, 1)

            @block.tensor
            def _(pe):
                for r in range(8):
                    h = r % 4
                    if r >= 1:
                        pe.wait_ge(ew_add, r)
                    for t0, n in ((0, 512), (512, 512), (1024, 128)):
                        nc.tensor.matmul(ps[:, t0:t0 + n], selm[0:64, r, :], r1[0:64, t0:t0 + n], start=True, stop=True)
                    if r >= 1:
                        pe.wait_ge(sw_rdy, r)
                    for t in range(NT):
                        last = nc.tensor.matmul(ps[:, 3 * BANK + t * P:3 * BANK + (t + 1) * P], kbT[0:MD, h, t * P:(t + 1) * P],
                                                qbT[0:MD, h, t * P:(t + 1) * P], start=True, stop=True)
                    last.then_inc(bc_mm, 1)
                    for t in ([r, 8] if r == 7 else [r]):
                        if t >= 2:
                            pe.wait_ge(kn_cp, t - 1)
                        for hh in range(MH):
                            last = nc.tensor.transpose(bank(6 + t % 2)[:, hh * MD:(hh + 1) * MD], kbT[0:MD, hh, t * P:(t + 1) * P], ident[0:MD, 0:MD])
                        last.then_inc(kn_turned, 1)

            @block.scalar
            def _(act):
                for r in range(8):
                    act.wait_ge(ew_add, r + 1)
                    nc.scalar.activation(ew[r % 2], ew[r % 2], ACT.Exp).then_inc(ew_exp, 1)
                    for t in ([r, 8] if r == 7 else [r]):
                        act.wait_ge(kn_turned, t + 1)
                        nc.scalar.activation(knat[:, t, :], bank(6 + t % 2)[:, 0:MW], ACT.Copy).then_inc(kn_cp, 1)

            @block.vector
            def _(dve):
                for r in range(8):
                    dve.wait_ge(bc_mm, r + 1)
                    dve.wait_ge(am_rdy, r + 1)
                    if r >= 2:
                        dve.wait_ge(sw_rdy, r - 1)
                    nc.vector.tensor_tensor(ew[r % 2], ps[:, 0:TOK].rearrange("p (c t) -> p c t", c=NT), am[r % 2], ALU.add).then_inc(ew_add, 1)
                    dve.wait_ge(ew_exp, r + 1)
                    nc.vector.tensor_tensor(sw[:, r], ew[r % 2], ps[:, 3 * BANK:3 * BANK + TOK].rearrange("p (c t) -> p c t", c=NT), ALU.mult).then_inc(sw_rdy, 1)
        ar.at = keep_s

        cs = ar.take([8, MA])
        cctx = ar.take([8, MA])
        hn = [ar.take([MH, MA]) for _ in range(2)]
        ct = ar.take([MH, MA])
        dn = ar.take([MH])
        KW_RING = 4
        kw = [ar.take([MW]) for _ in range(KW_RING)]
        sq = sw[:, 0:3].rearrange("p r c t -> p (r c t)").rearrange("p (n d) -> p n d", d=MD)
        ssb, lnb, ysb, tb = (ar.take([NT * MH]) for _ in range(4))
        mln = ar.take([MW])
        c_in, sc_mm, sc_used, c_new, hb_mean, hb_guess, hb_sq, c_ctx_rdy, kw_rdy = (sem(n) for n in (
            "state_in", "scan_mm", "scan_used", "state_new", "hb_mean", "hb_guess", "hb_squares", "ctx_state_ready", "keys_weighted"))
        dve_scan, act_scan = sem("dve_scan"), sem("act_scan")
        order = [(CTX_TILE, 0), (CTX_TILE, 1)]
        for c in range(8):
            order += [(c, 0), (7 - c, 1)]
        hb = mix[:, :, AW:AW + MW]
        with nc.Block() as block:
            @block.sync
            def _(sp):
                for way in range(2):
                    sp.dma_start(cs[0:MD, MH * way:MH * way + MH, 0:MD], state_C[way].rearrange("h d e -> d h e")).then_inc(c_in, 16)
                    sp.dma_start(cs[0:MD, MH * way:MH * way + MH, MD], state_n[way].rearrange("h d -> d h")).then_inc(c_in, 16)
                sp.dma_start(mln, bass.AP(ml_norm.tensor, 0, [[0, P], [1, MW]])).then_inc(c_in, 16)
                sp.wait_ge(c_ctx_rdy, 2)
                for way in range(2):
                    sp.dma_start(out_C[way].rearrange("h d e -> d h e"), cctx[0:MD, MH * way:MH * way + MH, 0:MD]).then_inc(out_stored, 16)
                    sp.dma_start(out_n[way].rearrange("h d -> d h"), cctx[0:MD, MH * way:MH * way + MH, MD]).then_inc(out_stored, 16)
                stored[0] += 64
                sp.wait_ge(out_stored, stored[0])

            @block.gpsimd
            def _(pool):
                for i, (t, way) in enumerate(order):
                    if i >= KW_RING:
                        pool.wait_ge(sc_mm, i - KW_RING + 1)
                    nc.gpsimd.tensor_tensor(kw[i % KW_RING].rearrange("p (h d) -> p h d", h=MH),
                                            knat[:, t, :].rearrange("p (h d) -> p h d", h=MH),
                                            bc(cols[:, t, 3, 32 * way:32 * way + MH][:, :, None], (P, MH, MD)), ALU.mult).then_inc(kw_rdy, 1)

            @block.tensor
            def _(pe):
                pe.wait_ge(c_in, 80)
                for i, (t, way) in enumerate(order):
                    pe.wait_ge(kw_rdy, i + 1)
                    b = 3 * (i % 2)
                    if i >= 2:
                        pe.wait_ge(sc_used, i - 1)
                    for h in range(MH):
                        nc.tensor.matmul(bank(b)[:, h * MA:(h + 1) * MA], sw[:, MH * way + h, t, :], vb[:, t, h, :], start=True, stop=True)
                    for h in range(MH):
                        last = nc.tensor.matmul(bank(b + 2)[0:MD, h * MA:(h + 1) * MA], kw[i % KW_RING][:, h * MD:(h + 1) * MD], vb[:, t, h, :], start=True, stop=True)
                    if t != CTX_TILE:
                        for h in range(MH):
                            last = nc.tensor.matmul(bank(b + 1)[:, h * MA:(h + 1) * MA], qbT[0:MD, h, t * P:(t + 1) * P], cs[0:MD, MH * way + h, :], start=True, stop=True)
                    last.then_inc(sc_mm, 1)

            @block.scalar
            def _(act):
                st = Steps(act, act_scan)
                act.wait_ge(hb_mean, 1)
                st.link(nc.scalar.activation(lnb, ssb, ACT.Ln))
                nc.scalar.activation(ysb, lnb, ACT.Exp, scale=-0.5).then_inc(hb_guess, 1)

            @block.vector
            def _(dve):
                st = Steps(dve, dve_scan)
                dve.wait_ge(c_in, 80)
                p4 = lambda n, rows=P: bank(n)[0:rows, 0:MH * MA].rearrange("p (h e) -> p h e", h=MH)
                for i, (t, way) in enumerate(order):
                    b = 3 * (i % 2)
                    hs = slice(MH * way, MH * way + MH)
                    dve.wait_ge(sc_mm, i + 1)
                    num = hn[i % 2]
                    w = lambda n: cols[:, t, n, 32 * way:32 * way + MH]
                    if t == CTX_TILE:
                        nc.vector.tensor_copy(cctx[0:MD, hs, :], p4(b + 2, MD)).then_inc(c_ctx_rdy, 1)
                        st.link(nc.vector.tensor_copy(num, p4(b)))
                    else:
                        st.link(nc.vector.tensor_tensor(ct[0:MD], cs[0:MD, hs, :], bc(decay[0:MD, hs, t:t + 1], (MD, MH, MA)), ALU.mult))
                        st.add(nc.vector.tensor_tensor(cs[0:MD, hs, :], ct[0:MD], p4(b + 2, MD), ALU.add))
                        st.link(nc.vector.tensor_tensor(num, p4(b + 1), bc(w(1)[:, :, None], (P, MH, MA)), ALU.mult))
                        st.link(nc.vector.tensor_tensor(num, num, p4(b), ALU.add))
                    st.link(nc.vector.scalar_tensor_tensor(out=dn[:, :, None], in0=num[:, :, MD:MA], scalar=-1.0, in1=num[:, :, MD:MA], op0=ALU.mult, op1=ALU.max))
                    st.link(nc.vector.tensor_tensor(dn, dn, w(2), ALU.max))
                    st.link(nc.vector.reciprocal(dn, dn))
                    dst = hb[:, t, :].rearrange("p (h d) -> p h d", h=MH)
                    first = (way == 0 and t <= 3) or (way == 1 and 4 <= t < 8) or (way == 0 and t == CTX_TILE)
                    if first:
                        nc.vector.tensor_tensor(dst, num[:, :, 0:MD], bc(dn[:, :, None], (P, MH, MD)), ALU.mult).then_inc(sc_used, 1)
                    else:
                        st.link(nc.vector.tensor_tensor(num[:, :, 0:MD], num[:, :, 0:MD], bc(dn[:, :, None], (P, MH, MD)), ALU.mult))
                        nc.vector.tensor_tensor(dst, dst, num[:, :, 0:MD], ALU.add).then_inc(sc_used, 1)
                dve.wait_ge(sc_used, len(order))
                for t in range(NT):
                    h4 = hb[:, t, :].rearrange("p (h d) -> p h d", h=MH)
                    st.add(nc.vector.tensor_tensor(sq[:, MH * t:MH * t + MH, :], h4, h4, ALU.mult))
                st.settle()
                st.link(nc.vector.tensor_reduce(ssb, sq, AX.X, ALU.add))
                nc.vector.tensor_scalar(ssb, ssb, 1.0 / MD, EPS, ALU.mult, ALU.add).then_inc(hb_mean, 1)
                dve.wait_ge(hb_guess, 1)
                st.link(nc.vector.tensor_tensor(tb, ysb, ysb, ALU.mult))
                st.link(nc.vector.scalar_tensor_tensor(out=tb, in0=tb, scalar=-0.5, in1=ssb, op0=ALU.mult, op1=ALU.mult))
                st.link(nc.vector.scalar_tensor_tensor(out=ysb, in0=tb, scalar=1.5, in1=ysb, op0=ALU.add, op1=ALU.mult))
                for t in range(NT):
                    h4 = hb[:, t, :].rearrange("p (h d) -> p h d", h=MH)
                    st.add(nc.vector.tensor_tensor(og[:, t, :], og[:, t, :], mln, ALU.mult))
                    st.link(nc.vector.tensor_tensor(h4, h4, bc(ysb[:, MH * t:MH * t + MH][:, :, None], (P, MH, MD)), ALU.mult))
                    st.link(nc.vector.tensor_tensor(hb[:, t, :], hb[:, t, :], og[:, t, :], ALU.mult))
        ar.at = mark_h

        x1 = ar.take([NT, D])
        h2 = ar.take([NT, D])
        after_x1 = ar.at
        wo = ar.take([KD, D])
        g1 = ar.take([2, D])
        mt = [ar.take([KD, P]) for _ in range(2)]
        o_in, ox_in, o_turned, o_cp, o_mm, o_add = (sem(n) for n in ("wo_in", "ox_in", "mix_turned", "mix_copied", "out_mm", "out_add"))
        dve_o = sem("dve_out")
        with nc.Block() as block:
            @block.sync
            def _(sp):
                sp.dma_start(g1, mod_row(2)).then_inc(o_in, 16)
                sp.dma_start(wo, w_out.rearrange("(k p) n -> p k n", p=P)).then_inc(o_in, 16)
                for t in range(NT):
                    sp.dma_start(x1[:, t, :], x_all[t * P:(t + 1) * P, :]).then_inc(ox_in, 16)

            @block.tensor
            def _(pe):
                def turn(t):
                    if t >= 2:
                        pe.wait_ge(o_cp, t - 1)
                    for k in range(KD):
                        at = 2 * (t % 2) * BANK + k * P
                        last = nc.tensor.transpose(ps[:, at:at + P], mix[:, t, k * P:(k + 1) * P], ident)
                    last.then_inc(o_turned, 1)

                turn(0)
                pe.wait_ge(o_in, 32)
                for t in range(NT):
                    if t + 1 < NT:
                        turn(t + 1)
                    pe.wait_ge(o_cp, t + 1)
                    if t >= 2:
                        pe.wait_ge(o_add, 2 * (t - 1))
                    for half in range(2):
                        for k in range(KD):
                            last = nc.tensor.matmul(bank(4 + 2 * (t % 2) + half), mt[t % 2][:, k, :], wo[:, k, half * BANK:(half + 1) * BANK],
                                                    start=(k == 0), stop=(k == KD - 1))
                    last.then_inc(o_mm, 1)

            @block.scalar
            def _(act):
                for t in range(NT):
                    act.wait_ge(o_turned, t + 1)
                    if t >= 2:
                        act.wait_ge(o_mm, t - 1)
                    for half in range(2):
                        ins = nc.scalar.activation(mt[t % 2][:, 4 * half:4 * half + 4, :], bank(2 * (t % 2) + half).rearrange("p (k t) -> p k t", k=4), ACT.Copy)
                    ins.then_inc(o_cp, 1)

            @block.vector
            def _(dve):
                st = Steps(dve, dve_o)
                dve.wait_ge(o_in, 32)
                dve.wait_ge(ox_in, 16 * NT)
                for t in range(NT):
                    dve.wait_ge(o_mm, t + 1)
                    for half in range(2):
                        hs = slice(half * BANK, (half + 1) * BANK)
                        st.link(nc.vector.tensor_tensor(h2[:, t, hs], bank(4 + 2 * (t % 2) + half), g1[:, side(t), hs], ALU.mult))
                        nc.vector.tensor_tensor(x1[:, t, hs], x1[:, t, hs], h2[:, t, hs], ALU.add).then_inc(o_add, 1)
        ar.at = after_x1

        h2T = mix.rearrange("p t d -> p (t d)").rearrange("p (k t) -> p k t", k=KD)
        norm_stage("n2_", x1, (3, 4), h2, h2T, None)

        wr = ar.take([KD, NE])
        upper, ones = ar.take([P]), ar.take([P])
        brr, tids = ar.take([NE]), ar.take([N_SLOT_TILES])
        NEt = NT * NE
        lg, sco, sel, cmpb = ar.take([NEt]), ar.take([NEt]), ar.take([NEt]), ar.take([NEt * EPG])
        rank, oh1, oh2, tmp, both, sl = (ar.take([NEt]) for _ in range(6))
        gs, gr = ar.take([NT * EG]), ar.take([NT * EG])
        gcmp = ar.take([NT * EG * EG])
        base_ = ar.take([NT, NE])
        tot = ar.take([NT, NE])
        cnt, ntl, cum, off = (ar.take([NE]) for _ in range(4))
        s12, rden = ar.take([3, NT]), ar.take([NT])
        tcmp = ar.take([N_SLOT_TILES, NE])
        tef = ar.take([N_SLOT_TILES])
        r_in, r_mm, r_exp, both_rdy, pos_mm, slot_rdy, scattered, dve_r = (sem(n) for n in (
            "router_in", "router_mm", "router_exp", "picked", "position_mm", "slot_ready", "scattered", "dve_router"))
        with nc.Block() as block:
            @block.sync
            def _(sp):
                sp.dma_start(wr, w_router.rearrange("(k p) n -> p k n", p=P)).then_inc(r_in, 16)
                sp.dma_start(upper, k_upper).then_inc(r_in, 16)
                sp.dma_start(brr, bass.AP(b_router.tensor, 0, [[0, P], [1, NE]])).then_inc(r_in, 16)
                sp.dma_start(tids, bass.AP(k_tile_ids.tensor, 0, [[0, P], [1, N_SLOT_TILES]])).then_inc(r_in, 16)

            @block.tensor
            def _(pe):
                pe.wait_ge(r_in, 64)
                for t in range(NT):
                    for k in range(KD):
                        last = nc.tensor.matmul(bank(0)[:, t * NE:(t + 1) * NE], h2T[:, k, t * P:(t + 1) * P], wr[:, k, :],
                                                start=(k == 0), stop=(k == KD - 1))
                last.then_inc(r_mm, 1)
                pe.wait_ge(both_rdy, 1)
                nc.tensor.matmul(bank(1)[:, 0:NEt], upper, both, start=True, stop=True)
                nc.tensor.matmul(bank(2)[:, 0:NEt], ones, both, start=True, stop=True).then_inc(pos_mm, 1)

            @block.scalar
            def _(act):
                act.wait_ge(r_mm, 1)
                nc.scalar.activation(lg, bank(0)[:, 0:NEt], ACT.Exp, scale=-1.0).then_inc(r_exp, 1)

            @block.gpsimd
            def _(pool):
                pool.wait_ge(slots_zeroed, 16 * N_SLOT_TILES)
                pool.wait_ge(slot_rdy, 1)
                for t in range(NT):
                    for n in range(2):
                        pool.indirect_dma_start(slot_x, bass.IndirectOffsetOnAxis(slot[n].bitcast(U32)[:, t:t + 1], 0), h2[:, t, :], None).then_inc(scattered, 16)
                pool.wait_ge(scattered, 16 * 2 * NT)

            @block.vector
            def _(dve):
                st = Steps(dve, dve_r)
                v = nc.vector
                st.add(v.memset(ones, 1.0))
                st.add(v.memset(cmpb, 0.0))
                st.add(v.memset(gcmp, 0.0))
                st.add(v.memset(base_, 0.0))
                dve.wait_ge(r_in, 64)
                dve.wait_ge(r_exp, 1)
                st.link(v.tensor_scalar(lg, lg, 1.0, None, ALU.add))
                st.link(v.reciprocal(sco, lg))
                st.link(v.tensor_tensor(sel.rearrange("p (t e) -> p t e", t=NT), sco.rearrange("p (t e) -> p t e", t=NT),
                                        bc(brr[:, None, :], (P, NT, NE)), ALU.add))

                def ranks(src, cmp, out, n):
                    s4 = src.rearrange("p (n e) -> p n e", e=4)
                    c4 = cmp.rearrange("p (n e f) -> p n e f", e=4, f=4)
                    for f in range(4):
                        if f < 3:
                            st.add(v.tensor_tensor(c4[:, :, f + 1:4, f], bc(s4[:, :, f:f + 1], (P, n, 3 - f)), s4[:, :, f + 1:4], ALU.is_ge))
                        if f > 0:
                            st.add(v.tensor_tensor(c4[:, :, 0:f, f], bc(s4[:, :, f:f + 1], (P, n, f)), s4[:, :, 0:f], ALU.is_gt))
                    st.settle()
                    st.link(v.tensor_reduce(out.rearrange("p (n e) -> p n e", e=4), c4, AX.X, ALU.add))

                ranks(sel, cmpb, rank, NT * EG)
                st.add(v.tensor_scalar(oh1, rank, 0.0, None, ALU.is_equal))
                st.add(v.tensor_scalar(oh2, rank, 1.0, None, ALU.is_equal))
                st.link(v.scalar_tensor_tensor(out=tmp, in0=rank, scalar=2.0, in1=sel, op0=ALU.is_lt, op1=ALU.mult))
                st.link(v.tensor_reduce(gs, tmp.rearrange("p (n e) -> p n e", e=EPG), AX.X, ALU.add))
                ranks(gs, gcmp, gr, NT)
                st.link(v.tensor_scalar(gs, gr, 0.0, None, ALU.is_equal))
                g4 = bc(gs[:, :, None], (P, NT * EG, EPG))
                for oh in (oh1, oh2):
                    o4 = oh.rearrange("p (n e) -> p n e", e=EPG)
                    st.add(v.tensor_tensor(o4, o4, g4, ALU.mult))
                st.settle()
                v.tensor_tensor(both, oh1, oh2, ALU.add).then_inc(both_rdy, 1)
                for n, oh in enumerate((oh1, oh2)):
                    st.link(v.tensor_tensor(tmp, sco, oh, ALU.mult))
                    st.link(v.tensor_reduce(s12[:, n, :], tmp.rearrange("p (t e) -> p t e", t=NT), AX.X, ALU.add))
                st.link(v.tensor_tensor(rden, s12[:, 0, :], s12[:, 1, :], ALU.add))
                st.link(v.reciprocal(rden, rden))
                for n in range(2):
                    st.add(v.tensor_tensor(gate[n], s12[:, n, :], rden, ALU.mult))
                dve.wait_ge(pos_mm, 1)
                st.link(v.tensor_copy(tot, bank(2)[:, 0:NEt].rearrange("p (t e) -> p t e", t=NT)))
                for t in range(1, NT):
                    st.link(v.tensor_tensor(base_[:, t, :], base_[:, t - 1, :], tot[:, t - 1, :], ALU.add))
                st.link(v.tensor_tensor(cnt, base_[:, NT - 1, :], tot[:, NT - 1, :], ALU.add))
                st.link(v.tensor_scalar(ntl, cnt, 0.0, None, ALU.is_gt))
                for k in range(1, NT):
                    st.link(v.scalar_tensor_tensor(out=ntl, in0=cnt, scalar=float(P * k), in1=ntl, op0=ALU.is_gt, op1=ALU.add))
                st.link(v.tensor_tensor_scan(cum, ones[:, 0:NE], ntl, 0.0, ALU.mult, ALU.add))
                st.link(v.tensor_tensor(off, cum, ntl, ALU.subtract))
                st.link(v.tensor_scalar(off, off, float(P), None, ALU.mult))
                s3 = sl.rearrange("p (t e) -> p t e", t=NT)
                st.link(v.tensor_tensor(s3, base_, bc(off[:, None, :], (P, NT, NE)), ALU.add))
                st.link(v.tensor_tensor(sl, sl, bank(1)[:, 0:NEt], ALU.add))
                for n, oh in enumerate((oh1, oh2)):
                    st.link(v.tensor_tensor(tmp, sl, oh, ALU.mult))
                    st.link(v.tensor_reduce(s12[:, 2, :], tmp.rearrange("p (t e) -> p t e", t=NT), AX.X, ALU.add))
                    st.link(v.tensor_copy(slot[n].bitcast(U32), s12[:, 2, :]))
                st.link(v.tensor_tensor(tcmp, bc(cum[:, None, :], (P, N_SLOT_TILES, NE)), bc(tids[:, :, None], (P, N_SLOT_TILES, NE)), ALU.is_le))
                st.link(v.tensor_reduce(tef, tcmp, AX.X, ALU.add))
                st.link(v.tensor_scalar(tef, tef, float(NE - 1), None, ALU.min))
                v.tensor_copy(te.bitcast(I32), tef).then_inc(slot_rdy, 1)
        ar.at = after_x1 - NT * D

        wg, wu = [ar.take([KD, DF]) for _ in range(2)], [ar.take([KD, DF]) for _ in range(2)]
        wd = [ar.take([KF, D]) for _ in range(2)]
        xs = [ar.take([D]) for _ in range(2)]
        xT = [ar.take([KD, P]) for _ in range(2)]
        ge = ar.take([DF])
        hid = ar.take([DF])
        hidT = [ar.take([KF, P]) for _ in range(2)]
        yo = [ar.take([D]) for _ in range(2)]
        x_ld, gu_ld, d_ld = ([sem(f"slot_x_in{s}") for s in range(2)], [sem(f"gate_up_in{s}") for s in range(2)], [sem(f"down_in{s}") for s in range(2)])
        x_turned, x_cp, gu_mm, g_exp, g_dve, hid_rdy, h_turned, h_cp, dn_mm, y_rdy = (sem(n) for n in (
            "slot_turned", "slot_copied", "gate_up_mm", "gate_exp", "dve_experts", "hid_ready", "hid_turned", "hid_copied", "down_mm", "y_ready"))
        y_st = [sem(f"y_stored{s}") for s in range(2)]
        LAST = N_SLOT_TILES // 2 - 1
        with nc.Block() as block:
            @block.sync
            def _(sp):
                def load(i, first):
                    for s in range(2):
                        j = 2 * i + s
                        e = sp.value_load(te.bitcast(I32)[0:1, bass.ds(j, 1)], min_val=0, max_val=NE - 1)
                        if not first:
                            sp.wait_ge(x_turned, j - 1)
                        sp.dma_start(xs[s], slot_x[bass.ds(j * P, P), :]).then_inc(x_ld[s], 16)
                        if not first:
                            sp.wait_ge(gu_mm, j - 1)
                        sp.dma_start(wg[s], w_gate[e].rearrange("(k p) n -> p k n", p=P)).then_inc(gu_ld[s], 16)
                        sp.dma_start(wu[s], w_up[e].rearrange("(k p) n -> p k n", p=P)).then_inc(gu_ld[s], 16)
                        if not first:
                            sp.wait_ge(dn_mm, j - 1)
                        sp.dma_start(wd[s], w_down[e].rearrange("(k p) n -> p k n", p=P)).then_inc(d_ld[s], 16)

                load(0, True)
                with sp.Fori(1, LAST + 1) as i:
                    load(i, False)

            @block.tensor
            def _(pe):
                def turn_x(j, s, i):
                    pe.wait_ge(x_ld[s], 16 * (i + 1))
                    for k in range(KD):
                        last = nc.tensor.transpose(ps[:, k * P:(k + 1) * P], xs[s][:, k * P:(k + 1) * P], ident)
                    last.then_inc(x_turned, 1)

                def gate_up(j, s, i, first):
                    pe.wait_ge(gu_ld[s], 32 * (i + 1))
                    pe.wait_ge(x_cp, j + 1)
                    if not first:
                        pe.wait_ge(hid_rdy, j)
                    for b, w in ((2, wg[s]), (3, wu[s])):
                        for k in range(KD):
                            last = nc.tensor.matmul(bank(b), xT[s][:, k, :], w[:, k, :], start=(k == 0), stop=(k == KD - 1))
                    last.then_inc(gu_mm, 1)

                def down(j, s, i, first):
                    pe.wait_ge(hid_rdy, j + 1)
                    for k in range(KF):
                        last = nc.tensor.transpose(bank(4)[:, k * P:(k + 1) * P], hid[:, k * P:(k + 1) * P], ident)
                    last.then_inc(h_turned, 1)
                    pe.wait_ge(d_ld[s], 16 * (i + 1))
                    pe.wait_ge(h_cp, j + 1)
                    if not first:
                        pe.wait_ge(y_rdy, j)
                    for half in range(2):
                        for k in range(KF):
                            last = nc.tensor.matmul(bank(5 + half), hidT[s][:, k, :], wd[s][:, k, half * BANK:(half + 1) * BANK],
                                                    start=(k == 0), stop=(k == KF - 1))
                    last.then_inc(dn_mm, 1)

                def turn(i, first=False, last=False):
                    gate_up(2 * i, 0, i, first)
                    if not first:
                        down(2 * i - 1, 1, i - 1, False)
                    turn_x(2 * i + 1, 1, i)
                    gate_up(2 * i + 1, 1, i, False)
                    down(2 * i, 0, i, first)
                    if not last:
                        turn_x(2 * i + 2, 0, i + 1)

                turn_x(0, 0, 0)
                turn(0, first=True)
                with pe.Fori(1, LAST) as i:
                    turn(i)
                turn(LAST, last=True)
                down(N_SLOT_TILES - 1, 1, LAST, False)

            @block.scalar
            def _(act):
                def copy_x(j, s, first):
                    act.wait_ge(x_turned, j + 1)
                    if not first:
                        act.wait_ge(gu_mm, j - 1)
                    for half in range(2):
                        ins = nc.scalar.activation(xT[s][:, 4 * half:4 * half + 4, :], bank(half).rearrange("p (k t) -> p k t", k=4), ACT.Copy)
                    ins.then_inc(x_cp, 1)

                def gate_exp(j):
                    act.wait_ge(gu_mm, j + 1)
                    nc.scalar.activation(ge, bank(2), ACT.Exp, scale=-1.0).then_inc(g_exp, 1)

                def copy_hid(j, s, first):
                    act.wait_ge(h_turned, j + 1)
                    if not first:
                        act.wait_ge(dn_mm, j - 1)
                    nc.scalar.activation(hidT[s], bank(4).rearrange("p (k t) -> p k t", k=KF), ACT.Copy).then_inc(h_cp, 1)

                def turn(i, first=False, last=False):
                    gate_exp(2 * i)
                    if not first:
                        copy_hid(2 * i - 1, 1, False)
                    copy_x(2 * i + 1, 1, first)
                    gate_exp(2 * i + 1)
                    copy_hid(2 * i, 0, first)
                    if not last:
                        copy_x(2 * i + 2, 0, False)

                copy_x(0, 0, True)
                turn(0, first=True)
                with act.Fori(1, LAST) as i:
                    turn(i)
                turn(LAST, last=True)
                copy_hid(N_SLOT_TILES - 1, 1, False)

            @block.vector
            def _(dve):
                st = Steps(dve, g_dve)

                def silu(j, link):
                    dve.wait_ge(g_exp, j + 1)
                    if not (isinstance(j, int) and j == 0):
                        dve.wait_ge(h_turned, j)
                    link(nc.vector.tensor_scalar(ge, ge, 1.0, None, ALU.add), 1)
                    link(nc.vector.reciprocal(ge, ge), 2)
                    link(nc.vector.tensor_tensor(hid, bank(2), ge, ALU.mult), 3)
                    nc.vector.tensor_tensor(hid, hid, bank(3), ALU.mult).then_inc(hid_rdy, 1)

                def store(j, s, i, first):
                    dve.wait_ge(dn_mm, j + 1)
                    if not first:
                        dve.wait_ge(y_st[s], 16 * i)
                    for half in range(2):
                        ins = nc.vector.tensor_copy(yo[s][:, half * BANK:(half + 1) * BANK], bank(5 + half))
                    ins.then_inc(y_rdy, 1)

                def linker(j):
                    def link(ins, n):
                        ins.then_inc(g_dve, 1)
                        dve.wait_ge(g_dve, 3 * j + n)
                    return link

                def turn(i, first=False):
                    silu(2 * i, linker(2 * i))
                    if not first:
                        store_prev(i)
                    silu(2 * i + 1, linker(2 * i + 1))
                    store(2 * i, 0, i, first)

                def store_prev(i):
                    dve.wait_ge(dn_mm, 2 * i)
                    if not (isinstance(i, int) and i == 1):
                        dve.wait_ge(y_st[1], 16 * (i - 1))
                    for half in range(2):
                        ins = nc.vector.tensor_copy(yo[1][:, half * BANK:(half + 1) * BANK], bank(5 + half))
                    ins.then_inc(y_rdy, 1)

                turn(0, first=True)
                turn(1)
                with dve.Fori(2, LAST + 1) as i:
                    turn(i)
                store_prev(LAST + 1)

            @block.gpsimd
            def _(pool):
                with pool.Fori(0, LAST + 1) as i:
                    for s in range(2):
                        pool.wait_ge(y_rdy, 2 * i + s + 1)
                        pool.dma_start(slot_y[bass.ds((2 * i + s) * P, P), :], yo[s]).then_inc(y_st[s], 16)
                for s in range(2):
                    pool.wait_ge(y_st[s], 16 * (LAST + 1))
        ar.at = after_x1
        g2 = ar.take([2, D])
        fn = ar.take([D])
        ya, yb = ([ar.take([D]) for _ in range(2)] for _ in range(2))
        z = [ar.take([D]) for _ in range(2)]
        junk = ar.take([D])
        fs = ar.take([NT, 4])
        f_in, z_rdy, z_sq, z_mean, z_guess, z_out, dve_f, act_f = (sem(n) for n in (
            "final_in", "z_ready", "z_squares", "z_mean", "z_guess", "z_out", "dve_final", "act_final"))
        y_in = [sem("rows_in0"), sem("rows_in1")]
        y_stored = [sem("y_out0"), sem("y_out1")]
        with nc.Block() as block:
            @block.sync
            def _(sp):
                sp.dma_start(g2, mod_row(5)).then_inc(f_in, 16)
                sp.dma_start(fn, bass.AP(final_norm.tensor, 0, [[0, P], [1, D]])).then_inc(f_in, 16)
                for t in range(NT):
                    sp.wait_ge(z_out, t + 1)
                    sp.dma_start(y_all[t * P:(t + 1) * P, :], z[t % 2]).then_inc(y_stored[t % 2], 16)
                for s in range(2):
                    sp.wait_ge(y_stored[s], 16 * ((NT + 1 - s) // 2))
                sp.wait_ge(out_stored, stored[0])

            @block.gpsimd
            def _(pool):
                for t in range(NT):
                    if t >= 2:
                        pool.wait_ge(z_rdy, t - 1)
                    for n, y in enumerate((ya, yb)):
                        pool.indirect_dma_start(y[t % 2], None, slot_y, bass.IndirectOffsetOnAxis(slot[n].bitcast(U32)[:, t:t + 1], 0)).then_inc(y_in[t % 2], 16)

            @block.scalar
            def _(act):
                st = Steps(act, act_f)
                for t in range(NT):
                    act.wait_ge(z_rdy, t + 1)
                    if t:
                        st.settle()
                    st.link(nc.scalar.activation(junk, z[t % 2], ACT.Square, accum_out=fs[:, t, 0:1]))
                    nc.scalar.activation(junk[:, 0:1], fs[:, t, 0:1], ACT.Square).then_inc(z_sq, 1)
                    act.wait_ge(z_mean, t + 1)
                    st.link(nc.scalar.activation(fs[:, t, 1:2], fs[:, t, 0:1], ACT.Ln))
                    nc.scalar.activation(fs[:, t, 2:3], fs[:, t, 1:2], ACT.Exp, scale=-0.5).then_inc(z_guess, 1)
                    act.wait_ge(z_sq, t + 1)

            @block.vector
            def _(dve):
                st = Steps(dve, dve_f)
                v = nc.vector
                dve.wait_ge(f_in, 32)
                for t in range(NT):
                    dve.wait_ge(y_in[t % 2], 32 * (t // 2 + 1))
                    if t >= 2:
                        dve.wait_ge(y_stored[t % 2], 16 * (t // 2))
                    zt = z[t % 2]
                    st.link(v.tensor_scalar(zt, ya[t % 2], gate[0][:, t:t + 1], None, ALU.mult))
                    st.link(v.scalar_tensor_tensor(out=zt, in0=yb[t % 2], scalar=gate[1][:, t:t + 1], in1=zt, op0=ALU.mult, op1=ALU.add))
                    st.link(v.tensor_tensor(zt, zt, g2[:, side(t), :], ALU.mult))
                    v.tensor_tensor(zt, zt, x1[:, t, :], ALU.add).then_inc(z_rdy, 1)
                    dve.wait_ge(z_sq, t + 1)
                    f = lambda n: fs[:, t, n:n + 1]
                    v.tensor_scalar(f(0), f(0), 1.0 / D, EPS, ALU.mult, ALU.add).then_inc(z_mean, 1)
                    dve.wait_ge(z_guess, t + 1)
                    st.link(v.tensor_tensor(f(3), f(2), f(2), ALU.mult))
                    st.link(v.scalar_tensor_tensor(out=f(3), in0=f(3), scalar=-0.5, in1=f(0), op0=ALU.mult, op1=ALU.mult))
                    st.link(v.scalar_tensor_tensor(out=f(2), in0=f(3), scalar=1.5, in1=f(2), op0=ALU.add, op1=ALU.mult))
                    v.scalar_tensor_tensor(out=zt, in0=zt, scalar=f(2), in1=fn, op0=ALU.mult, op1=ALU.mult).then_inc(z_out, 1)


def constants():
    f = np.float32
    ident = np.eye(P, dtype=f)
    upper = np.triu(np.ones((P, P), f), 1)
    sel = np.zeros((64, 8, P), f)
    for way in range(2):
        for h in range(MH):
            sel[32 * way + h, MH * way + h, :] = 1
    s, t = np.arange(P)[:, None], np.arange(P)[None, :]
    scanmask = np.stack([np.where(s <= t, 0, NEG), np.where(s >= t, 0, NEG)]).astype(f)
    reset = np.ones((64, TOK), f)
    reset[:32, 0::P] = 0
    reset[32:, P - 1::P] = 0
    q = np.arange(GRID_W)
    start = np.clip(q - KCOLS // 2, 0, GRID_W - KCOLS)[:, None]
    k = np.arange(GRID_W)[None, :]
    window = np.where((k >= start) & (k < start + KCOLS), 0, NEG).astype(f)
    winmask = np.tile(window[None, :, None, :], (2, 1, TAB_SLOTS, 1))
    winmask[0, :, EDGE_SLOTS + 8:, :] = NEG
    winmask[1, :, EDGE_SLOTS, :] = NEG
    winmask[1, :, EDGE_SLOTS + 9, :] = NEG
    winmask = winmask.reshape(P, TAB_SLOTS, GRID_W)
    band = np.zeros((PG, 6, P, P), f)
    for g, w in enumerate(WINDOWS):
        for b, (lo_end, hi_end) in enumerate(((False, False), (True, False), (False, True), (True, True))):
            for tt in range(P):
                lo, hi = tt - w // 2, tt - w // 2 + w
                n_lo, n_hi = max(lo, 0) if lo_end else lo, min(hi, P) if hi_end else hi
                band[g, b, max(lo, 0):min(hi, P), tt] = f(1) / f(n_hi - n_lo)
                band[g, b, tt, tt] -= 1
                if b == 0:
                    if lo < 0:
                        band[g, 4, P + lo:P, tt] = f(1) / f(w)
                    if hi > P:
                        band[g, 5, 0:hi - P, tt] = f(1) / f(w)
    return {"k_ident": ident, "k_upper": upper, "k_sel": sel, "k_scanmask": scanmask, "k_reset": reset,
            "k_winmask": winmask, "k_band": band.reshape(PG * 6, P, P), "k_tile_ids": np.arange(N_SLOT_TILES, dtype=f)}


def kernel(**inputs):
    import concourse.bacc as bacc
    from concourse.bass_utils import run_bass_kernel_spmd as run

    a = {k: np.ascontiguousarray(v) for k, v in inputs.items()}
    ins = {
        "x_all": np.concatenate([a["x_sample"].reshape(LAT, D), a["x_prompt"].reshape(CTX, D)]),
        "cache_k": a["cache_k_attn"].reshape(CTX, AW), "cache_v": a["cache_v_attn"].reshape(CTX, AW),
        "state_C": a["state_mlstm_C"].reshape(2, MH, MD, MD), "state_n": a["state_mlstm_n"].reshape(2, MH, MD),
        "state_m": a["state_mlstm_m"].reshape(2, MH), "c_both": np.stack([a["c"].reshape(D), a["c_ctx"].reshape(D)]),
        "w_ada": a["w_ada"].reshape(D, 6 * D), "b_ada": a["b_ada"].reshape(6 * D), "norm1": a["norm1"].reshape(D),
        "w_in": a["w_in"].reshape(D, -1), "b_in": a["b_in"].reshape(-1),
        "rpb_pad": np.pad(a["rpb"].reshape(HEADS, RPB_R, RPB_C), ((0, 0), (0, 0), (GRID_W - KCOLS, GRID_W - KCOLS))),
        "ml_norm": a["ml_norm"].reshape(MW), "w_pool": a["w_pool"].reshape(PG, PD, PD), "pool_scale": a["pool_scale"].reshape(PW),
        "w_out": a["w_out"].reshape(D, D), "norm2": a["norm2"].reshape(D), "w_router": a["w_router"], "b_router": a["b_router"],
        "w_gate": a["w_gate"].reshape(NE, D, DF), "w_up": a["w_up"].reshape(NE, D, DF), "w_down": a["w_down"].reshape(NE, DF, D),
        "final_norm": a["final_norm"], **constants(),
    }
    outs = {"y_all": (TOK, D), "out_k": (CTX, AW), "out_v": (CTX, AW), "out_C": (2, MH, MD, MD), "out_n": (2, MH, MD), "out_m": (2, MH)}
    nc = bacc.Bacc("TRN2", target_bir_lowering=False, num_devices=1)
    aps = {k: nc.dram_tensor("in_" + k, v.shape, F32, kind="ExternalInput").ap() for k, v in ins.items()}
    aps |= {k: nc.dram_tensor(k, s, F32, kind="ExternalOutput").ap() for k, s in outs.items()}
    program(nc, **aps)
    r = run(nc, [{"in_" + k: v for k, v in ins.items()}], core_ids=[0]).results[0]
    y = r["y_all"]
    return (y[LAT:].reshape(1, CTX, D), y[:LAT].reshape(1, LAT, D),
            r["out_k"].reshape(1, 1, CTX, HEADS, HD), r["out_v"].reshape(1, 1, CTX, HEADS, HD),
            r["out_C"].reshape(1, 1, 2, MH, MD, MD), r["out_n"].reshape(1, 1, 2, MH, MD), r["out_m"].reshape(1, 1, 2, MH))
```

```python
from contextlib import ExitStack

import numpy as np

import concourse.bass as bass
from concourse import mybir

F32 = mybir.dt.float32
U32 = mybir.dt.uint32
I32 = mybir.dt.int32
ALU = mybir.AluOpType
ACT = mybir.ActivationFunctionType
AX = mybir.AxisListType

P = 128
D = 1024
KD = D // P
LAT, CTX = 1024, 128
TOK = LAT + CTX
NT = TOK // P
CTX_TILE = NT - 1
EPS = 1e-6
NEG = -1e30
BANK = 512

HEADS, HD = 6, 64
AW = HEADS * HD
GRID_W, ROWS = 64, 16
KROWS, KCOLS = 8, 16
EDGE_SLOTS = 14
INNER_ROWS = 10
TAB_SLOTS = EDGE_SLOTS + INNER_ROWS
RPB_R, RPB_C = 15, 31
PADW = 2 * GRID_W - 1

MH, MD = 4, 96
MW = MH * MD
MA = MD + 1
PG, PD = 4, 64
PW = PG * PD
WINDOWS = (2, 4, 8, 16)
N_GATES = 16
C_QA, C_KA, C_VA = 0, AW, 2 * AW
C_QB = 3 * AW
C_KB, C_VB, C_OB, C_TAIL = C_QB + MW, C_QB + 2 * MW, C_QB + 3 * MW, C_QB + 4 * MW
TAIL = N_GATES + PW

NE, EG, EPG, DF = 16, 4, 4, 512
KF = DF // P
N_SLOT_TILES = 34
SLOTS = N_SLOT_TILES * P
MIN_TILES = 2 * TOK // P
X_TILES = N_SLOT_TILES + 2


class Steps:

    def __init__(self, engine, sem):
        self.engine, self.sem, self.n = engine, sem, 0

    def add(self, instruction):
        instruction.then_inc(self.sem, 1)
        self.n = self.n + 1
        return instruction

    def settle(self):
        self.engine.wait_ge(self.sem, self.n)

    def link(self, instruction):
        self.add(instruction)
        self.settle()


class Arena:

    def __init__(self, tensor, columns):
        self.tensor, self.columns, self.at, self.high = tensor, columns, 0, 0

    def take(self, shape, rows=P):
        n = int(np.prod(shape))
        a = self.tensor[0:rows, self.at:self.at + n]
        self.at += n
        self.high = max(self.high, self.at)
        assert self.at <= self.columns, (self.at, self.columns)
        if len(shape) == 2:
            a = a.rearrange("p (a b) -> p a b", a=shape[0])
        if len(shape) == 3:
            a = a.rearrange("p (a b c) -> p a b c", a=shape[0], b=shape[1])
        return a


def bc(ap, shape):
    return ap.to_broadcast(list(shape))


def program(nc, x_all, cache_k, cache_v, state_C, state_n, state_m, c_both, w_ada, b_ada, norm1, w_in, b_in,
            rpb_pad, ml_norm, w_pool, pool_scale, w_out, norm2, w_router, b_router, w_gate, w_up, w_down,
            final_norm, k_ident, k_upper, k_sel, k_scanmask, k_reset, k_winmask, k_band, k_tile_ids,
            y_all, out_k, out_v, out_C, out_n, out_m):
    ctx = ExitStack()
    with ctx, nc.allow_non_contiguous_dma(reason="biases, states and modulation inputs as columns"):
        sb = ctx.enter_context(nc.sbuf_tensor("sb", [P, 52992], F32))
        ps = ctx.enter_context(nc.psum_tensor("ps", [P, 8 * BANK], F32))
        ar = Arena(sb, 52992)

        def sem(name):
            return ctx.enter_context(nc.semaphore(name))

        def bank(n, cols=BANK, at=0):
            return ps[:, n * BANK + at:n * BANK + at + cols]

        mod_rows = nc.dram_tensor("mod_rows", [2, 6 * D], F32, kind="Internal").ap()
        rpb_rows = nc.dram_tensor("rpb_rows", [HEADS * RPB_R, GRID_W, PADW], F32, kind="Internal").ap()
        slot_x = nc.dram_tensor("slot_x", [X_TILES * P, D], F32, kind="Internal").ap()
        slot_y = nc.dram_tensor("slot_y", [SLOTS, D], F32, kind="Internal").ap()

        ident = ar.take([P])
        zero_tile = ar.take([D])
        gate = [ar.take([NT]) for _ in range(2)]
        slot = [ar.take([NT]) for _ in range(2)]
        te = ar.take([N_SLOT_TILES + 2 + NE])
        ss2, ln2, y2, t2 = (ar.take([NT]) for _ in range(4))
        const_ready = sem("const_ready")
        zero_ready = sem("zero_ready")
        slots_zeroed = sem("slots_zeroed")
        out_stored = sem("out_stored")
        stored = [0]

        start_h = ar.at
        ar.take([KD, TOK])
        mark_h = ar.at
        x_res = ar.take([NT, D])
        ss, lnv, y0, nt1 = (ar.take([NT]) for _ in range(4))
        sq_junk = ar.take([D])
        cc = ar.take([2, KD])
        ce = ar.take([2, KD])
        ada = [ar.take([KD, BANK]) for _ in range(2)]
        brow = ar.take([6 * D])
        nrow = ar.take([2, D])
        mrow = ar.take([6 * D])
        c_ready = sem("c_ready")
        silu_exp = sem("silu_exp")
        silu_done = sem("silu_done")
        ada_loaded = [sem(f"ada_loaded{s}") for s in range(2)]
        mod_mm = sem("mod_mm")
        mod_evac = sem("mod_evac")
        mod_ready = sem("mod_ready")
        mod_stored = sem("mod_stored")
        x_loaded = sem("x_loaded")
        dve_mod, act_mod = sem("dve_mod"), sem("act_mod")
        squares, mean_ready, guess_ready = sem("n1_squares"), sem("n1_mean"), sem("n1_guess")
        MOD_BLOCKS, EARLY_BLOCKS = 6 * D // BANK, 2 * D // BANK
        ada_src = w_ada.rearrange("(k p) n -> p k n", p=P)

        def load_ada(sp, n):
            if n >= 2:
                sp.wait_ge(mod_mm, n - 1)
            sp.dma_start(ada[n % 2], ada_src[:, :, n * BANK:(n + 1) * BANK]).then_inc(ada_loaded[n % 2], 16)

        def multiply_ada(pe, n):
            pe.wait_ge(ada_loaded[n % 2], 16 * (n // 2 + 1))
            if n >= 2:
                pe.wait_ge(mod_evac, n - 1)
            for k in range(KD):
                last = nc.tensor.matmul(bank(2 + n % 2)[0:2], cc[:, :, k], ada[n % 2][:, k, :],
                                        start=(k == 0), stop=(k == KD - 1))
            last.then_inc(mod_mm, 1)

        def read_ada(dve, n):
            dve.wait_ge(mod_mm, n + 1)
            cols_n = slice(n * BANK, (n + 1) * BANK)
            nc.vector.tensor_tensor(mrow[0:2, cols_n], bank(2 + n % 2)[0:2], brow[0:2, cols_n], ALU.add).then_inc(mod_evac, 1)

        def scale_ada(part, v):
            row = mrow[0:2, part * D:(part + 1) * D]
            nc.vector.scalar_tensor_tensor(out=row, in0=row, scalar=1.0, in1=nrow[0:2, v],
                                           op0=ALU.add, op1=ALU.mult).then_inc(mod_ready, 1)

        def newton(st, y, t, ms):
            st.link(nc.vector.tensor_tensor(t, y, y, ALU.mult))
            st.link(nc.vector.scalar_tensor_tensor(out=t, in0=t, scalar=-0.5, in1=ms, op0=ALU.mult, op1=ALU.mult))
            st.link(nc.vector.scalar_tensor_tensor(out=y, in0=t, scalar=1.5, in1=y, op0=ALU.add, op1=ALU.mult))

        with nc.Block() as block:
            @block.sync
            def _(sp):
                for v in range(2):
                    sp.dma_start(cc[:, v, :], c_both[v].rearrange("(k p) -> p k", p=P)).then_inc(c_ready, 16)
                sp.dma_start(brow[0:2], bass.AP(b_ada.tensor, 0, [[0, 2], [1, 6 * D]])).then_inc(c_ready, 16)
                for v, n in enumerate((norm1, norm2)):
                    sp.dma_start(nrow[0:2, v], bass.AP(n.tensor, 0, [[0, 2], [1, D]])).then_inc(c_ready, 16)
                for n in range(EARLY_BLOCKS):
                    load_ada(sp, n)
                sp.wait_ge(mod_ready, 1)
                sp.dma_start(mod_rows[:, 0:2 * D], mrow[0:2, 0:2 * D]).then_inc(mod_stored, 16)
                sp.wait_ge(mod_stored, 16)

            @block.scalar
            def _(act):
                st = Steps(act, act_mod)
                act.dma_start(ident, k_ident).then_inc(const_ready, 16)
                act.dma_start(x_res, x_all.rearrange("(t p) d -> p t d", p=P)).then_inc(x_loaded, 16)
                act.wait_ge(c_ready, 16 * 5)
                nc.scalar.activation(ce, cc, ACT.Exp, scale=-1.0).then_inc(silu_exp, 1)
                act.wait_ge(x_loaded, 16)
                for t in range(NT):
                    if t:
                        st.settle()
                    st.add(nc.scalar.activation(sq_junk, x_res[:, t, :], ACT.Square, accum_out=ss[:, t:t + 1]))
                st.settle()
                nc.scalar.activation(sq_junk[:, 0:1], ss[:, 0:1], ACT.Square).then_inc(squares, 1)
                act.wait_ge(mean_ready, 1)
                st.link(nc.scalar.activation(lnv, ss, ACT.Ln))
                nc.scalar.activation(y0, lnv, ACT.Exp, scale=-0.5).then_inc(guess_ready, 1)
                act.wait_ge(const_ready, 16)

            @block.vector
            def _(dve):
                st = Steps(dve, dve_mod)
                dve.wait_ge(silu_exp, 1)
                st.link(nc.vector.tensor_scalar(ce, ce, 1.0, None, ALU.add))
                st.link(nc.vector.reciprocal(ce, ce))
                nc.vector.tensor_tensor(cc, cc, ce, ALU.mult).then_inc(silu_done, 1)
                for n in range(EARLY_BLOCKS):
                    read_ada(dve, n)
                dve.wait_ge(mod_evac, EARLY_BLOCKS)
                scale_ada(1, 0)
                dve.wait_ge(squares, 1)
                nc.vector.tensor_scalar(ss, ss, 1.0 / D, EPS, ALU.mult, ALU.add).then_inc(mean_ready, 1)
                dve.wait_ge(guess_ready, 1)
                newton(st, y0, nt1, ss)

            @block.tensor
            def _(pe):
                pe.wait_ge(silu_done, 1)
                for n in range(EARLY_BLOCKS):
                    multiply_ada(pe, n)

        def mod_row(part):
            return bass.AP(mod_rows.tensor, part * D, [[0, P], [6 * D, 2], [1, D]])

        def side(t):
            return 1 if t == CTX_TILE else 0

        def norm_stage(tag, x, rinv, rows_of, nat, outT, sp_more=None, pe_more=None, dve_more=None, dve_last=None):
            mark = ar.at
            scale_row, shift_row = ar.take([2, D]), ar.take([2, D])
            ring = nat is None
            if ring:
                two = [ar.take([D]) for _ in range(2)]
            row_loaded = sem(tag + "row_loaded")
            nat_ready, turned, copied, dve_s = (sem(tag + n) for n in ("nat_ready", "turned", "copied", "dve"))
            nat_of = lambda t: two[t % 2] if ring else nat[:, t, :]
            with nc.Block() as block:
                @block.sync
                def _(sp):
                    for row, part in zip((shift_row, scale_row), rows_of):
                        sp.dma_start(row, mod_row(part)).then_inc(row_loaded, 16)
                    if sp_more:
                        sp_more(sp)

                @block.scalar
                def _(act):
                    for t in range(NT):
                        act.wait_ge(turned, t + 1)
                        for half in range(2):
                            ins = nc.scalar.activation(
                                outT[:, 4 * half:4 * half + 4, t * P:(t + 1) * P],
                                bank(4 * (t % 2) + half).rearrange("p (k t) -> p k t", k=4), ACT.Copy)
                        ins.then_inc(copied, 1)

                @block.vector
                def _(dve):
                    st = Steps(dve, dve_s)
                    dve.wait_ge(row_loaded, 32)
                    for t in range(NT):
                        if ring and t >= 2:
                            dve.wait_ge(turned, t - 1)
                        st.link(nc.vector.scalar_tensor_tensor(
                            out=nat_of(t), in0=x[:, t, :], scalar=rinv[:, t:t + 1], in1=scale_row[:, side(t), :],
                            op0=ALU.mult, op1=ALU.mult))
                        nc.vector.tensor_tensor(nat_of(t), nat_of(t), shift_row[:, side(t), :],
                                                ALU.add).then_inc(nat_ready, 1)
                        if dve_more:
                            dve_more(dve, t)
                    if dve_last:
                        dve_last(dve)

                @block.tensor
                def _(pe):
                    for t in range(NT):
                        pe.wait_ge(nat_ready, t + 1)
                        if t >= 2:
                            pe.wait_ge(copied, t - 1)
                        for k in range(KD):
                            last = nc.tensor.transpose(
                                ps[:, (4 * (t % 2)) * BANK + k * P:(4 * (t % 2)) * BANK + (k + 1) * P],
                                nat_of(t)[:, k * P:(k + 1) * P], ident)
                        last.then_inc(turned, 1)
                        if pe_more:
                            pe_more(pe, t, copied)
            ar.at = mark

        hT = sb[:, start_h:mark_h].rearrange("p (k t) -> p k t", k=KD)

        def rest_sp(sp):
            for n in range(EARLY_BLOCKS, MOD_BLOCKS):
                load_ada(sp, n)
            sp.dma_start(rpb_rows, bass.AP(rpb_pad.tensor, 0, [[PADW, HEADS * RPB_R], [0, GRID_W], [1, PADW]])).then_inc(mod_stored, 16)
            sp.wait_ge(mod_ready, 2)
            sp.dma_start(mod_rows[:, 2 * D:6 * D], mrow[0:2, 2 * D:6 * D]).then_inc(mod_stored, 16)
            sp.wait_ge(mod_stored, 48)

        def rest_pe(pe, t, copied):
            if t < MOD_BLOCKS - EARLY_BLOCKS:
                multiply_ada(pe, EARLY_BLOCKS + t)

        def rest_dve(dve, t):
            if t < MOD_BLOCKS - EARLY_BLOCKS:
                read_ada(dve, EARLY_BLOCKS + t)

        def rest_scale(dve):
            dve.wait_ge(mod_evac, MOD_BLOCKS)
            scale_ada(4, 1)

        norm_stage("n1_", x_res, y0, (0, 1), None, hT, rest_sp, rest_pe, rest_dve, rest_scale)
        ar.at = mark_h

        qbT, kbT = ar.take([MH, TOK]), ar.take([MH, TOK])
        vb = ar.take([NT, MH, MA])
        og = ar.take([NT, MW])
        gi, gf = ar.take([NT, 64]), ar.take([NT, 64])
        after_mlstm_in = ar.at
        qaT, kaT = ar.take([HEADS, TOK]), ar.take([3, TOK])
        va = ar.take([NT, AW])
        after_attention_in = ar.at
        pin = ar.take([NT, PW])
        after_proj = ar.at
        wring = [ar.take([KD, AW]) for _ in range(2)]
        bias_a, bias_b = ar.take([6]), ar.take([8])
        bias_row = ar.take([3 * MW + TAIL])
        ofs = {C_VA: 0, C_VB: MW, C_OB: 2 * MW, C_TAIL: 3 * MW}
        groups = [("T", C_QA, AW), ("T", C_KA, AW), ("N", C_VA, AW), ("T", C_QB, MW), ("T", C_KB, MW),
                  ("N", C_VB, MW), ("N", C_OB, MW), ("N", C_TAIL, TAIL)]
        units = []
        for g, (kind, c0, n) in enumerate(groups):
            if kind == "T":
                m = P if c0 < C_VA else MD
                for b in range(n // m):
                    units += [(g, b, m, t0, tn) for t0, tn in ((0, 512), (512, 512), (1024, 128))]
            else:
                units += [(g, t, n, t * P, P) for t in range(NT)]
        last_of = {g: max(i for i, u in enumerate(units) if u[0] == g) for g in range(len(groups))}
        w_loaded = [sem(f"w_loaded{s}") for s in range(2)]
        bias_loaded = sem("bias_loaded")
        proj_mm, proj_evac = sem("proj_mm"), sem("proj_evac")
        dve_proj, sig_exp, sig_in = sem("dve_proj"), sem("sig_exp"), sem("sig_in")
        with nc.Block() as block:
            @block.sync
            def _(sp):
                src = w_in.rearrange("(k p) n -> p k n", p=P)
                sp.dma_start(bias_a, b_in[0:2 * AW].rearrange("(b p) -> p b", p=P)).then_inc(bias_loaded, 16)
                sp.dma_start(bias_b[0:MD], b_in[C_QB:C_QB + 2 * MW].rearrange("(b p) -> p b", p=MD)).then_inc(bias_loaded, 16)
                for c0, at in ofs.items():
                    n = TAIL if c0 == C_TAIL else MW
                    sp.dma_start(bias_row[:, at:at + n], bass.AP(b_in.tensor, c0, [[0, P], [1, n]])).then_inc(bias_loaded, 16)
                for g, (_, c0, n) in enumerate(groups):
                    if g >= 2:
                        sp.wait_ge(proj_mm, last_of[g - 2] + 1)
                    sp.dma_start(wring[g % 2][:, :, 0:n], src[:, :, c0:c0 + n]).then_inc(w_loaded[g % 2], 16)

            @block.tensor
            def _(pe):
                seen = set()
                for i, (g, b, m, t0, tn) in enumerate(units):
                    if g not in seen:
                        seen.add(g)
                        pe.wait_ge(w_loaded[g % 2], 16 * (g // 2 + 1))
                    if i >= 8:
                        pe.wait_ge(proj_evac, i - 7)
                    w = wring[g % 2]
                    for k in range(KD):
                        if groups[g][0] == "T":
                            last = nc.tensor.matmul(bank(i % 8)[0:m, 0:tn], w[:, k, b * m:(b + 1) * m],
                                                    hT[:, k, t0:t0 + tn], start=(k == 0), stop=(k == KD - 1))
                        else:
                            last = nc.tensor.matmul(bank(i % 8)[:, 0:m], hT[:, k, t0:t0 + P], w[:, k, 0:m],
                                                    start=(k == 0), stop=(k == KD - 1))
                    last.then_inc(proj_mm, 1)

            @block.gpsimd
            def _(pool):
                nc.gpsimd.memset(zero_tile, 0.0).then_inc(zero_ready, 1)
                nc.gpsimd.memset(qaT, 0.0).then_inc(sig_in, 1)
                nc.gpsimd.memset(vb, 1.0).then_inc(sig_in, 1)
                nc.gpsimd.memset(gi, 0.0).then_inc(sig_in, 1)
                nc.gpsimd.memset(gf, 0.0).then_inc(sig_in, 1)
                pool.wait_ge(zero_ready, 1)
                with pool.Fori(0, X_TILES) as j:
                    pool.dma_start(slot_x[bass.ds(j * P, P), :], zero_tile).then_inc(slots_zeroed, 16)
                with pool.Fori(MIN_TILES, N_SLOT_TILES) as j:
                    pool.dma_start(slot_y[bass.ds(j * P, P), :], zero_tile).then_inc(slots_zeroed, 16)
                pool.wait_ge(slots_zeroed, 16 * (X_TILES + N_SLOT_TILES - MIN_TILES))

            @block.scalar
            def _(act):
                act.wait_ge(proj_evac, last_of[6] + 1)
                nc.scalar.activation(og, og, ACT.Exp, scale=-1.0).then_inc(sig_exp, 1)

            @block.vector
            def _(dve):
                st = Steps(dve, dve_proj)
                dve.wait_ge(bias_loaded, 16 * 6)
                dve.wait_ge(sig_in, 4)
                for i, (g, b, m, t0, tn) in enumerate(units):
                    dve.wait_ge(proj_mm, i + 1)
                    c0 = groups[g][1]
                    p = bank(i % 8)
                    if groups[g][0] == "T":
                        if c0 < C_VA:
                            dst, bias = (qaT if c0 == C_QA else kaT), bias_a[:, (c0 // P) + b:(c0 // P) + b + 1]
                            scale = HD ** -0.5 if c0 == C_QA else 1.0
                        else:
                            col = (0 if c0 == C_QB else MH) + b
                            dst, bias = (qbT if c0 == C_QB else kbT), bias_b[0:MD, col:col + 1]
                            scale = float(MD) ** -0.5 if c0 == C_QB else 1.0
                        if c0 == C_QA:
                            for half in range(2):
                                rows = slice(HD * half, HD * half + HD)
                                ins = nc.vector.tensor_scalar(qaT[rows, 2 * b + half, t0:t0 + tn], p[rows, 0:tn], bias[rows],
                                                              scale, ALU.add, ALU.mult)
                        else:
                            ins = nc.vector.tensor_scalar(dst[0:m, b, t0:t0 + tn], p[0:m, 0:tn], bias, scale, ALU.add, ALU.mult)
                    else:
                        row = bias_row[:, ofs[c0]:ofs[c0] + m]
                        if c0 == C_VA:
                            ins = nc.vector.tensor_tensor(va[:, b, :], p[:, 0:m], row, ALU.add)
                        elif c0 == C_VB:
                            ins = nc.vector.tensor_tensor(vb[:, b, :, 0:MD], p[:, 0:m].rearrange("p (h d) -> p h d", h=MH),
                                                          row.rearrange("p (h d) -> p h d", h=MH), ALU.add)
                        elif c0 == C_OB:
                            ins = nc.vector.tensor_tensor(og[:, b, :], p[:, 0:m], row, ALU.add)
                        else:
                            for dst, at in ((gi, 0), (gf, MH)):
                                for way in range(2):
                                    c = at + 2 * MH * way
                                    st.add(nc.vector.tensor_tensor(dst[:, b, 32 * way:32 * way + MH], p[:, c:c + MH],
                                                                   row[:, c:c + MH], ALU.add))
                            ins = nc.vector.tensor_tensor(pin[:, b, :], p[:, N_GATES:TAIL], row[:, N_GATES:TAIL], ALU.add)
                    ins.then_inc(proj_evac, 1)
                dve.wait_ge(sig_exp, 1)
                st.link(nc.vector.tensor_scalar(og, og, 1.0, None, ALU.add))
                st.link(nc.vector.reciprocal(og, og))
        ar.at = start_h
        mix = ar.take([NT, D])
        ar.at = after_proj

        mark = ar.at
        band = ar.take([PG * 6, P])
        wp = ar.take([PG, PD])
        ps_row = ar.take([PW])
        pT = [ar.take([PG, P]) for _ in range(2)]
        pool_in, pool_mm, pool_cp, pool_y, pool_out = (sem("pool_in"), sem("pool_mm"), sem("pool_cp"), sem("pool_y"), sem("pool_out"))

        def band_terms(t):
            if t == CTX_TILE:
                return [(t, 3)]
            terms = [(t, 1 if t == 0 else 2 if t == CTX_TILE - 1 else 0)]
            if t > 0:
                terms.append((t - 1, 4))
            if t < CTX_TILE - 1:
                terms.append((t + 1, 5))
            return terms

        with nc.Block() as block:
            @block.sync
            def _(sp):
                sp.dma_start(band, k_band).then_inc(pool_in, 16)
                sp.dma_start(wp[0:PD], w_pool.rearrange("g c e -> c g e")).then_inc(pool_in, 16)
                sp.dma_start(ps_row, bass.AP(pool_scale.tensor, 0, [[0, P], [1, PW]])).then_inc(pool_in, 16)

            @block.tensor
            def _(pe):
                pe.wait_ge(pool_in, 48)
                for t in range(NT + 1):
                    if t < NT:
                        if t >= 2:
                            pe.wait_ge(pool_cp, t - 1)
                        for g in range(PG):
                            terms = band_terms(t)
                            for n, (s, b) in enumerate(terms):
                                last = nc.tensor.matmul(bank(t % 2)[0:PD, g * P:(g + 1) * P], pin[:, s, g * PD:(g + 1) * PD],
                                                        band[:, g * 6 + b, :], start=(n == 0), stop=(n == len(terms) - 1))
                        last.then_inc(pool_mm, 1)
                    if t >= 1:
                        u = t - 1
                        pe.wait_ge(pool_cp, u + 1)
                        if u >= 2:
                            pe.wait_ge(pool_out, u - 1)
                        for g in range(PG):
                            last = nc.tensor.matmul(bank(2 + u % 2)[:, g * PD:(g + 1) * PD], pT[u % 2][0:PD, g, :],
                                                    wp[0:PD, g, :], start=True, stop=True)
                        last.then_inc(pool_y, 1)

            @block.scalar
            def _(act):
                for t in range(NT):
                    act.wait_ge(pool_mm, t + 1)
                    if t >= 2:
                        act.wait_ge(pool_y, t - 1)
                    nc.scalar.activation(pT[t % 2][0:PD], bank(t % 2)[0:PD].rearrange("p (g t) -> p g t", g=PG),
                                         ACT.Copy).then_inc(pool_cp, 1)

            @block.vector
            def _(dve):
                for t in range(NT):
                    dve.wait_ge(pool_y, t + 1)
                    nc.vector.tensor_tensor(mix[:, t, AW + MW:D], bank(2 + t % 2)[:, 0:PW], ps_row, ALU.mult).then_inc(pool_out, 1)
        ar.at = mark

        ar.at = after_attention_in
        ck, ckT, cv = ar.take([AW]), ar.take([3, P]), ar.take([AW])
        kc_nat = ar.take([AW])
        winmask = ar.take([TAB_SLOTS, GRID_W])
        tab = [ar.take([TAB_SLOTS, GRID_W]) for _ in range(2)]
        SW_ = INNER_ROWS * GRID_W + P
        sc = [ar.take([SW_]) for _ in range(2)]
        pr = [ar.take([SW_]) for _ in range(2)]
        pt = [ar.take([SW_ // P, P]) for _ in range(2)]
        stat = ar.take([HEADS * NT, 4])
        LOCALS = {0: (0, 8, 6), 2: (0, 8, 4), 12: (8, 8, 2), 14: (8, 8, 0)}
        att = []
        for h in range(HEADS):
            for t in range(NT):
                if t == CTX_TILE:
                    att.append((h, t, None, 0, 0))
                elif 2 * t in LOCALS:
                    att.append((h, t) + LOCALS[2 * t])
                else:
                    att.append((h, t, 2 * t - 4, INNER_ROWS, EDGE_SLOTS))
        att_in, ck_turned, ck_ready, tab_in, tab_ready = (sem("att_in"), sem("ck_turned"), sem("ck_ready"), [sem("tab_in0"), sem("tab_in1")], sem("tab_ready"))
        s_mm, s_read, negmax, probs, p_turned, p_cp_act, p_cp_dve, pv_mm, att_out = (sem(n) for n in (
            "score_mm", "score_read", "negmax", "probs", "probs_turned", "pt_copied_act", "pt_copied_dve", "pv_mm", "att_out"))
        dve_att = sem("dve_att")
        with nc.Block() as block:
            @block.sync
            def _(sp):
                sp.dma_start(ck, cache_k).then_inc(att_in, 16)
                sp.dma_start(cv, cache_v).then_inc(att_in, 16)
                sp.dma_start(winmask, k_winmask).then_inc(att_in, 16)
                sp.dma_start(out_v, va[:, CTX_TILE, :]).then_inc(out_stored, 16)
                stored[0] += 16
                for h in range(HEADS):
                    if h >= 2:
                        sp.wait_ge(s_read, NT * (h - 1))
                    for half in range(2):
                        for s0, n, dr in ((0, EDGE_SLOTS, 1 - half), (EDGE_SLOTS, INNER_ROWS, 3 - half)):
                            src = bass.AP(rpb_rows.tensor, (h * RPB_R + dr) * GRID_W * PADW + GRID_W - 1,
                                          [[PADW - 1, GRID_W], [GRID_W * PADW, n], [1, GRID_W]])
                            sp.dma_start(tab[h % 2][GRID_W * half:GRID_W * (half + 1), s0:s0 + n, :],
                                         src).then_inc(tab_in[h % 2], 16)
                    if h == 1:
                        sp.wait_ge(ck_ready, 2)
                        sp.dma_start(out_k, kc_nat).then_inc(out_stored, 16)
                        stored[0] += 16

            @block.gpsimd
            def _(pool):
                pool.wait_ge(att_in, 48)
                for h in range(HEADS):
                    pool.wait_ge(tab_in[h % 2], 64 * (h // 2 + 1))
                    nc.gpsimd.tensor_tensor(tab[h % 2], tab[h % 2], winmask, ALU.add).then_inc(tab_ready, 1)

            def keys(n):
                return n[3] * GRID_W

            def dve_copies(n):
                return n - n // NT

            @block.tensor
            def _(pe):
                pe.wait_ge(att_in, 48)
                for j in range(3):
                    last = nc.tensor.transpose(bank(0)[:, j * P:(j + 1) * P], ck[:, j * P:(j + 1) * P], ident)
                for j in range(3):
                    last = nc.tensor.transpose(bank(2)[:, j * P:(j + 1) * P], kaT[:, j, LAT:TOK], ident)
                last.then_inc(ck_turned, 1)
                pe.wait_ge(ck_ready, 2)

                def score(i):
                    h, t, r0, _, _ = att[i]
                    if i >= 2:
                        pe.wait_ge(s_read, i - 1)
                    q = qaT[:, h, t * P:(t + 1) * P]
                    base = 2 * (i % 2)
                    if r0 is None:
                        nc.tensor.matmul(bank(base)[:, 0:P], q, kaT[:, h // 2, LAT:TOK], start=True, stop=True).then_inc(s_mm, 1)
                        return
                    n = keys(att[i])
                    nc.tensor.matmul(bank(base), q, kaT[:, h // 2, r0 * GRID_W:r0 * GRID_W + BANK], start=True, stop=True)
                    if n > BANK:
                        nc.tensor.matmul(bank(base + 1)[:, 0:P], q, kaT[:, h // 2, r0 * GRID_W + BANK:r0 * GRID_W + n], start=True, stop=True)
                    nc.tensor.matmul(bank(base + 1)[:, n - BANK:n - BANK + P], q, ckT[:, h // 2, :], start=True, stop=True).then_inc(s_mm, 1)

                def turn(i):
                    pe.wait_ge(probs, i + 1)
                    if i >= 1:
                        pe.wait_ge(p_cp_act, i)
                        if dve_copies(i):
                            pe.wait_ge(p_cp_dve, dve_copies(i))
                    for j in range(keys(att[i]) // P + 1):
                        last = nc.tensor.transpose(ps[:, 4 * BANK + j * P:4 * BANK + (j + 1) * P],
                                                   pr[i % 2][:, j * P:(j + 1) * P], ident)
                    last.then_inc(p_turned, 1)

                def weigh(i):
                    h, t, r0, _, _ = att[i]
                    pe.wait_ge(p_cp_act, i + 1)
                    pe.wait_ge(p_cp_dve, dve_copies(i + 1))
                    if i >= 2:
                        pe.wait_ge(att_out, i - 1)
                    out = bank(6 + i % 2)[:, 0:HD]
                    cols = slice(h * HD, (h + 1) * HD)
                    n = keys(att[i]) // P
                    for j in range(n):
                        nc.tensor.matmul(out, pt[i % 2][:, j, :], va[:, r0 // 2 + j, cols], start=(j == 0), stop=False)
                    v = va[:, CTX_TILE, cols] if r0 is None else cv[:, cols]
                    nc.tensor.matmul(out, pt[i % 2][:, n, :], v, start=(n == 0), stop=True).then_inc(pv_mm, 1)

                score(0)
                for i in range(len(att)):
                    if i + 1 < len(att):
                        score(i + 1)
                    if i:
                        weigh(i - 1)
                    turn(i)
                weigh(len(att) - 1)

            @block.scalar
            def _(act):
                for i, u in enumerate(att):
                    n = keys(u)
                    act.wait_ge(negmax, i + 1)
                    if i >= 2:
                        act.wait_ge(p_turned, i - 1)
                    nc.scalar.activation(pr[i % 2][:, 0:n + P], sc[i % 2][:, 0:n + P], ACT.Exp, bias=stat[:, i, 1:2],
                                         accum_out=stat[:, i, 2:3]).then_inc(probs, 1)
                    act.wait_ge(p_turned, i + 1)
                    if i >= 2:
                        act.wait_ge(pv_mm, i - 1)
                    c = min(n // P + 1, 4)
                    nc.scalar.activation(pt[i % 2][:, 0:c, :], bank(4)[:, 0:c * P].rearrange("p (j t) -> p j t", j=c), ACT.Copy).then_inc(p_cp_act, 1)

            @block.vector
            def _(dve):
                st = Steps(dve, dve_att)
                dve.wait_ge(ck_turned, 1)
                nc.vector.tensor_copy(ckT, bank(0)[:, 0:3 * P].rearrange("p (j t) -> p j t", j=3)).then_inc(ck_ready, 1)
                nc.vector.tensor_copy(kc_nat, bank(2)[:, 0:3 * P]).then_inc(ck_ready, 1)

                def bias_and_max(i):
                    h, t, r0, nrows, slot = att[i]
                    n = keys(att[i])
                    if i % NT == 0:
                        dve.wait_ge(tab_ready, h + 1)
                    dve.wait_ge(s_mm, i + 1)
                    if i >= 2:
                        dve.wait_ge(probs, i - 1)
                    base = 2 * (i % 2) * BANK
                    m = stat[:, i, 0:1]
                    if n:
                        ins = nc.vector.tensor_tensor_reduce(
                            out=sc[i % 2][:, 0:n], in0=ps[:, base:base + n],
                            in1=tab[h % 2][:, slot:slot + nrows, :].rearrange("p s k -> p (s k)"), scale=1.0, scalar=-3e38,
                            op0=ALU.add, op1=ALU.max, accum_out=stat[:, i, 3:4])
                        st.link(ins)
                        nc.vector.tensor_scalar(sc[i % 2][:, n:n + P], ps[:, base + n:base + n + P], 0.0, stat[:, i, 3:4],
                                                ALU.add, ALU.max, accum_out=m).then_inc(s_read, 1)
                    else:
                        nc.vector.tensor_scalar(sc[i % 2][:, 0:P], ps[:, base:base + P], 0.0, None,
                                                ALU.add, ALU.max, accum_out=m).then_inc(s_read, 1)
                    dve.wait_ge(s_read, i + 1)
                    nc.vector.tensor_scalar(stat[:, i, 1:2], m, -1.0, None, ALU.mult).then_inc(negmax, 1)

                def copy_turned(i):
                    n = keys(att[i]) // P + 1
                    dve.wait_ge(p_turned, i + 1)
                    if i >= 2:
                        dve.wait_ge(pv_mm, i - 1)
                    if n > 4:
                        nc.vector.tensor_copy(pt[i % 2][:, 4:n, :], bank(5)[:, 0:(n - 4) * P].rearrange("p (j t) -> p j t", j=n - 4)).then_inc(p_cp_dve, 1)

                def normalise(i):
                    h, t = att[i][0:2]
                    dve.wait_ge(probs, i + 1)
                    st.link(nc.vector.reciprocal(stat[:, i, 3:4], stat[:, i, 2:3]))
                    dve.wait_ge(pv_mm, i + 1)
                    nc.vector.tensor_scalar(mix[:, t, h * HD:(h + 1) * HD], bank(6 + i % 2)[:, 0:HD], stat[:, i, 3:4], None, ALU.mult).then_inc(att_out, 1)

                bias_and_max(0)
                for i in range(len(att)):
                    if i + 1 < len(att):
                        bias_and_max(i + 1)
                    if i:
                        normalise(i - 1)
                    copy_turned(i)
                normalise(len(att) - 1)

        ar.at = after_mlstm_in
        cols = ar.take([NT, 4, 64])
        decay = ar.take([8, NT])
        selm = ar.take([8, P])
        r1 = ar.take([TOK])
        keep = ar.at
        giT, gfT, bT, mT, reset, w1, w2 = (ar.take([TOK]) for _ in range(7))
        m0, min_, r1e, ewe = ar.take([1]), ar.take([NT]), ar.take([NT]), ar.take([NT])
        g_in, g_turned, g_copied, f_abs, f_exp, a_rdy, e_rdy, ew_turned, dec_mm, ml_gates = (sem(n) for n in (
            "gate_in", "gate_turned", "gate_copied", "f_abs", "f_softplus", "exps_in", "exps_ready", "cols_turned", "decay_mm", "dve_gates"))
        act_g = sem("act_gates")
        FW, BW = slice(0, 32), slice(32, 64)
        with nc.Block() as block:
            @block.sync
            def _(sp):
                sp.dma_start(selm[0:64], k_sel).then_inc(g_in, 16)
                sp.dma_start(reset[0:64], k_reset).then_inc(g_in, 16)
                sp.wait_ge(ml_gates, 1)
                for way in range(2):
                    sp.dma_start(m0[32 * way:32 * way + MH], state_m[way, :, None]).then_inc(g_in, 16)
                sp.wait_ge(ml_gates, 8)
                sp.dma_start(out_m[0, :, None], mT[0:MH, TOK - 1:TOK]).then_inc(out_stored, 16)
                sp.dma_start(out_m[1, :, None], mT[32:32 + MH, LAT:LAT + 1]).then_inc(out_stored, 16)
                stored[0] += 32
                sp.wait_ge(out_stored, stored[0])

            @block.tensor
            def _(pe):
                for t in range(NT):
                    nc.tensor.transpose(ps[0:64, t * P:(t + 1) * P], gi[:, t, :], ident)
                    last = nc.tensor.transpose(ps[0:64, 4 * BANK + t * P:4 * BANK + (t + 1) * P], gf[:, t, :], ident)
                last.then_inc(g_turned, 1)
                pe.wait_ge(e_rdy, 3)
                pe.wait_ge(a_rdy, 2)
                pe.wait_ge(g_in, 64)
                for t in range(NT):
                    for n, src in enumerate((giT, w1, gfT, w2)):
                        last = nc.tensor.transpose(ps[:, (4 * t + n) * 64:(4 * t + n + 1) * 64], src[0:64, t * P:(t + 1) * P], ident[0:64, 0:64])
                last.then_inc(ew_turned, 1)
                for r in range(8):
                    last = nc.tensor.matmul(bank(6)[:, r * NT:(r + 1) * NT], selm[0:64, r, :], ewe[0:64], start=True, stop=True)
                last.then_inc(dec_mm, 1)

            @block.scalar
            def _(act):
                st = Steps(act, act_g)
                act.wait_ge(f_abs, 1)
                st.link(nc.scalar.activation(w1[0:64], w1[0:64], ACT.Exp, scale=-1.0))
                nc.scalar.activation(w1[0:64], w1[0:64], ACT.Ln, bias=1.0).then_inc(f_exp, 1)
                act.wait_ge(a_rdy, 1)
                nc.scalar.activation(w1[0:64], w1[0:64], ACT.Exp).then_inc(e_rdy, 1)
                nc.scalar.activation(w2[0:64], w2[0:64], ACT.Exp).then_inc(e_rdy, 1)
                nc.scalar.activation(gfT[0:64], mT[0:64], ACT.Exp, scale=-1.0).then_inc(e_rdy, 1)

            @block.vector
            def _(dve):
                st = Steps(dve, ml_gates)
                st.add(nc.vector.memset(m0[0:64], 0.0))
                dve.wait_ge(g_turned, 1)
                nc.vector.tensor_copy(giT[0:64], ps[0:64, 0:TOK]).then_inc(g_copied, 1)
                nc.vector.tensor_copy(gfT[0:64], ps[0:64, 4 * BANK:4 * BANK + TOK]).then_inc(g_copied, 1)
                dve.wait_ge(g_copied, 2)
                nc.vector.scalar_tensor_tensor(out=w1[0:64], in0=gfT[0:64], scalar=-1.0, in1=gfT[0:64], op0=ALU.mult, op1=ALU.max).then_inc(f_abs, 1)
                dve.wait_ge(f_exp, 1)
                st.link(nc.vector.scalar_tensor_tensor(out=gfT[0:64], in0=gfT[0:64], scalar=0.0, in1=w1[0:64], op0=ALU.min, op1=ALU.subtract))
                dve.wait_ge(g_in, 64)
                st.add(nc.vector.tensor_tensor_scan(bT[FW], reset[FW], gfT[FW], 0.0, ALU.mult, ALU.add))
                st.add(nc.vector.tensor_tensor_scan(bT[BW][:, ::-1], reset[BW][:, ::-1], gfT[BW][:, ::-1], 0.0, ALU.mult, ALU.add))
                for seg, init in ((slice(0, LAT), True), (slice(LAT, TOK), False)):
                    for rows, way in ((FW, 0), (BW, 1)):
                        o, a, b = (x[rows, seg] for x in (mT, gfT, giT))
                        if way:
                            o, a, b = (x[:, ::-1] for x in (o, a, b))
                        st.add(nc.vector.tensor_tensor_scan(o, a, b, m0[rows, 0:1] if init else 0.0, ALU.add, ALU.max))
                st.settle()
                st.add(nc.vector.tensor_tensor(r1[0:64], bT[0:64], mT[0:64], ALU.subtract))
                st.add(nc.vector.memset(min_[0:64], 0.0))
                st.link(nc.vector.tensor_tensor(giT[0:64], giT[0:64], bT[0:64], ALU.subtract))
                v3 = lambda x, rows: x[rows].rearrange("p (c t) -> p c t", c=NT)
                st.add(nc.vector.tensor_copy(min_[FW, 0:1], m0[FW]))
                st.add(nc.vector.tensor_copy(min_[FW, 1:8], v3(mT, FW)[:, 0:7, P - 1]))
                st.add(nc.vector.tensor_copy(min_[BW, 7:8], m0[BW]))
                st.add(nc.vector.tensor_copy(min_[BW, 0:7], v3(mT, BW)[:, 1:8, 0]))
                st.add(nc.vector.tensor_copy(r1e[FW], v3(r1, FW)[:, :, P - 1]))
                st.link(nc.vector.tensor_copy(r1e[BW], v3(r1, BW)[:, :, 0]))
                A = slice(0, 64)
                st.add(nc.vector.tensor_tensor(v3(w1, A), v3(r1, A), bc(min_[A, :, None], (64, NT, P)), ALU.add))
                st.settle()
                nc.vector.tensor_tensor(v3(w2, A), v3(giT, A), bc(r1e[A, :, None], (64, NT, P)), ALU.add).then_inc(a_rdy, 1)
                dve.wait_ge(e_rdy, 3)
                st.add(nc.vector.tensor_copy(ewe[FW], v3(w1, FW)[:, :, P - 1]))
                st.settle()
                nc.vector.tensor_copy(ewe[BW], v3(w1, BW)[:, :, 0]).then_inc(a_rdy, 1)
                dve.wait_ge(ew_turned, 1)
                st.add(nc.vector.tensor_copy(cols, ps[:, 0:NT * 256].rearrange("p (t n r) -> p t n r", t=NT, n=4)))
                dve.wait_ge(dec_mm, 1)
                st.add(nc.vector.tensor_copy(decay, bank(6)[:, 0:8 * NT].rearrange("p (r t) -> p r t", r=8)))
        ar.at = keep

        sw = ar.take([8, NT, P])
        knat = ar.take([NT, MW])
        keep_s = ar.at
        scanmask = ar.take([2, P])
        am = [ar.take([NT, P]) for _ in range(2)]
        ew = [ar.take([NT, P]) for _ in range(2)]
        sm_in, am_rdy, bc_mm, ew_add, ew_exp, sw_rdy, kn_turned, kn_cp = (sem(n) for n in (
            "scanmask_in", "a_masked", "weights_mm", "weights_added", "weights_exp", "sw_ready", "k_turned", "k_copied"))

        def a_col(t, way, h0=0, n=1):
            return cols[:, t, 0, 32 * way + h0:32 * way + h0 + n]

        with nc.Block() as block:
            @block.sync
            def _(sp):
                sp.dma_start(scanmask, k_scanmask).then_inc(sm_in, 16)

            @block.gpsimd
            def _(pool):
                pool.wait_ge(sm_in, 16)
                for r in range(8):
                    way, h = divmod(r, 4)
                    if r >= 2:
                        pool.wait_ge(ew_add, r - 1)
                    nc.gpsimd.tensor_tensor(am[r % 2], bc(scanmask[:, way:way + 1, :], (P, NT, P)),
                                            bc(cols[:, :, 0, 32 * way + h:32 * way + h + 1], (P, NT, P)), ALU.add).then_inc(am_rdy, 1)

            @block.tensor
            def _(pe):
                for r in range(8):
                    h = r % 4
                    if r >= 1:
                        pe.wait_ge(ew_add, r)
                    for t0, n in ((0, 512), (512, 512), (1024, 128)):
                        nc.tensor.matmul(ps[:, t0:t0 + n], selm[0:64, r, :], r1[0:64, t0:t0 + n], start=True, stop=True)
                    if r >= 1:
                        pe.wait_ge(sw_rdy, r)
                    for t in range(NT):
                        last = nc.tensor.matmul(ps[:, 3 * BANK + t * P:3 * BANK + (t + 1) * P], kbT[0:MD, h, t * P:(t + 1) * P],
                                                qbT[0:MD, h, t * P:(t + 1) * P], start=True, stop=True)
                    last.then_inc(bc_mm, 1)
                    for t in ([r, 8] if r == 7 else [r]):
                        if t >= 2:
                            pe.wait_ge(kn_cp, t - 1)
                        for hh in range(MH):
                            last = nc.tensor.transpose(bank(6 + t % 2)[:, hh * MD:(hh + 1) * MD], kbT[0:MD, hh, t * P:(t + 1) * P], ident[0:MD, 0:MD])
                        last.then_inc(kn_turned, 1)

            @block.scalar
            def _(act):
                for r in range(8):
                    act.wait_ge(ew_add, r + 1)
                    nc.scalar.activation(ew[r % 2], ew[r % 2], ACT.Exp).then_inc(ew_exp, 1)
                    for t in ([r, 8] if r == 7 else [r]):
                        act.wait_ge(kn_turned, t + 1)
                        nc.scalar.activation(knat[:, t, :], bank(6 + t % 2)[:, 0:MW], ACT.Copy).then_inc(kn_cp, 1)

            @block.vector
            def _(dve):
                for r in range(8):
                    dve.wait_ge(bc_mm, r + 1)
                    dve.wait_ge(am_rdy, r + 1)
                    if r >= 2:
                        dve.wait_ge(sw_rdy, r - 1)
                    nc.vector.tensor_tensor(ew[r % 2], ps[:, 0:TOK].rearrange("p (c t) -> p c t", c=NT), am[r % 2], ALU.add).then_inc(ew_add, 1)
                    dve.wait_ge(ew_exp, r + 1)
                    nc.vector.tensor_tensor(sw[:, r], ew[r % 2], ps[:, 3 * BANK:3 * BANK + TOK].rearrange("p (c t) -> p c t", c=NT), ALU.mult).then_inc(sw_rdy, 1)
        ar.at = keep_s

        cs = ar.take([8, MA])
        cctx = ar.take([8, MA])
        hn = [ar.take([MH, MA]) for _ in range(2)]
        ct = ar.take([MH, MA])
        dn = ar.take([MH])
        KW_RING = 4
        kw = [ar.take([MW]) for _ in range(KW_RING)]
        sq = sw[:, 0:3].rearrange("p r c t -> p (r c t)").rearrange("p (n d) -> p n d", d=MD)
        ssb, lnb, ysb, tb = (ar.take([NT * MH]) for _ in range(4))
        mln = ar.take([MW])
        c_in, sc_mm, sc_used, c_new, hb_mean, hb_guess, hb_sq, c_ctx_rdy, kw_rdy = (sem(n) for n in (
            "state_in", "scan_mm", "scan_used", "state_new", "hb_mean", "hb_guess", "hb_squares", "ctx_state_ready", "keys_weighted"))
        dve_scan, act_scan = sem("dve_scan"), sem("act_scan")
        order = [(CTX_TILE, 0), (CTX_TILE, 1)]
        for c in range(8):
            order += [(c, 0), (7 - c, 1)]
        hb = mix[:, :, AW:AW + MW]
        with nc.Block() as block:
            @block.sync
            def _(sp):
                for way in range(2):
                    sp.dma_start(cs[0:MD, MH * way:MH * way + MH, 0:MD], state_C[way].rearrange("h d e -> d h e")).then_inc(c_in, 16)
                    sp.dma_start(cs[0:MD, MH * way:MH * way + MH, MD], state_n[way].rearrange("h d -> d h")).then_inc(c_in, 16)
                sp.dma_start(mln, bass.AP(ml_norm.tensor, 0, [[0, P], [1, MW]])).then_inc(c_in, 16)
                sp.wait_ge(c_ctx_rdy, 2)
                for way in range(2):
                    sp.dma_start(out_C[way].rearrange("h d e -> d h e"), cctx[0:MD, MH * way:MH * way + MH, 0:MD]).then_inc(out_stored, 16)
                    sp.dma_start(out_n[way].rearrange("h d -> d h"), cctx[0:MD, MH * way:MH * way + MH, MD]).then_inc(out_stored, 16)
                stored[0] += 64
                sp.wait_ge(out_stored, stored[0])

            @block.gpsimd
            def _(pool):
                for i, (t, way) in enumerate(order):
                    if i >= KW_RING:
                        pool.wait_ge(sc_mm, i - KW_RING + 1)
                    nc.gpsimd.tensor_tensor(kw[i % KW_RING].rearrange("p (h d) -> p h d", h=MH),
                                            knat[:, t, :].rearrange("p (h d) -> p h d", h=MH),
                                            bc(cols[:, t, 3, 32 * way:32 * way + MH][:, :, None], (P, MH, MD)), ALU.mult).then_inc(kw_rdy, 1)

            @block.tensor
            def _(pe):
                pe.wait_ge(c_in, 80)
                for i, (t, way) in enumerate(order):
                    pe.wait_ge(kw_rdy, i + 1)
                    b = 3 * (i % 2)
                    if i >= 2:
                        pe.wait_ge(sc_used, i - 1)
                    for h in range(MH):
                        nc.tensor.matmul(bank(b)[:, h * MA:(h + 1) * MA], sw[:, MH * way + h, t, :], vb[:, t, h, :], start=True, stop=True)
                    for h in range(MH):
                        last = nc.tensor.matmul(bank(b + 2)[0:MD, h * MA:(h + 1) * MA], kw[i % KW_RING][:, h * MD:(h + 1) * MD], vb[:, t, h, :], start=True, stop=True)
                    if t != CTX_TILE:
                        for h in range(MH):
                            last = nc.tensor.matmul(bank(b + 1)[:, h * MA:(h + 1) * MA], qbT[0:MD, h, t * P:(t + 1) * P], cs[0:MD, MH * way + h, :], start=True, stop=True)
                    last.then_inc(sc_mm, 1)

            @block.scalar
            def _(act):
                st = Steps(act, act_scan)
                act.wait_ge(hb_mean, 1)
                st.link(nc.scalar.activation(lnb, ssb, ACT.Ln))
                nc.scalar.activation(ysb, lnb, ACT.Exp, scale=-0.5).then_inc(hb_guess, 1)

            @block.vector
            def _(dve):
                st = Steps(dve, dve_scan)
                dve.wait_ge(c_in, 80)
                p4 = lambda n, rows=P: bank(n)[0:rows, 0:MH * MA].rearrange("p (h e) -> p h e", h=MH)
                for i, (t, way) in enumerate(order):
                    b = 3 * (i % 2)
                    hs = slice(MH * way, MH * way + MH)
                    dve.wait_ge(sc_mm, i + 1)
                    num = hn[i % 2]
                    w = lambda n: cols[:, t, n, 32 * way:32 * way + MH]
                    if t == CTX_TILE:
                        nc.vector.tensor_copy(cctx[0:MD, hs, :], p4(b + 2, MD)).then_inc(c_ctx_rdy, 1)
                        st.link(nc.vector.tensor_copy(num, p4(b)))
                    else:
                        st.link(nc.vector.tensor_tensor(ct[0:MD], cs[0:MD, hs, :], bc(decay[0:MD, hs, t:t + 1], (MD, MH, MA)), ALU.mult))
                        st.add(nc.vector.tensor_tensor(cs[0:MD, hs, :], ct[0:MD], p4(b + 2, MD), ALU.add))
                        st.link(nc.vector.tensor_tensor(num, p4(b + 1), bc(w(1)[:, :, None], (P, MH, MA)), ALU.mult))
                        st.link(nc.vector.tensor_tensor(num, num, p4(b), ALU.add))
                    st.link(nc.vector.scalar_tensor_tensor(out=dn[:, :, None], in0=num[:, :, MD:MA], scalar=-1.0, in1=num[:, :, MD:MA], op0=ALU.mult, op1=ALU.max))
                    st.link(nc.vector.tensor_tensor(dn, dn, w(2), ALU.max))
                    st.link(nc.vector.reciprocal(dn, dn))
                    dst = hb[:, t, :].rearrange("p (h d) -> p h d", h=MH)
                    first = (way == 0 and t <= 3) or (way == 1 and 4 <= t < 8) or (way == 0 and t == CTX_TILE)
                    if first:
                        nc.vector.tensor_tensor(dst, num[:, :, 0:MD], bc(dn[:, :, None], (P, MH, MD)), ALU.mult).then_inc(sc_used, 1)
                    else:
                        st.link(nc.vector.tensor_tensor(num[:, :, 0:MD], num[:, :, 0:MD], bc(dn[:, :, None], (P, MH, MD)), ALU.mult))
                        nc.vector.tensor_tensor(dst, dst, num[:, :, 0:MD], ALU.add).then_inc(sc_used, 1)
                dve.wait_ge(sc_used, len(order))
                for t in range(NT):
                    h4 = hb[:, t, :].rearrange("p (h d) -> p h d", h=MH)
                    st.add(nc.vector.tensor_tensor(sq[:, MH * t:MH * t + MH, :], h4, h4, ALU.mult))
                st.settle()
                st.link(nc.vector.tensor_reduce(ssb, sq, AX.X, ALU.add))
                nc.vector.tensor_scalar(ssb, ssb, 1.0 / MD, EPS, ALU.mult, ALU.add).then_inc(hb_mean, 1)
                dve.wait_ge(hb_guess, 1)
                st.link(nc.vector.tensor_tensor(tb, ysb, ysb, ALU.mult))
                st.link(nc.vector.scalar_tensor_tensor(out=tb, in0=tb, scalar=-0.5, in1=ssb, op0=ALU.mult, op1=ALU.mult))
                st.link(nc.vector.scalar_tensor_tensor(out=ysb, in0=tb, scalar=1.5, in1=ysb, op0=ALU.add, op1=ALU.mult))
                for t in range(NT):
                    h4 = hb[:, t, :].rearrange("p (h d) -> p h d", h=MH)
                    st.add(nc.vector.tensor_tensor(og[:, t, :], og[:, t, :], mln, ALU.mult))
                    st.link(nc.vector.tensor_tensor(h4, h4, bc(ysb[:, MH * t:MH * t + MH][:, :, None], (P, MH, MD)), ALU.mult))
                    st.link(nc.vector.tensor_tensor(hb[:, t, :], hb[:, t, :], og[:, t, :], ALU.mult))
        ar.at = mark_h

        x1 = ar.take([NT, D])
        h2 = ar.take([NT, D])
        after_x1 = ar.at
        wo = ar.take([KD, D])
        g1 = ar.take([2, D])
        mt = [ar.take([KD, P]) for _ in range(2)]
        o_in, ox_in, o_turned, o_cp, o_mm, o_add = (sem(n) for n in ("g1_in", "ox_in", "mix_turned", "mix_copied", "out_mm", "out_add"))
        wo_in = [sem("wo_in0"), sem("wo_in1")]
        dve_o, act_o = sem("dve_out"), sem("act_out")
        sq_junk = ar.take([D])
        sq2, mean2, guess2 = sem("n2_squares"), sem("n2_mean"), sem("n2_guess")
        with nc.Block() as block:
            @block.sync
            def _(sp):
                for half in range(2):
                    hs = slice(half * BANK, (half + 1) * BANK)
                    sp.dma_start(wo[:, :, hs], w_out.rearrange("(k p) n -> p k n", p=P)[:, :, hs]).then_inc(wo_in[half], 16)
                sp.dma_start(g1, mod_row(2)).then_inc(o_in, 16)
                sp.wait_ge(wo_in[1], 16)
                for t in range(NT):
                    sp.dma_start(x1[:, t, :], x_all[t * P:(t + 1) * P, :]).then_inc(ox_in, 16)

            @block.tensor
            def _(pe):
                def turn(t):
                    if t >= 2:
                        pe.wait_ge(o_cp, t - 1)
                    for k in range(KD):
                        at = 2 * (t % 2) * BANK + k * P
                        last = nc.tensor.transpose(ps[:, at:at + P], mix[:, t, k * P:(k + 1) * P], ident)
                    last.then_inc(o_turned, 1)

                turn(0)
                for t in range(NT):
                    if t + 1 < NT:
                        turn(t + 1)
                    pe.wait_ge(o_cp, t + 1)
                    if t >= 2:
                        pe.wait_ge(o_add, 2 * (t - 1))
                    for half in range(2):
                        if t == 0:
                            pe.wait_ge(wo_in[half], 16)
                        for k in range(KD):
                            last = nc.tensor.matmul(bank(4 + 2 * (t % 2) + half), mt[t % 2][:, k, :], wo[:, k, half * BANK:(half + 1) * BANK],
                                                    start=(k == 0), stop=(k == KD - 1))
                    last.then_inc(o_mm, 1)

            @block.scalar
            def _(act):
                st = Steps(act, act_o)

                def square(t):
                    act.wait_ge(o_add, 2 * (t + 1))
                    if t:
                        st.settle()
                    st.add(nc.scalar.activation(sq_junk, x1[:, t, :], ACT.Square, accum_out=ss2[:, t:t + 1]))

                for t in range(NT):
                    act.wait_ge(o_turned, t + 1)
                    if t >= 2:
                        act.wait_ge(o_mm, t - 1)
                    for half in range(2):
                        ins = nc.scalar.activation(mt[t % 2][:, 4 * half:4 * half + 4, :], bank(2 * (t % 2) + half).rearrange("p (k t) -> p k t", k=4), ACT.Copy)
                    ins.then_inc(o_cp, 1)
                    if t:
                        square(t - 1)
                square(NT - 1)
                st.settle()
                nc.scalar.activation(sq_junk[:, 0:1], ss2[:, 0:1], ACT.Square).then_inc(sq2, 1)
                act.wait_ge(mean2, 1)
                st.link(nc.scalar.activation(ln2, ss2, ACT.Ln))
                nc.scalar.activation(y2, ln2, ACT.Exp, scale=-0.5).then_inc(guess2, 1)

            @block.vector
            def _(dve):
                st = Steps(dve, dve_o)
                dve.wait_ge(o_in, 16)
                dve.wait_ge(ox_in, 16 * NT)
                for t in range(NT):
                    dve.wait_ge(o_mm, t + 1)
                    for half in range(2):
                        hs = slice(half * BANK, (half + 1) * BANK)
                        st.link(nc.vector.tensor_tensor(h2[:, t, hs], bank(4 + 2 * (t % 2) + half), g1[:, side(t), hs], ALU.mult))
                        nc.vector.tensor_tensor(x1[:, t, hs], x1[:, t, hs], h2[:, t, hs], ALU.add).then_inc(o_add, 1)
                dve.wait_ge(sq2, 1)
                nc.vector.tensor_scalar(ss2, ss2, 1.0 / D, EPS, ALU.mult, ALU.add).then_inc(mean2, 1)
                dve.wait_ge(guess2, 1)
                newton(st, y2, t2, ss2)
        ar.at = after_x1
        assert after_x1 + 4096 < 40704

        h2T = mix.rearrange("p t d -> p (t d)").rearrange("p (k t) -> p k t", k=KD)
        wr = ar.take([KD, NE])
        router_mark = ar.at
        wr_in, r_mm, moe_w = sem("router_weights_in"), sem("router_mm"), ar.columns - 2 * 3 * KD * DF
        assert moe_w + 3 * KD * DF >= ar.at + 4 * D
        half_cols = 3 * KD * DF
        halves = sb[:, moe_w:moe_w + 2 * half_cols].rearrange("p (s n) -> p s n", s=2)
        w_even, w_odd = halves[:, 1, :], halves[:, 0, :]
        gu_ld, d_ld = [sem(f"gate_up_in{s}") for s in range(2)], [sem(f"down_in{s}") for s in range(2)]

        def load_gate_up(sp, dst, e, s):
            for n, w in enumerate((w_gate, w_up)):
                sp.dma_start(dst[:, n * KD * DF:(n + 1) * KD * DF].rearrange("p (k f) -> p k f", k=KD),
                             w[e].rearrange("(k p) n -> p k n", p=P)).then_inc(gu_ld[s], 16)

        def load_down(sp, dst, e, s):
            for n in range(2):
                sp.dma_start(dst[:, (2 * KD + n * KD // 2) * DF:(2 * KD + (n + 1) * KD // 2) * DF].rearrange("p (k f) -> p k f", k=KF // 2),
                             w_down[e].rearrange("(k p) n -> p k n", p=P)[:, n * KF // 2:(n + 1) * KF // 2]).then_inc(d_ld[s], 16)

        def router_sp(sp):
            sp.dma_start(wr, w_router.rearrange("(k p) n -> p k n", p=P)).then_inc(wr_in, 16)
            load_gate_up(sp, w_even, 0, 0)
            load_down(sp, w_even, 0, 0)
            sp.dma_start(w_odd[:, half_cols - 8:half_cols - 4], k_ident[:, 0:4]).then_inc(gu_ld[1], 16)
            sp.dma_start(w_odd[:, half_cols - 4:half_cols], k_ident[:, 0:4]).then_inc(d_ld[1], 16)

        def router_pe(pe, t, copied):
            if t == 0:
                pe.wait_ge(wr_in, 16)
            for u in ([t - 1] if t else []) + ([t] if t == NT - 1 else []):
                pe.wait_ge(copied, u + 1)
                for k in range(KD):
                    last = nc.tensor.matmul(bank(2)[:, u * NE:(u + 1) * NE], h2T[:, k, u * P:(u + 1) * P], wr[:, k, :],
                                            start=(k == 0), stop=(k == KD - 1))
            if t == NT - 1:
                last.then_inc(r_mm, 1)

        norm_stage("n2_", x1, y2, (3, 4), h2, h2T, router_sp, router_pe)
        ar.at = router_mark

        upper, ones = ar.take([P]), ar.take([P])
        brr, tids = ar.take([NE]), ar.take([N_SLOT_TILES])
        NEt = NT * NE
        lg, sco, sel, cmpb = ar.take([NEt]), ar.take([NEt]), ar.take([NEt]), ar.take([NEt * EPG])
        rank, oh1, oh2, tmp, both, sl = (ar.take([NEt]) for _ in range(6))
        gs, gr = ar.take([NT * EG]), ar.take([NT * EG])
        gcmp = ar.take([NT * EG * EG])
        base_ = ar.take([NT, NE])
        tot = ar.take([NT, NE])
        cnt, ntl, cum, off = (ar.take([NE]) for _ in range(4))
        s12, rden = ar.take([3, NT]), ar.take([NT])
        tcmp = ar.take([N_SLOT_TILES, NE])
        tef = ar.take([N_SLOT_TILES])
        assert ar.at <= moe_w + half_cols
        r_in, r_exp, both_rdy, pos_mm, slot_rdy, scattered, dve_r = (sem(n) for n in (
            "router_in", "router_exp", "picked", "position_mm", "slot_ready", "scattered", "dve_router"))
        with nc.Block() as block:
            @block.sync
            def _(sp):
                sp.dma_start(upper, k_upper).then_inc(r_in, 16)
                sp.dma_start(brr, bass.AP(b_router.tensor, 0, [[0, P], [1, NE]])).then_inc(r_in, 16)
                sp.dma_start(tids, bass.AP(k_tile_ids.tensor, 0, [[0, P], [1, N_SLOT_TILES]])).then_inc(r_in, 16)

            @block.tensor
            def _(pe):
                pe.wait_ge(r_in, 48)
                pe.wait_ge(both_rdy, 1)
                nc.tensor.matmul(bank(1)[:, 0:NEt], upper, both, start=True, stop=True)
                nc.tensor.matmul(bank(3)[:, 0:NEt], ones, both, start=True, stop=True).then_inc(pos_mm, 1)

            @block.scalar
            def _(act):
                act.wait_ge(r_mm, 1)
                nc.scalar.activation(lg, bank(2)[:, 0:NEt], ACT.Exp, scale=-1.0).then_inc(r_exp, 1)

            @block.gpsimd
            def _(pool):
                pool.wait_ge(slot_rdy, 1)
                for t in range(NT):
                    for n in range(2):
                        pool.indirect_dma_start(slot_x, bass.IndirectOffsetOnAxis(slot[n].bitcast(U32)[:, t:t + 1], 0), h2[:, t, :], None).then_inc(scattered, 16)
                pool.wait_ge(scattered, 16 * 2 * NT)

            @block.vector
            def _(dve):
                st = Steps(dve, dve_r)
                v = nc.vector
                st.add(v.memset(ones, 1.0))
                st.add(v.memset(cmpb, 0.0))
                st.add(v.memset(gcmp, 0.0))
                st.add(v.memset(base_, 0.0))
                dve.wait_ge(r_in, 48)
                dve.wait_ge(r_exp, 1)
                st.link(v.tensor_scalar(lg, lg, 1.0, None, ALU.add))
                st.link(v.reciprocal(sco, lg))
                st.link(v.tensor_tensor(sel.rearrange("p (t e) -> p t e", t=NT), sco.rearrange("p (t e) -> p t e", t=NT),
                                        bc(brr[:, None, :], (P, NT, NE)), ALU.add))

                def ranks(src, cmp, out, n):
                    s4 = src.rearrange("p (n e) -> p n e", e=4)
                    c4 = cmp.rearrange("p (n e f) -> p n e f", e=4, f=4)
                    for f in range(4):
                        if f < 3:
                            st.add(v.tensor_tensor(c4[:, :, f + 1:4, f], bc(s4[:, :, f:f + 1], (P, n, 3 - f)), s4[:, :, f + 1:4], ALU.is_ge))
                        if f > 0:
                            st.add(v.tensor_tensor(c4[:, :, 0:f, f], bc(s4[:, :, f:f + 1], (P, n, f)), s4[:, :, 0:f], ALU.is_gt))
                    st.settle()
                    st.link(v.tensor_reduce(out.rearrange("p (n e) -> p n e", e=4), c4, AX.X, ALU.add))

                ranks(sel, cmpb, rank, NT * EG)
                st.add(v.tensor_scalar(oh1, rank, 0.0, None, ALU.is_equal))
                st.add(v.tensor_scalar(oh2, rank, 1.0, None, ALU.is_equal))
                st.link(v.scalar_tensor_tensor(out=tmp, in0=rank, scalar=2.0, in1=sel, op0=ALU.is_lt, op1=ALU.mult))
                st.link(v.tensor_reduce(gs, tmp.rearrange("p (n e) -> p n e", e=EPG), AX.X, ALU.add))
                ranks(gs, gcmp, gr, NT)
                st.link(v.tensor_scalar(gs, gr, 0.0, None, ALU.is_equal))
                g4 = bc(gs[:, :, None], (P, NT * EG, EPG))
                for oh in (oh1, oh2):
                    o4 = oh.rearrange("p (n e) -> p n e", e=EPG)
                    st.add(v.tensor_tensor(o4, o4, g4, ALU.mult))
                st.settle()
                v.tensor_tensor(both, oh1, oh2, ALU.add).then_inc(both_rdy, 1)
                for n, oh in enumerate((oh1, oh2)):
                    st.link(v.tensor_tensor(tmp, sco, oh, ALU.mult))
                    st.link(v.tensor_reduce(s12[:, n, :], tmp.rearrange("p (t e) -> p t e", t=NT), AX.X, ALU.add))
                st.link(v.tensor_tensor(rden, s12[:, 0, :], s12[:, 1, :], ALU.add))
                st.link(v.reciprocal(rden, rden))
                for n in range(2):
                    st.add(v.tensor_tensor(gate[n], s12[:, n, :], rden, ALU.mult))
                dve.wait_ge(pos_mm, 1)
                st.link(v.tensor_copy(tot, bank(3)[:, 0:NEt].rearrange("p (t e) -> p t e", t=NT)))
                for t in range(1, NT):
                    st.link(v.tensor_tensor(base_[:, t, :], base_[:, t - 1, :], tot[:, t - 1, :], ALU.add))
                st.link(v.tensor_tensor(cnt, base_[:, NT - 1, :], tot[:, NT - 1, :], ALU.add))
                st.link(v.tensor_scalar(ntl, cnt, 0.0, None, ALU.is_gt))
                for k in range(1, NT):
                    st.link(v.scalar_tensor_tensor(out=ntl, in0=cnt, scalar=float(P * k), in1=ntl, op0=ALU.is_gt, op1=ALU.add))
                st.link(v.tensor_tensor_scan(cum, ones[:, 0:NE], ntl, 0.0, ALU.mult, ALU.add))
                st.link(v.tensor_tensor(off, cum, ntl, ALU.subtract))
                st.link(v.tensor_scalar(off, off, float(P), None, ALU.mult))
                s3 = sl.rearrange("p (t e) -> p t e", t=NT)
                st.link(v.tensor_tensor(s3, base_, bc(off[:, None, :], (P, NT, NE)), ALU.add))
                st.link(v.tensor_tensor(sl, sl, bank(1)[:, 0:NEt], ALU.add))
                for n, oh in enumerate((oh1, oh2)):
                    st.link(v.tensor_tensor(tmp, sl, oh, ALU.mult))
                    st.link(v.tensor_reduce(s12[:, 2, :], tmp.rearrange("p (t e) -> p t e", t=NT), AX.X, ALU.add))
                    st.link(v.tensor_copy(slot[n].bitcast(U32), s12[:, 2, :]))
                st.link(v.tensor_tensor(tcmp, bc(cum[:, None, :], (P, N_SLOT_TILES, NE)), bc(tids[:, :, None], (P, N_SLOT_TILES, NE)), ALU.is_le))
                st.link(v.tensor_reduce(tef, tcmp, AX.X, ALU.add))
                st.link(v.tensor_scalar(tef, tef, float(NE - 1), None, ALU.min))
                st.add(v.tensor_copy(te[:, 0:N_SLOT_TILES].bitcast(I32), tef))
                st.add(v.tensor_copy(te[:, N_SLOT_TILES + 2:].bitcast(I32), cum))
                st.link(v.tensor_scalar(tcmp[:, :, 0], tids, cum[:, NE - 1:NE], None, ALU.is_lt))
                st.link(v.tensor_reduce(rden[:, 0:1], tcmp[:, 0::2, 0], AX.X, ALU.add))
                v.tensor_copy(te[:, N_SLOT_TILES:N_SLOT_TILES + 1].bitcast(I32), rden[:, 0:1]).then_inc(slot_rdy, 1)
        ar.at = after_x1 - NT * D

        ar.at = start_h
        xs = [ar.take([D]) for _ in range(2)]
        xT = [ar.take([KD, P]) for _ in range(2)]
        ge = ar.take([DF])
        hid = [ar.take([DF]) for _ in range(2)]
        hidT = [ar.take([KF, P]) for _ in range(2)]
        yo = [ar.take([D]) for _ in range(2)]
        assert ar.at <= mark_h
        x_ld = [sem(f"slot_x_in{s}") for s in range(2)]
        x_turned, x_cp, gu_mm, g_exp, g_dve, hid_rdy, h_turned, h_cp, dn_mm, y_rdy = (sem(n) for n in (
            "slot_turned", "slot_copied", "gate_up_mm", "gate_exp", "dve_experts", "hid_ready", "hid_turned", "hid_copied", "down_mm", "y_ready"))
        y_st = [sem(f"y_stored{s}") for s in range(2)]
        PAIRS = N_SLOT_TILES // 2
        te_i = te.bitcast(I32)

        def pairs_in_use(engine):
            return engine.value_load(te_i[0:1, N_SLOT_TILES:N_SLOT_TILES + 1], min_val=MIN_TILES // 2, max_val=PAIRS)

        def over_pairs(engine, turn):
            used = pairs_in_use(engine)
            turn(0, True)
            with engine.Fori(1, PAIRS) as i:
                with engine.If(i < used):
                    turn(i, False)
                with engine.Else():
                    engine.nop()

        with nc.Block() as block:
            @block.sync
            def _(sp):
                load_gate_up(sp, w_odd, 1, 1)
                load_down(sp, w_odd, 1, 1)
                with sp.Fori(1, NE // 2) as i:
                    for s, dst in enumerate((w_even, w_odd)):
                        e = 2 * i + s
                        done = sp.value_load(te_i[0:1, bass.ds(N_SLOT_TILES + 2 + e - 2, 1)], min_val=0, max_val=N_SLOT_TILES)
                        sp.wait_ge(gu_mm, done + 1)
                        load_gate_up(sp, dst, e, s)
                        sp.wait_ge(dn_mm, done + 1)
                        load_down(sp, dst, e, s)

            @block.gpsimd
            def _(pool):
                def load_x(i, first):
                    for s in range(2):
                        if not first:
                            pool.wait_ge(x_turned, 2 * i + s - 1)
                        pool.dma_start(xs[s], slot_x[bass.ds((2 * i + s) * P, P), :]).then_inc(x_ld[s], 16)

                def turn(i, first):
                    load_x(i + 1, False)
                    for s in range(2):
                        pool.wait_ge(y_rdy, 2 * i + s + 1)
                        pool.dma_start(slot_y[bass.ds((2 * i + s) * P, P), :], yo[s]).then_inc(y_st[s], 16)

                load_x(0, True)
                over_pairs(pool, turn)
                used = pairs_in_use(pool)
                for s in range(2):
                    pool.wait_ge(y_st[s], used * 16)
                    pool.wait_ge(x_ld[s], used * 16 + 16)

            @block.tensor
            def _(pe):
                def turn_x(i, s):
                    pe.wait_ge(x_ld[s], 16 * (i + 1))
                    pe.wait_ge(x_cp, 2 * i + s)
                    for k in range(KD):
                        last = nc.tensor.transpose(ps[:, k * P:(k + 1) * P], xs[s][:, k * P:(k + 1) * P], ident)
                    last.then_inc(x_turned, 1)

                def weights_of(j):
                    e = pe.value_load(te_i[0:1, bass.ds(j, 1)], min_val=0, max_val=NE - 1)
                    return 1 - e % 2, e // 2 + 1, (e + 1) // 2

                def gate_up(i, s, half, n_even, n_odd):
                    j = 2 * i + s
                    pe.wait_ge(gu_ld[0], n_even * 32)
                    pe.wait_ge(gu_ld[1], n_odd * 32 + 16)
                    pe.wait_ge(x_cp, j + 1)
                    for n in range(2):
                        for k in range(KD):
                            at = (n * KD + k) * DF
                            last = nc.tensor.matmul(bank(2 + 2 * s + n), xT[s][:, k, :], halves[:, bass.ds(half, 1), at:at + DF],
                                                    start=(k == 0), stop=(k == KD - 1))
                    last.then_inc(gu_mm, 1)

                def turn_hid(i, s):
                    pe.wait_ge(hid_rdy, 2 * i + s + 1)
                    for k in range(KF):
                        last = nc.tensor.transpose(bank(2 + 2 * s)[:, k * P:(k + 1) * P], hid[s][:, k * P:(k + 1) * P], ident)
                    last.then_inc(h_turned, 1)

                def down(i, s, half, n_even, n_odd, first):
                    j = 2 * i + s
                    pe.wait_ge(d_ld[0], n_even * 32)
                    pe.wait_ge(d_ld[1], n_odd * 32 + 16)
                    pe.wait_ge(h_cp, j + 1)
                    if not (first and s == 0):
                        pe.wait_ge(y_rdy, j)
                    for n in range(2):
                        for k in range(KF):
                            at = (2 * KD + 2 * k + n) * DF
                            last = nc.tensor.matmul(bank(6 + n), hidT[s][:, k, :], halves[:, bass.ds(half, 1), at:at + DF],
                                                    start=(k == 0), stop=(k == KF - 1))
                    last.then_inc(dn_mm, 1)

                def turn(i, first):
                    a = weights_of(2 * i)
                    b = weights_of(2 * i + 1)
                    gate_up(i, 0, *a)
                    turn_x(i + 1, 0)
                    gate_up(i, 1, *b)
                    turn_hid(i, 0)
                    turn_x(i + 1, 1)
                    down(i, 0, *a, first)
                    turn_hid(i, 1)
                    down(i, 1, *b, first)

                pe.wait_ge(x_ld[0], 16)
                for k in range(KD):
                    last = nc.tensor.transpose(ps[:, k * P:(k + 1) * P], xs[0][:, k * P:(k + 1) * P], ident)
                last.then_inc(x_turned, 1)
                turn_x(0, 1)
                pe.sem_inc(gu_mm, 1)
                pe.sem_inc(dn_mm, 1)
                over_pairs(pe, turn)

            @block.scalar
            def _(act):
                def copy_x(i, s, first):
                    act.wait_ge(x_turned, 2 * i + s + 1)
                    if not first:
                        act.wait_ge(gu_mm, 2 * i + s)
                    for half in range(2):
                        ins = nc.scalar.activation(xT[s][:, 4 * half:4 * half + 4, :], bank(half).rearrange("p (k t) -> p k t", k=4), ACT.Copy)
                    ins.then_inc(x_cp, 1)

                def gate_exp(i, s, first):
                    j = 2 * i + s
                    act.wait_ge(gu_mm, j + 2)
                    if not (first and s == 0):
                        act.wait_ge(hid_rdy, j)
                    nc.scalar.activation(ge, bank(2 + 2 * s), ACT.Exp, scale=-1.0).then_inc(g_exp, 1)

                def copy_hid(i, s, first):
                    j = 2 * i + s
                    act.wait_ge(h_turned, j + 1)
                    if not first:
                        act.wait_ge(dn_mm, j)
                    nc.scalar.activation(hidT[s], bank(2 + 2 * s).rearrange("p (k t) -> p k t", k=KF), ACT.Copy).then_inc(h_cp, 1)

                def turn(i, first):
                    gate_exp(i, 0, first)
                    copy_x(i + 1, 0, False)
                    gate_exp(i, 1, first)
                    copy_hid(i, 0, first)
                    copy_x(i + 1, 1, False)
                    copy_hid(i, 1, first)

                copy_x(0, 0, True)
                copy_x(0, 1, True)
                over_pairs(act, turn)

            @block.vector
            def _(dve):
                def silu(i, s, first):
                    j = 2 * i + s

                    def link(ins, n):
                        ins.then_inc(g_dve, 1)
                        dve.wait_ge(g_dve, 3 * j + n)

                    dve.wait_ge(g_exp, j + 1)
                    if not first:
                        dve.wait_ge(h_turned, j - 1)
                    link(nc.vector.tensor_scalar(ge, ge, 1.0, None, ALU.add), 1)
                    link(nc.vector.reciprocal(ge, ge), 2)
                    link(nc.vector.tensor_tensor(hid[s], bank(2 + 2 * s), ge, ALU.mult), 3)
                    nc.vector.tensor_tensor(hid[s], hid[s], bank(3 + 2 * s), ALU.mult).then_inc(hid_rdy, 1)

                def store(i, s, first):
                    dve.wait_ge(dn_mm, 2 * i + s + 2)
                    if not first:
                        dve.wait_ge(y_st[s], 16 * i)
                    for half in range(2):
                        ins = nc.vector.tensor_copy(yo[s][:, half * BANK:(half + 1) * BANK], bank(6 + half))
                    ins.then_inc(y_rdy, 1)

                def turn(i, first):
                    silu(i, 0, first)
                    silu(i, 1, first)
                    store(i, 0, first)
                    store(i, 1, first)

                over_pairs(dve, turn)

        ar.at = after_x1
        g2 = ar.take([2, D])
        fn = ar.take([D])
        Y_RING = 3
        ya, yb = ([ar.take([D]) for _ in range(Y_RING)] for _ in range(2))
        z = [ar.take([D]) for _ in range(2)]
        junk = ar.take([D])
        fs = ar.take([NT, 4])
        f_in, ya_scaled, z_rdy, z_sq, z_mean, z_guess, z_out, dve_f, act_f = (sem(n) for n in (
            "final_in", "first_rows_gated", "z_ready", "z_squares", "z_mean", "z_guess", "z_out", "dve_final", "act_final"))
        y_in = [sem(f"rows_in{s}") for s in range(Y_RING)]
        y_stored = [sem("y_out0"), sem("y_out1")]
        with nc.Block() as block:
            @block.sync
            def _(sp):
                sp.dma_start(g2, mod_row(5)).then_inc(f_in, 16)
                sp.dma_start(fn, bass.AP(final_norm.tensor, 0, [[0, P], [1, D]])).then_inc(f_in, 16)
                for t in range(NT):
                    sp.wait_ge(z_out, t + 1)
                    sp.dma_start(y_all[t * P:(t + 1) * P, :], z[t % 2]).then_inc(y_stored[t % 2], 16)
                for s in range(2):
                    sp.wait_ge(y_stored[s], 16 * ((NT + 1 - s) // 2))
                sp.wait_ge(out_stored, stored[0])

            @block.gpsimd
            def _(pool):
                for t in range(NT):
                    if t >= Y_RING:
                        pool.wait_ge(z_rdy, t - Y_RING + 1)
                    for n, y in enumerate((ya, yb)):
                        pool.indirect_dma_start(y[t % Y_RING], None, slot_y, bass.IndirectOffsetOnAxis(slot[n].bitcast(U32)[:, t:t + 1], 0)).then_inc(y_in[t % Y_RING], 16)

            @block.scalar
            def _(act):
                st = Steps(act, act_f)
                for t in range(NT + 1):
                    if t < NT:
                        act.wait_ge(y_in[t % Y_RING], 32 * (t // Y_RING + 1))
                        nc.scalar.activation(ya[t % Y_RING], ya[t % Y_RING], ACT.Copy, scale=gate[0][:, t:t + 1]).then_inc(ya_scaled, 1)
                    if t:
                        u = t - 1
                        act.wait_ge(z_rdy, u + 1)
                        st.link(nc.scalar.activation(junk, x1[:, u, :], ACT.Square, accum_out=fs[:, u, 0:1]))
                        nc.scalar.activation(junk[:, 0:1], fs[:, u, 0:1], ACT.Square).then_inc(z_sq, 1)
                        act.wait_ge(z_mean, u + 1)
                        st.link(nc.scalar.activation(fs[:, u, 1:2], fs[:, u, 0:1], ACT.Ln))
                        nc.scalar.activation(fs[:, u, 2:3], fs[:, u, 1:2], ACT.Exp, scale=-0.5).then_inc(z_guess, 1)

            @block.vector
            def _(dve):
                st = Steps(dve, dve_f)
                v = nc.vector
                f = lambda t, n: fs[:, t, n:n + 1]

                def combine(t):
                    y = yb[t % Y_RING]
                    dve.wait_ge(ya_scaled, t + 1)
                    st.link(v.scalar_tensor_tensor(out=y, in0=y, scalar=gate[1][:, t:t + 1], in1=ya[t % Y_RING], op0=ALU.mult, op1=ALU.add))
                    st.link(v.tensor_tensor(y, y, g2[:, side(t), :], ALU.mult))
                    v.tensor_tensor(x1[:, t, :], y, x1[:, t, :], ALU.add).then_inc(z_rdy, 1)

                def mean(t):
                    dve.wait_ge(z_sq, t + 1)
                    v.tensor_scalar(f(t, 0), f(t, 0), 1.0 / D, EPS, ALU.mult, ALU.add).then_inc(z_mean, 1)

                def finish(t):
                    dve.wait_ge(z_guess, t + 1)
                    newton(st, f(t, 2), f(t, 3), f(t, 0))
                    if t >= 2:
                        dve.wait_ge(y_stored[t % 2], 16 * (t // 2))
                    v.scalar_tensor_tensor(out=z[t % 2], in0=x1[:, t, :], scalar=f(t, 2), in1=fn, op0=ALU.mult, op1=ALU.mult).then_inc(z_out, 1)

                dve.wait_ge(f_in, 32)
                for t in range(NT + 2):
                    if t < NT:
                        combine(t)
                    if 1 <= t <= NT:
                        mean(t - 1)
                    if t >= 2:
                        finish(t - 2)


def constants():
    f = np.float32
    ident = np.eye(P, dtype=f)
    upper = np.triu(np.ones((P, P), f), 1)
    sel = np.zeros((64, 8, P), f)
    for way in range(2):
        for h in range(MH):
            sel[32 * way + h, MH * way + h, :] = 1
    s, t = np.arange(P)[:, None], np.arange(P)[None, :]
    scanmask = np.stack([np.where(s <= t, 0, NEG), np.where(s >= t, 0, NEG)]).astype(f)
    reset = np.ones((64, TOK), f)
    reset[:32, 0::P] = 0
    reset[32:, P - 1::P] = 0
    q = np.arange(GRID_W)
    start = np.clip(q - KCOLS // 2, 0, GRID_W - KCOLS)[:, None]
    k = np.arange(GRID_W)[None, :]
    window = np.where((k >= start) & (k < start + KCOLS), 0, NEG).astype(f)
    winmask = np.tile(window[None, :, None, :], (2, 1, TAB_SLOTS, 1))
    winmask[0, :, EDGE_SLOTS + 8:, :] = NEG
    winmask[1, :, EDGE_SLOTS, :] = NEG
    winmask[1, :, EDGE_SLOTS + 9, :] = NEG
    winmask = winmask.reshape(P, TAB_SLOTS, GRID_W)
    band = np.zeros((PG, 6, P, P), f)
    for g, w in enumerate(WINDOWS):
        for b, (lo_end, hi_end) in enumerate(((False, False), (True, False), (False, True), (True, True))):
            for tt in range(P):
                lo, hi = tt - w // 2, tt - w // 2 + w
                n_lo, n_hi = max(lo, 0) if lo_end else lo, min(hi, P) if hi_end else hi
                band[g, b, max(lo, 0):min(hi, P), tt] = f(1) / f(n_hi - n_lo)
                band[g, b, tt, tt] -= 1
                if b == 0:
                    if lo < 0:
                        band[g, 4, P + lo:P, tt] = f(1) / f(w)
                    if hi > P:
                        band[g, 5, 0:hi - P, tt] = f(1) / f(w)
    return {"k_ident": ident, "k_upper": upper, "k_sel": sel, "k_scanmask": np.ascontiguousarray(scanmask.transpose(1, 0, 2)), "k_reset": reset,
            "k_winmask": winmask, "k_band": np.ascontiguousarray(band.reshape(PG * 6, P, P).transpose(1, 0, 2)), "k_tile_ids": np.arange(N_SLOT_TILES, dtype=f)}


def kernel(**inputs):
    import concourse.bacc as bacc
    from concourse.bass_utils import run_bass_kernel_spmd as run

    a = {k: np.ascontiguousarray(v) for k, v in inputs.items()}
    ins = {
        "x_all": np.concatenate([a["x_sample"].reshape(LAT, D), a["x_prompt"].reshape(CTX, D)]),
        "cache_k": a["cache_k_attn"].reshape(CTX, AW), "cache_v": a["cache_v_attn"].reshape(CTX, AW),
        "state_C": a["state_mlstm_C"].reshape(2, MH, MD, MD), "state_n": a["state_mlstm_n"].reshape(2, MH, MD),
        "state_m": a["state_mlstm_m"].reshape(2, MH), "c_both": np.stack([a["c"].reshape(D), a["c_ctx"].reshape(D)]),
        "w_ada": a["w_ada"].reshape(D, 6 * D), "b_ada": a["b_ada"].reshape(6 * D), "norm1": a["norm1"].reshape(D),
        "w_in": a["w_in"].reshape(D, -1), "b_in": a["b_in"].reshape(-1),
        "rpb_pad": np.pad(a["rpb"].reshape(HEADS, RPB_R, RPB_C), ((0, 0), (0, 0), (GRID_W - KCOLS, GRID_W - KCOLS))),
        "ml_norm": a["ml_norm"].reshape(MW), "w_pool": a["w_pool"].reshape(PG, PD, PD), "pool_scale": a["pool_scale"].reshape(PW),
        "w_out": a["w_out"].reshape(D, D), "norm2": a["norm2"].reshape(D), "w_router": a["w_router"], "b_router": a["b_router"],
        "w_gate": a["w_gate"].reshape(NE, D, DF), "w_up": a["w_up"].reshape(NE, D, DF), "w_down": a["w_down"].reshape(NE, DF, D),
        "final_norm": a["final_norm"], **constants(),
    }
    outs = {"y_all": (TOK, D), "out_k": (CTX, AW), "out_v": (CTX, AW), "out_C": (2, MH, MD, MD), "out_n": (2, MH, MD), "out_m": (2, MH)}
    nc = bacc.Bacc("TRN2", target_bir_lowering=False, num_devices=1)
    aps = {k: nc.dram_tensor("in_" + k, v.shape, F32, kind="ExternalInput").ap() for k, v in ins.items()}
    aps |= {k: nc.dram_tensor(k, s, F32, kind="ExternalOutput").ap() for k, s in outs.items()}
    program(nc, **aps)
    r = run(nc, [{"in_" + k: v for k, v in ins.items()}], core_ids=[0]).results[0]
    y = r["y_all"]
    return (y[LAT:].reshape(1, CTX, D), y[:LAT].reshape(1, LAT, D),
            r["out_k"].reshape(1, 1, CTX, HEADS, HD), r["out_v"].reshape(1, 1, CTX, HEADS, HD),
            r["out_C"].reshape(1, 1, 2, MH, MD, MD), r["out_n"].reshape(1, 1, 2, MH, MD), r["out_m"].reshape(1, 1, 2, MH))
```

```python
from contextlib import ExitStack

import numpy as np

import concourse.bass as bass
from concourse import mybir

F32 = mybir.dt.float32
U32 = mybir.dt.uint32
I32 = mybir.dt.int32
ALU = mybir.AluOpType
ACT = mybir.ActivationFunctionType
AX = mybir.AxisListType

P = 128
D = 1024
KD = D // P
LAT, CTX = 1024, 128
TOK = LAT + CTX
NT = TOK // P
CTX_TILE = NT - 1
EPS = 1e-6
NEG = -1e30
BANK = 512
SB_COLUMNS = 52992

HEADS, HD = 6, 64
AW = HEADS * HD
GRID_W, ROWS = 64, 16
KROWS, KCOLS = 8, 16
EDGE_SLOTS = 14
INNER_ROWS = 10
TAB_SLOTS = EDGE_SLOTS + INNER_ROWS
RPB_R, RPB_C = 15, 31
PADW = 2 * GRID_W - 1

MH, MD = 4, 96
MW = MH * MD
MA = MD + 1
PG, PD = 4, 64
PW = PG * PD
WINDOWS = (2, 4, 8, 16)
N_GATES = 16
C_QA, C_KA, C_VA = 0, AW, 2 * AW
C_QB = 3 * AW
C_KB, C_VB, C_OB, C_TAIL = C_QB + MW, C_QB + 2 * MW, C_QB + 3 * MW, C_QB + 4 * MW
TAIL = N_GATES + PW

NE, EG, EPG, DF = 16, 4, 4, 512
KF = DF // P
N_SLOT_TILES = 34
SLOTS = N_SLOT_TILES * P
MIN_TILES = 2 * TOK // P
CHUNK = 2 * P
MAX_CHUNKS = (2 * TOK - NE) // CHUNK + NE
MIN_CHUNKS = 2 * TOK // CHUNK
CHUNKS = MAX_CHUNKS + 2
CODE = 2048
WIDTHS = (128, 144, 160, 176, 192, 256)


class Steps:

    def __init__(self, engine, sem):
        self.engine, self.sem, self.n = engine, sem, 0

    def add(self, instruction):
        instruction.then_inc(self.sem, 1)
        self.n = self.n + 1
        return instruction

    def settle(self):
        self.engine.wait_ge(self.sem, self.n)

    def link(self, instruction):
        self.add(instruction)
        self.settle()


class Arena:

    def __init__(self, tensor, columns):
        self.tensor, self.columns, self.at, self.high = tensor, columns, 0, 0

    def take(self, shape, rows=P):
        n = int(np.prod(shape))
        a = self.tensor[0:rows, self.at:self.at + n]
        self.at += n
        self.high = max(self.high, self.at)
        assert self.at <= self.columns, (self.at, self.columns)
        if len(shape) == 2:
            a = a.rearrange("p (a b) -> p a b", a=shape[0])
        if len(shape) == 3:
            a = a.rearrange("p (a b c) -> p a b c", a=shape[0], b=shape[1])
        return a


def bc(ap, shape):
    return ap.to_broadcast(list(shape))


def program(nc, x_all, cache_k, cache_v, state_C, state_n, state_m, c_both, w_ada, b_ada, norm1, w_in, b_in,
            rpb_pad, ml_norm, w_pool, pool_scale, w_out, norm2, w_router, b_router, w_gate, w_up, w_down,
            final_norm, k_ident, k_upper, k_sel, k_scanmask, k_reset, k_winmask, k_band, k_chunk_ids, k_token_ids,
            y_all, out_k, out_v, out_C, out_n, out_m):
    ctx = ExitStack()
    with ctx, nc.allow_non_contiguous_dma(reason="biases, states and modulation inputs as columns"):
        sb = ctx.enter_context(nc.sbuf_tensor("sb", [P, SB_COLUMNS], F32))
        ps = ctx.enter_context(nc.psum_tensor("ps", [P, 8 * BANK], F32))
        ar = Arena(sb, SB_COLUMNS)

        def sem(name):
            return ctx.enter_context(nc.semaphore(name))

        def bank(n, cols=BANK, at=0):
            return ps[:, n * BANK + at:n * BANK + at + cols]

        mod_rows = nc.dram_tensor("mod_rows", [2, 6 * D], F32, kind="Internal").ap()
        rpb_rows = nc.dram_tensor("rpb_rows", [HEADS * RPB_R, GRID_W, PADW], F32, kind="Internal").ap()
        h2_rows = nc.dram_tensor("h2_rows", [TOK, D], F32, kind="Internal").ap()
        slot_token = nc.dram_tensor("slot_token", [SLOTS, 1], I32, kind="Internal").ap()
        slot_y = nc.dram_tensor("slot_y", [SLOTS, D], F32, kind="Internal").ap()

        ident = ar.take([P])
        gate = [ar.take([NT]) for _ in range(2)]
        slot = [ar.take([NT]) for _ in range(2)]
        chunk_tab = ar.take([2 * CHUNKS + 1 + NE]).bitcast(I32)
        tile_of, code_of = (chunk_tab[:, n * CHUNKS:(n + 1) * CHUNKS] for n in range(2))
        n_chunks, last_chunk = chunk_tab[:, 2 * CHUNKS:2 * CHUNKS + 1], chunk_tab[:, 2 * CHUNKS + 1:]
        ss2, y2, t2 = (ar.take([NT]) for _ in range(3))
        ysb = ar.take([NT * MH])
        const_ready = sem("const_ready")
        slots_zeroed = sem("slots_zeroed")
        out_stored = sem("out_stored")
        stored = [0]

        ar.columns -= NT * MW
        og = sb[:, ar.columns:ar.columns + NT * MW].rearrange("p (t n) -> p t n", t=NT)
        start_h = ar.at
        ar.take([KD, TOK])
        mark_h = ar.at
        x_res = ar.take([NT, D])
        ss, y0, nt1 = (ar.take([NT]) for _ in range(3))
        sq_junk = ar.take([D])
        cc = ar.take([2, KD])
        ce = ar.take([2, KD])
        ada = [ar.take([KD, BANK]) for _ in range(2)]
        brow = ar.take([6 * D])
        nrow = ar.take([2, D])
        mrow = ar.take([6 * D])
        c_ready = sem("c_ready")
        silu_exp = sem("silu_exp")
        silu_done = sem("silu_done")
        ada_loaded = [sem(f"ada_loaded{s}") for s in range(2)]
        mod_mm = sem("mod_mm")
        mod_evac = sem("mod_evac")
        mod_ready = sem("mod_ready")
        mod_stored = sem("mod_stored")
        x_loaded = sem("x_loaded")
        dve_mod, act_mod = sem("dve_mod"), sem("act_mod")
        squares, mean_ready, guess_ready = sem("n1_squares"), sem("n1_mean"), sem("n1_guess")
        MOD_BLOCKS, EARLY_BLOCKS, AHEAD = 6 * D // BANK, 2 * D // BANK, 2
        ada_src = w_ada.rearrange("(k p) n -> p k n", p=P)

        def load_ada(sp, n):
            if n >= 2:
                sp.wait_ge(mod_mm, n - 1)
            sp.dma_start(ada[n % 2], ada_src[:, :, n * BANK:(n + 1) * BANK]).then_inc(ada_loaded[n % 2], 16)

        def multiply_ada(pe, n):
            pe.wait_ge(ada_loaded[n % 2], 16 * (n // 2 + 1))
            if n >= 2:
                pe.wait_ge(mod_evac, n - 1)
            for k in range(KD):
                last = nc.tensor.matmul(bank(2 + n % 2)[0:2], cc[:, :, k], ada[n % 2][:, k, :],
                                        start=(k == 0), stop=(k == KD - 1))
            last.then_inc(mod_mm, 1)

        def read_ada(dve, n):
            dve.wait_ge(mod_mm, n + 1)
            cols_n = slice(n * BANK, (n + 1) * BANK)
            nc.vector.tensor_tensor(mrow[0:2, cols_n], bank(2 + n % 2)[0:2], brow[0:2, cols_n], ALU.add).then_inc(mod_evac, 1)

        def scale_ada(part, v):
            row = mrow[0:2, part * D:(part + 1) * D]
            nc.vector.scalar_tensor_tensor(out=row, in0=row, scalar=1.0, in1=nrow[0:2, v],
                                           op0=ALU.add, op1=ALU.mult).then_inc(mod_ready, 1)

        def newton(st, y, t, ms):
            st.link(nc.vector.reciprocal(y, y))
            st.link(nc.vector.tensor_tensor(t, y, y, ALU.mult))
            st.link(nc.vector.scalar_tensor_tensor(out=t, in0=t, scalar=-0.5, in1=ms, op0=ALU.mult, op1=ALU.mult))
            st.link(nc.vector.scalar_tensor_tensor(out=y, in0=t, scalar=1.5, in1=y, op0=ALU.add, op1=ALU.mult))

        with nc.Block() as block:
            @block.sync
            def _(sp):
                for v in range(2):
                    sp.dma_start(cc[:, v, :], c_both[v].rearrange("(k p) -> p k", p=P)).then_inc(c_ready, 16)
                sp.dma_start(brow[0:2], bass.AP(b_ada.tensor, 0, [[0, 2], [1, 6 * D]])).then_inc(c_ready, 16)
                for v, n in enumerate((norm1, norm2)):
                    sp.dma_start(nrow[0:2, v], bass.AP(n.tensor, 0, [[0, 2], [1, D]])).then_inc(c_ready, 16)
                for n in range(EARLY_BLOCKS + AHEAD):
                    load_ada(sp, n)
                sp.wait_ge(mod_ready, 1)
                sp.dma_start(mod_rows[:, 0:2 * D], mrow[0:2, 0:2 * D]).then_inc(mod_stored, 16)
                sp.wait_ge(mod_stored, 16)

            @block.scalar
            def _(act):
                st = Steps(act, act_mod)
                act.dma_start(ident, k_ident).then_inc(const_ready, 16)
                act.wait_ge(c_ready, 16 * 5)
                nc.scalar.activation(ce, cc, ACT.Exp, scale=-1.0).then_inc(silu_exp, 1)
                for n in range(3):
                    act.wait_ge(ada_loaded[n % 2], 16 * (n // 2 + 1))
                    for t in range(3 * n, 3 * n + 3):
                        act.dma_start(x_res[:, t, :], x_all[t * P:(t + 1) * P, :]).then_inc(x_loaded, 16)
                act.wait_ge(x_loaded, 16 * NT)
                for t in range(NT):
                    if t:
                        st.settle()
                    st.add(nc.scalar.activation(sq_junk, x_res[:, t, :], ACT.Square, accum_out=ss[:, t:t + 1]))
                st.settle()
                nc.scalar.activation(sq_junk[:, 0:1], ss[:, 0:1], ACT.Square).then_inc(squares, 1)
                act.wait_ge(mean_ready, 1)
                nc.scalar.activation(y0, ss, ACT.Sqrt).then_inc(guess_ready, 1)
                act.wait_ge(const_ready, 16)

            @block.vector
            def _(dve):
                st = Steps(dve, dve_mod)
                dve.wait_ge(silu_exp, 1)
                st.link(nc.vector.tensor_scalar(ce, ce, 1.0, None, ALU.add))
                st.link(nc.vector.reciprocal(ce, ce))
                nc.vector.tensor_tensor(cc, cc, ce, ALU.mult).then_inc(silu_done, 1)
                for n in range(EARLY_BLOCKS):
                    read_ada(dve, n)
                dve.wait_ge(mod_evac, EARLY_BLOCKS)
                scale_ada(1, 0)
                dve.wait_ge(squares, 1)
                nc.vector.tensor_scalar(ss, ss, 1.0 / D, EPS, ALU.mult, ALU.add).then_inc(mean_ready, 1)
                dve.wait_ge(guess_ready, 1)
                newton(st, y0, nt1, ss)

            @block.tensor
            def _(pe):
                pe.wait_ge(silu_done, 1)
                for n in range(EARLY_BLOCKS):
                    multiply_ada(pe, n)

        def mod_row(part):
            return bass.AP(mod_rows.tensor, part * D, [[0, P], [6 * D, 2], [1, D]])

        def side(t):
            return 1 if t == CTX_TILE else 0

        def load_rows_of(rows, parts, sp, loaded):
            for row, part in zip(rows, parts[::-1]):
                sp.dma_start(row, mod_row(part)).then_inc(loaded, 16)

        def norm_stage(tag, x, rinv, rows_of, nat, outT, sp_more=None, pe_more=None, dve_more=None, dve_last=None, pool_more=None, pe_first=None, dve_first=None, rows=None):
            mark = ar.at
            row_loaded = sem(tag + "row_loaded")
            scale_row, shift_row = rows[0] if rows else (ar.take([2, D]), ar.take([2, D]))
            if rows:
                row_loaded = rows[1]
            ring = nat is None
            if ring:
                two = [ar.take([D]) for _ in range(2)]
            nat_ready, turned, copied, dve_s = (sem(tag + n) for n in ("nat_ready", "turned", "copied", "dve"))
            nat_of = lambda t: two[t % 2] if ring else nat[:, t, :]
            with nc.Block() as block:
                @block.sync
                def _(sp):
                    if not rows:
                        load_rows_of((scale_row, shift_row), rows_of, sp, row_loaded)
                    if sp_more:
                        sp_more(sp)

                @block.scalar
                def _(act):
                    for t in range(NT):
                        act.wait_ge(turned, t + 1)
                        for half in range(2):
                            ins = nc.scalar.activation(
                                outT[:, 4 * half:4 * half + 4, t * P:(t + 1) * P],
                                bank(4 * (t % 2) + half).rearrange("p (k t) -> p k t", k=4), ACT.Copy)
                        ins.then_inc(copied, 1)

                @block.gpsimd
                def _(pool):
                    if pool_more:
                        pool_more(pool, nat_ready)

                @block.vector
                def _(dve):
                    st = Steps(dve, dve_s)
                    if dve_first:
                        dve_first(dve)
                    dve.wait_ge(row_loaded, 32)
                    for t in range(NT):
                        if ring and t >= 2:
                            dve.wait_ge(turned, t - 1)
                        st.link(nc.vector.scalar_tensor_tensor(
                            out=nat_of(t), in0=x[:, t, :], scalar=rinv[:, t:t + 1], in1=scale_row[:, side(t), :],
                            op0=ALU.mult, op1=ALU.mult))
                        nc.vector.tensor_tensor(nat_of(t), nat_of(t), shift_row[:, side(t), :],
                                                ALU.add).then_inc(nat_ready, 1)
                        if dve_more:
                            dve_more(dve, t)
                    if dve_last:
                        dve_last(dve)

                @block.tensor
                def _(pe):
                    if pe_first:
                        pe_first(pe)
                    for t in range(NT):
                        pe.wait_ge(nat_ready, t + 1)
                        if t >= 2:
                            pe.wait_ge(copied, t - 1)
                        for k in range(KD):
                            last = nc.tensor.transpose(
                                ps[:, (4 * (t % 2)) * BANK + k * P:(4 * (t % 2)) * BANK + (k + 1) * P],
                                nat_of(t)[:, k * P:(k + 1) * P], ident)
                        last.then_inc(turned, 1)
                        if pe_more:
                            pe_more(pe, t, copied)
            ar.at = mark

        hT = sb[:, start_h:mark_h].rearrange("p (k t) -> p k t", k=KD)

        FROM = EARLY_BLOCKS + AHEAD

        def rest_sp(sp):
            for n in range(FROM, MOD_BLOCKS):
                load_ada(sp, n)
            sp.dma_start(w_first, w_in.rearrange("(k p) n -> p k n", p=P)[:, :, C_QA:C_QA + AW]).then_inc(w_first_in, 16)
            sp.wait_ge(mod_ready, 2)
            sp.dma_start(mod_rows[:, 2 * D:6 * D], mrow[0:2, 2 * D:6 * D]).then_inc(mod_stored, 16)
            sp.wait_ge(mod_stored, 32)

        def first_pe(pe):
            for n in range(EARLY_BLOCKS, FROM):
                multiply_ada(pe, n)

        def first_dve(dve):
            for n in range(EARLY_BLOCKS, FROM):
                read_ada(dve, n)

        def rest_pe(pe, t, copied):
            if FROM + t < MOD_BLOCKS:
                multiply_ada(pe, FROM + t)

        def rest_dve(dve, t):
            if t and FROM + t - 1 < MOD_BLOCKS:
                read_ada(dve, FROM + t - 1)

        def rest_scale(dve):
            dve.wait_ge(mod_evac, MOD_BLOCKS)
            scale_ada(4, 1)

        w_first = sb[:, ar.columns:ar.columns + KD * AW].rearrange("p (k n) -> p k n", k=KD)
        w_first_in = sem("w_first_in")

        norm_stage("n1_", x_res, y0, (0, 1), None, hT, rest_sp, rest_pe, rest_dve, rest_scale,
                   pe_first=first_pe, dve_first=first_dve)
        ar.at = mark_h

        qbT, kbT = ar.take([MH, TOK]), ar.take([MH, TOK])
        vb = ar.take([NT, MH, MA])
        gi, gf = ar.take([NT, 64]), ar.take([NT, 64])
        after_mlstm_in = ar.at
        qaT, kaT = ar.take([HEADS, TOK]), ar.take([3, TOK])
        va = ar.take([NT, AW])
        after_attention_in = ar.at
        pin = ar.take([NT, PW])
        after_proj = ar.at
        wring = [ar.take([KD, AW]) for _ in range(2)]
        zero_tile = ar.take([D])
        mln = ar.take([MW])
        bias_a, bias_b = ar.take([6]), ar.take([6])
        block_of = [ar.take([BANK]) for _ in range(2)]
        HEAD_PIECES = [[(0, 0, 0, 96), (96, 1, 0, 32)],
                       [(0, 1, 32, 32), (32, 1, 64, 32), (64, 2, 0, 64)],
                       [(0, 2, 64, 32), (32, 3, 0, 32), (64, 3, 32, 32), (96, 3, 64, 32)]]
        bias_row = ar.take([3 * MW + TAIL])
        ofs = {C_VA: 0, C_VB: MW, C_OB: 2 * MW, C_TAIL: 3 * MW}
        groups = [("T", C_QA, AW), ("N", C_OB, MW), ("T", C_KA, AW), ("N", C_VA, AW), ("S", C_QB, MW), ("S", C_KB, MW),
                  ("N", C_VB, MW), ("N", C_TAIL, TAIL)]
        units = []
        for g, (kind, c0, n) in enumerate(groups):
            if kind != "N":
                for b in range(n // P):
                    units += [(g, b, P, t0, tn) for t0, tn in ((0, 512), (512, 512), (1024, 128))]
            else:
                units += [(g, t, n, t * P, P) for t in range(NT)]
        last_of = {g: max(i for i, u in enumerate(units) if u[0] == g) for g in range(len(groups))}
        w_loaded = [sem(f"w_loaded{s}") for s in range(2)]
        by_block = [i for i, u in enumerate(units) if groups[u[0]][0] == "S"]
        bias_loaded, shifted = sem("bias_loaded"), sem("heads_shifted")
        proj_mm, proj_evac = sem("proj_mm"), sem("proj_evac")
        dve_proj, sig_exp, zeros_ready = sem("dve_proj"), sem("sig_exp"), sem("zeros_ready")
        with nc.Block() as block:
            @block.sync
            def _(sp):
                src = w_in.rearrange("(k p) n -> p k n", p=P)
                sp.dma_start(mln, bass.AP(ml_norm.tensor, 0, [[0, P], [1, MW]])).then_inc(bias_loaded, 16)
                sp.dma_start(bias_a, b_in[0:2 * AW].rearrange("(b p) -> p b", p=P)).then_inc(bias_loaded, 16)
                sp.dma_start(bias_b, b_in[C_QB:C_QB + 2 * MW].rearrange("(b p) -> p b", p=P)).then_inc(bias_loaded, 16)
                for c0, at in ofs.items():
                    n = TAIL if c0 == C_TAIL else MW
                    sp.dma_start(bias_row[:, at:at + n], bass.AP(b_in.tensor, c0, [[0, P], [1, n]])).then_inc(bias_loaded, 16)
                for g, (_, c0, n) in list(enumerate(groups))[1:]:
                    if g >= 3:
                        sp.wait_ge(proj_mm, last_of[g - 2] + 1)
                    sp.dma_start(wring[g % 2][:, :, 0:n], src[:, :, c0:c0 + n]).then_inc(w_loaded[g % 2], 16)
                    if g == 2:
                        sp.dma_start(rpb_rows, bass.AP(rpb_pad.tensor, 0, [[PADW, HEADS * RPB_R], [0, GRID_W], [1, PADW]])).then_inc(mod_stored, 16)
                sp.wait_ge(mod_stored, 48)

            @block.tensor
            def _(pe):
                seen = set()
                for i, (g, b, m, t0, tn) in enumerate(units):
                    if g not in seen:
                        seen.add(g)
                        if g == 0:
                            pe.wait_ge(w_first_in, 16)
                        else:
                            pe.wait_ge(w_loaded[g % 2], 16 * ((g + 1) // 2))
                    if i >= 8:
                        pe.wait_ge(proj_evac, i - 7)
                    w = wring[g % 2] if g else w_first
                    for k in range(KD):
                        if groups[g][0] != "N":
                            last = nc.tensor.matmul(bank(i % 8)[0:m, 0:tn], w[:, k, b * m:(b + 1) * m],
                                                    hT[:, k, t0:t0 + tn], start=(k == 0), stop=(k == KD - 1))
                        else:
                            last = nc.tensor.matmul(bank(i % 8)[:, 0:m], hT[:, k, t0:t0 + P], w[:, k, 0:m],
                                                    start=(k == 0), stop=(k == KD - 1))
                    last.then_inc(proj_mm, 1)

            @block.gpsimd
            def _(pool):
                nc.gpsimd.memset(zero_tile, 0.0).then_inc(zeros_ready, 1)
                nc.gpsimd.memset(qaT, 0.0).then_inc(zeros_ready, 1)
                nc.gpsimd.memset(vb, 1.0).then_inc(zeros_ready, 1)
                nc.gpsimd.memset(gi, 0.0).then_inc(zeros_ready, 1)
                nc.gpsimd.memset(gf, 0.0).then_inc(zeros_ready, 1)
                pool.wait_ge(zeros_ready, 5)
                pool.dma_start(slot_token.rearrange("(p c) o -> p (c o)", p=P), zero_tile[:, 0:N_SLOT_TILES].bitcast(I32)).then_inc(slots_zeroed, 16)
                with pool.Fori(MIN_TILES, N_SLOT_TILES) as j:
                    pool.dma_start(slot_y[bass.ds(j * P, P), :], zero_tile).then_inc(slots_zeroed, 16)
                pool.wait_ge(slots_zeroed, 16 * (1 + N_SLOT_TILES - MIN_TILES))

            @block.scalar
            def _(act):
                act.wait_ge(proj_evac, last_of[1] + 1)
                nc.scalar.activation(og, og, ACT.Exp, scale=-1.0).then_inc(sig_exp, 1)
                for n, i in enumerate(by_block):
                    g, b, _, t0, tn = units[i]
                    dst = qbT if groups[g][1] == C_QB else kbT
                    act.wait_ge(proj_evac, i + 1)
                    for row, h, to, rows in HEAD_PIECES[b]:
                        ins = nc.scalar.activation(dst[to:to + rows, h, t0:t0 + tn], block_of[n % 2][row:row + rows, 0:tn], ACT.Copy)
                    ins.then_inc(shifted, 1)

            @block.vector
            def _(dve):
                st = Steps(dve, dve_proj)
                dve.wait_ge(bias_loaded, 16 * 7)
                dve.wait_ge(zeros_ready, 5)
                for i, (g, b, m, t0, tn) in enumerate(units):
                    dve.wait_ge(proj_mm, i + 1)
                    c0 = groups[g][1]
                    p = bank(i % 8)
                    if groups[g][0] != "N":
                        if c0 < C_VA:
                            bias = bias_a[:, (c0 // P) + b:(c0 // P) + b + 1]
                            scale = HD ** -0.5 if c0 == C_QA else 1.0
                        else:
                            col = (0 if c0 == C_QB else MW // P) + b
                            bias = bias_b[:, col:col + 1]
                            scale = float(MD) ** -0.5 if c0 == C_QB else 1.0
                        if c0 == C_QA:
                            for half in range(2):
                                rows = slice(HD * half, HD * half + HD)
                                ins = nc.vector.tensor_scalar(qaT[rows, 2 * b + half, t0:t0 + tn], p[rows, 0:tn], bias[rows],
                                                              scale, ALU.add, ALU.mult)
                        elif groups[g][0] == "T":
                            ins = nc.vector.tensor_scalar(kaT[:, b, t0:t0 + tn], p[:, 0:tn], bias, scale, ALU.add, ALU.mult)
                        else:
                            n = by_block.index(i)
                            if n >= 2:
                                dve.wait_ge(shifted, n - 1)
                            ins = nc.vector.tensor_scalar(block_of[n % 2][:, 0:tn], p[:, 0:tn], bias, scale, ALU.add, ALU.mult)
                    else:
                        row = bias_row[:, ofs[c0]:ofs[c0] + m]
                        if c0 == C_VA:
                            ins = nc.vector.tensor_tensor(va[:, b, :], p[:, 0:m], row, ALU.add)
                        elif c0 == C_VB:
                            ins = nc.vector.tensor_tensor(vb[:, b, :, 0:MD], p[:, 0:m].rearrange("p (h d) -> p h d", h=MH),
                                                          row.rearrange("p (h d) -> p h d", h=MH), ALU.add)
                        elif c0 == C_OB:
                            ins = nc.vector.tensor_tensor(og[:, b, :], p[:, 0:m], row, ALU.add)
                        else:
                            for dst, at in ((gi, 0), (gf, MH)):
                                for way in range(2):
                                    c = at + 2 * MH * way
                                    st.add(nc.vector.tensor_tensor(dst[:, b, 32 * way:32 * way + MH], p[:, c:c + MH],
                                                                   row[:, c:c + MH], ALU.add))
                            ins = nc.vector.tensor_tensor(pin[:, b, :], p[:, N_GATES:TAIL], row[:, N_GATES:TAIL], ALU.add)
                    ins.then_inc(proj_evac, 1)
                    if last_of[1] < i <= last_of[1] + NT:
                        o = og[:, i - last_of[1] - 1, :]
                        if i == last_of[1] + 1:
                            dve.wait_ge(sig_exp, 1)
                        st.link(nc.vector.tensor_scalar(o, o, 1.0, None, ALU.add))
                        st.link(nc.vector.reciprocal(o, o))
                        st.link(nc.vector.tensor_tensor(o, o, mln, ALU.mult))
        ar.at = start_h
        mix = ar.take([NT, D])
        ar.at = after_proj

        mark = ar.at
        band = ar.take([PG * 6, P])
        wp = ar.take([PG, PD])
        ps_row = ar.take([PW])
        pT = [ar.take([PG, P]) for _ in range(2)]
        att_low = ar.at
        ck, ckT, cv = ar.take([AW]), ar.take([3, P]), ar.take([AW])
        kc_nat = ar.take([AW])
        winmask = ar.take([TAB_SLOTS, GRID_W])
        tab = [ar.take([TAB_SLOTS, GRID_W])]
        att_high = ar.at
        att_in, tab_in = sem("att_in"), [sem("tab_in0"), sem("tab_in1")]

        def load_table(sp, h):
            for half in range(2):
                for s0, n, dr in ((0, EDGE_SLOTS, 1 - half), (EDGE_SLOTS, INNER_ROWS, 3 - half)):
                    src = bass.AP(rpb_rows.tensor, (h * RPB_R + dr) * GRID_W * PADW + GRID_W - 1,
                                  [[PADW - 1, GRID_W], [GRID_W * PADW, n], [1, GRID_W]])
                    sp.dma_start(tab[h % 2][GRID_W * half:GRID_W * (half + 1), s0:s0 + n, :], src).then_inc(tab_in[h % 2], 16)

        pool_in, pool_mm, pool_cp, pool_y, pool_out = (sem("pool_in"), sem("pool_mm"), sem("pool_cp"), sem("pool_y"), sem("pool_out"))

        def band_terms(t):
            if t == CTX_TILE:
                return [(t, 3)]
            terms = [(t, 1 if t == 0 else 2 if t == CTX_TILE - 1 else 0)]
            if t > 0:
                terms.append((t - 1, 4))
            if t < CTX_TILE - 1:
                terms.append((t + 1, 5))
            return terms

        with nc.Block() as block:
            @block.sync
            def _(sp):
                sp.dma_start(band, k_band).then_inc(pool_in, 16)
                sp.dma_start(wp[0:PD], w_pool.rearrange("g c e -> c g e")).then_inc(pool_in, 16)
                sp.dma_start(ps_row, bass.AP(pool_scale.tensor, 0, [[0, P], [1, PW]])).then_inc(pool_in, 16)
                sp.dma_start(ck, cache_k).then_inc(att_in, 16)
                sp.dma_start(cv, cache_v).then_inc(att_in, 16)
                sp.dma_start(winmask, k_winmask).then_inc(att_in, 16)
                load_table(sp, 0)

            @block.tensor
            def _(pe):
                pe.wait_ge(pool_in, 48)
                for t in range(NT + 1):
                    if t < NT:
                        if t >= 2:
                            pe.wait_ge(pool_cp, t - 1)
                        for g in range(PG):
                            terms = band_terms(t)
                            for n, (s, b) in enumerate(terms):
                                last = nc.tensor.matmul(bank(t % 2)[0:PD, g * P:(g + 1) * P], pin[:, s, g * PD:(g + 1) * PD],
                                                        band[:, g * 6 + b, :], start=(n == 0), stop=(n == len(terms) - 1))
                        last.then_inc(pool_mm, 1)
                    if t >= 1:
                        u = t - 1
                        pe.wait_ge(pool_cp, u + 1)
                        if u >= 2:
                            pe.wait_ge(pool_out, u - 1)
                        for g in range(PG):
                            last = nc.tensor.matmul(bank(2 + u % 2)[:, g * PD:(g + 1) * PD], pT[u % 2][0:PD, g, :],
                                                    wp[0:PD, g, :], start=True, stop=True)
                        last.then_inc(pool_y, 1)

            @block.scalar
            def _(act):
                for t in range(NT):
                    act.wait_ge(pool_mm, t + 1)
                    if t >= 2:
                        act.wait_ge(pool_y, t - 1)
                    nc.scalar.activation(pT[t % 2][0:PD], bank(t % 2)[0:PD].rearrange("p (g t) -> p g t", g=PG),
                                         ACT.Copy).then_inc(pool_cp, 1)

            @block.vector
            def _(dve):
                for t in range(NT):
                    dve.wait_ge(pool_y, t + 1)
                    nc.vector.tensor_tensor(mix[:, t, AW + MW:D], bank(2 + t % 2)[:, 0:PW], ps_row, ALU.mult).then_inc(pool_out, 1)
        ar.at = mark

        ar.at = after_attention_in
        SW_ = INNER_ROWS * GRID_W + P
        sc = [ar.take([SW_]) for _ in range(2)]
        ar.at = after_proj
        tab += [ar.take([TAB_SLOTS, GRID_W])]
        pr = [ar.take([SW_]) for _ in range(2)]
        pt = [ar.take([SW_ // P, P]) for _ in range(2)]
        assert ar.at <= att_low
        ar.at = att_high
        stat = ar.take([HEADS * NT, 4])
        LOCALS = {0: (0, 8, 6), 2: (0, 8, 4), 12: (8, 8, 2), 14: (8, 8, 0)}
        att = []
        for h in range(HEADS):
            for t in range(NT):
                if t == CTX_TILE:
                    att.append((h, t, None, 0, 0))
                elif 2 * t in LOCALS:
                    att.append((h, t) + LOCALS[2 * t])
                else:
                    att.append((h, t, 2 * t - 4, INNER_ROWS, EDGE_SLOTS))
        ck_turned, ck_ready, tab_ready = sem("ck_turned"), sem("ck_ready"), sem("tab_ready")
        s_mm, s_read, negmax, probs, p_turned, p_cp_act, p_cp_dve, pv_mm, att_out = (sem(n) for n in (
            "score_mm", "score_read", "negmax", "probs", "probs_turned", "pt_copied_act", "pt_copied_dve", "pv_mm", "att_out"))
        dve_att = sem("dve_att")
        with nc.Block() as block:
            @block.sync
            def _(sp):
                sp.dma_start(out_v, va[:, CTX_TILE, :]).then_inc(out_stored, 16)
                stored[0] += 16
                for h in range(HEADS):
                    if h >= 2:
                        sp.wait_ge(s_read, NT * (h - 1))
                    if h:
                        load_table(sp, h)
                    if h == 1:
                        sp.wait_ge(ck_ready, 2)
                        sp.dma_start(out_k, kc_nat).then_inc(out_stored, 16)
                        stored[0] += 16

            @block.gpsimd
            def _(pool):
                pool.wait_ge(att_in, 48)
                for h in range(HEADS):
                    pool.wait_ge(tab_in[h % 2], 64 * (h // 2 + 1))
                    nc.gpsimd.tensor_tensor(tab[h % 2], tab[h % 2], winmask, ALU.add).then_inc(tab_ready, 1)

            def keys(n):
                return n[3] * GRID_W

            def dve_copies(n):
                return n - n // NT

            @block.tensor
            def _(pe):
                pe.wait_ge(att_in, 48)
                for j in range(3):
                    last = nc.tensor.transpose(bank(0)[:, j * P:(j + 1) * P], ck[:, j * P:(j + 1) * P], ident)
                for j in range(3):
                    last = nc.tensor.transpose(bank(2)[:, j * P:(j + 1) * P], kaT[:, j, LAT:TOK], ident)
                last.then_inc(ck_turned, 1)
                pe.wait_ge(ck_ready, 2)

                def score(i):
                    h, t, r0, _, _ = att[i]
                    if i >= 2:
                        pe.wait_ge(s_read, i - 1)
                    q = qaT[:, h, t * P:(t + 1) * P]
                    base = 2 * (i % 2)
                    if r0 is None:
                        nc.tensor.matmul(bank(base)[:, 0:P], q, kaT[:, h // 2, LAT:TOK], start=True, stop=True).then_inc(s_mm, 1)
                        return
                    n = keys(att[i])
                    nc.tensor.matmul(bank(base), q, kaT[:, h // 2, r0 * GRID_W:r0 * GRID_W + BANK], start=True, stop=True)
                    if n > BANK:
                        nc.tensor.matmul(bank(base + 1)[:, 0:P], q, kaT[:, h // 2, r0 * GRID_W + BANK:r0 * GRID_W + n], start=True, stop=True)
                    nc.tensor.matmul(bank(base + 1)[:, n - BANK:n - BANK + P], q, ckT[:, h // 2, :], start=True, stop=True).then_inc(s_mm, 1)

                def turn(i):
                    pe.wait_ge(probs, i + 1)
                    if i >= 1:
                        pe.wait_ge(p_cp_act, i)
                        if dve_copies(i):
                            pe.wait_ge(p_cp_dve, dve_copies(i))
                    for j in range(keys(att[i]) // P + 1):
                        last = nc.tensor.transpose(ps[:, 4 * BANK + j * P:4 * BANK + (j + 1) * P],
                                                   pr[i % 2][:, j * P:(j + 1) * P], ident)
                    last.then_inc(p_turned, 1)

                def weigh(i):
                    h, t, r0, _, _ = att[i]
                    pe.wait_ge(p_cp_act, i + 1)
                    pe.wait_ge(p_cp_dve, dve_copies(i + 1))
                    if i >= 2:
                        pe.wait_ge(att_out, i - 1)
                    out = bank(6 + i % 2)[:, 0:HD]
                    cols = slice(h * HD, (h + 1) * HD)
                    n = keys(att[i]) // P
                    for j in range(n):
                        nc.tensor.matmul(out, pt[i % 2][:, j, :], va[:, r0 // 2 + j, cols], start=(j == 0), stop=False)
                    v = va[:, CTX_TILE, cols] if r0 is None else cv[:, cols]
                    nc.tensor.matmul(out, pt[i % 2][:, n, :], v, start=(n == 0), stop=True).then_inc(pv_mm, 1)

                score(0)
                for i in range(len(att)):
                    if i + 1 < len(att):
                        score(i + 1)
                    if i:
                        weigh(i - 1)
                    turn(i)
                weigh(len(att) - 1)

            @block.scalar
            def _(act):
                for i, u in enumerate(att):
                    n = keys(u)
                    act.wait_ge(negmax, i + 1)
                    if i >= 2:
                        act.wait_ge(p_turned, i - 1)
                    nc.scalar.activation(pr[i % 2][:, 0:n + P], sc[i % 2][:, 0:n + P], ACT.Exp, bias=stat[:, i, 1:2],
                                         accum_out=stat[:, i, 2:3]).then_inc(probs, 1)
                    act.wait_ge(p_turned, i + 1)
                    if i >= 2:
                        act.wait_ge(pv_mm, i - 1)
                    c = min(n // P + 1, 4)
                    nc.scalar.activation(pt[i % 2][:, 0:c, :], bank(4)[:, 0:c * P].rearrange("p (j t) -> p j t", j=c), ACT.Copy).then_inc(p_cp_act, 1)

            @block.vector
            def _(dve):
                st = Steps(dve, dve_att)
                dve.wait_ge(ck_turned, 1)
                nc.vector.tensor_copy(ckT, bank(0)[:, 0:3 * P].rearrange("p (j t) -> p j t", j=3)).then_inc(ck_ready, 1)
                nc.vector.tensor_copy(kc_nat, bank(2)[:, 0:3 * P]).then_inc(ck_ready, 1)

                def bias_and_max(i):
                    h, t, r0, nrows, slot = att[i]
                    n = keys(att[i])
                    if i % NT == 0:
                        dve.wait_ge(tab_ready, h + 1)
                    dve.wait_ge(s_mm, i + 1)
                    if i >= 2:
                        dve.wait_ge(probs, i - 1)
                    base = 2 * (i % 2) * BANK
                    m = stat[:, i, 0:1]
                    if n:
                        ins = nc.vector.tensor_tensor_reduce(
                            out=sc[i % 2][:, 0:n], in0=ps[:, base:base + n],
                            in1=tab[h % 2][:, slot:slot + nrows, :].rearrange("p s k -> p (s k)"), scale=1.0, scalar=-3e38,
                            op0=ALU.add, op1=ALU.max, accum_out=stat[:, i, 3:4])
                        st.link(ins)
                        nc.vector.tensor_scalar(sc[i % 2][:, n:n + P], ps[:, base + n:base + n + P], 0.0, stat[:, i, 3:4],
                                                ALU.add, ALU.max, accum_out=m).then_inc(s_read, 1)
                    else:
                        nc.vector.tensor_scalar(sc[i % 2][:, 0:P], ps[:, base:base + P], 0.0, None,
                                                ALU.add, ALU.max, accum_out=m).then_inc(s_read, 1)
                    dve.wait_ge(s_read, i + 1)
                    nc.vector.tensor_scalar(stat[:, i, 1:2], m, -1.0, None, ALU.mult).then_inc(negmax, 1)

                def copy_turned(i):
                    n = keys(att[i]) // P + 1
                    dve.wait_ge(p_turned, i + 1)
                    if i >= 2:
                        dve.wait_ge(pv_mm, i - 1)
                    if n > 4:
                        nc.vector.tensor_copy(pt[i % 2][:, 4:n, :], bank(5)[:, 0:(n - 4) * P].rearrange("p (j t) -> p j t", j=n - 4)).then_inc(p_cp_dve, 1)

                def normalise(i):
                    h, t = att[i][0:2]
                    dve.wait_ge(probs, i + 1)
                    st.link(nc.vector.reciprocal(stat[:, i, 3:4], stat[:, i, 2:3]))
                    dve.wait_ge(pv_mm, i + 1)
                    nc.vector.tensor_scalar(mix[:, t, h * HD:(h + 1) * HD], bank(6 + i % 2)[:, 0:HD], stat[:, i, 3:4], None, ALU.mult).then_inc(att_out, 1)

                bias_and_max(0)
                for i in range(len(att)):
                    if i + 1 < len(att):
                        bias_and_max(i + 1)
                    if i:
                        normalise(i - 1)
                    copy_turned(i)
                normalise(len(att) - 1)

        ar.at = after_mlstm_in
        cols = ar.take([NT, 4, 64])
        decay = ar.take([8, NT])
        selm = ar.take([8, P])
        r1 = ar.take([TOK])
        keep = ar.at
        ar_top = Arena(sb, ar.columns)
        ar_top.at = ar.columns - 8 * TOK - NT * MW
        ar.columns = ar_top.at
        giT, gfT, bT, mT, reset, w1, w2 = (ar.take([TOK]) for _ in range(7))
        sw = ar_top.take([8, NT, P])
        knat = ar_top.take([NT, MW])
        kq_mm, kq_cp, kn_turned, kn_cp = sem("kq_mm"), sem("kq_copied"), sem("k_turned"), sem("k_copied")
        m0, min_, r1e, ewe = ar.take([1]), ar.take([NT]), ar.take([NT]), ar.take([NT])
        g_in, g_turned, g_copied, f_abs, f_exp, a_rdy, e_rdy, ew_turned, dec_mm, ml_gates = (sem(n) for n in (
            "gate_in", "gate_turned", "gate_copied", "f_abs", "f_softplus", "exps_in", "exps_ready", "cols_turned", "decay_mm", "dve_gates"))
        act_g, r1_zeroed = sem("act_gates"), sem("r1_zeroed")
        FW, BW = slice(0, 32), slice(32, 64)
        with nc.Block() as block:
            @block.sync
            def _(sp):
                sp.dma_start(selm, k_sel).then_inc(g_in, 16)
                sp.dma_start(reset[0:64], k_reset).then_inc(g_in, 16)
                sp.wait_ge(ml_gates, 1)
                for way in range(2):
                    sp.dma_start(m0[32 * way:32 * way + MH], state_m[way, :, None]).then_inc(g_in, 16)
                sp.wait_ge(ml_gates, 8)
                sp.dma_start(out_m[0, :, None], mT[0:MH, TOK - 1:TOK]).then_inc(out_stored, 16)
                sp.dma_start(out_m[1, :, None], mT[32:32 + MH, LAT:LAT + 1]).then_inc(out_stored, 16)
                stored[0] += 32
                sp.wait_ge(out_stored, stored[0])

            @block.tensor
            def _(pe):
                for t in range(NT):
                    nc.tensor.transpose(ps[0:64, t * P:(t + 1) * P], gi[:, t, :], ident)
                    last = nc.tensor.transpose(ps[0:64, 4 * BANK + t * P:4 * BANK + (t + 1) * P], gf[:, t, :], ident)
                last.then_inc(g_turned, 1)
                pe.wait_ge(g_copied, 2)
                for h in range(MH):
                    if h >= 2:
                        pe.wait_ge(kq_cp, h - 1)
                    for t in range(NT):
                        at = 4 * (h % 2) * BANK + t * P
                        last = nc.tensor.matmul(ps[:, at:at + P], kbT[0:MD, h, t * P:(t + 1) * P], qbT[0:MD, h, t * P:(t + 1) * P],
                                                start=True, stop=True)
                    last.then_inc(kq_mm, 1)
                for t in range(NT):
                    if t >= 2:
                        pe.wait_ge(kn_cp, t - 1)
                    for h in range(MH):
                        last = nc.tensor.transpose(bank(3 + 4 * (t % 2))[:, h * MD:(h + 1) * MD], kbT[0:MD, h, t * P:(t + 1) * P], ident[0:MD, 0:MD])
                    last.then_inc(kn_turned, 1)
                pe.wait_ge(kq_cp, MH)
                pe.wait_ge(kn_cp, NT)
                pe.wait_ge(e_rdy, 3)
                pe.wait_ge(a_rdy, 2)
                pe.wait_ge(g_in, 64)
                for t in range(NT):
                    for n, src in enumerate((giT, w1, gfT, w2)):
                        last = nc.tensor.transpose(ps[:, (4 * t + n) * 64:(4 * t + n + 1) * 64], src[0:64, t * P:(t + 1) * P], ident[0:64, 0:64])
                last.then_inc(ew_turned, 1)
                for r in range(8):
                    last = nc.tensor.matmul(bank(6)[:, r * NT:(r + 1) * NT], selm[0:64, r, :], ewe[0:64], start=True, stop=True)
                last.then_inc(dec_mm, 1)

            @block.scalar
            def _(act):
                st = Steps(act, act_g)
                act.wait_ge(f_abs, 1)
                st.link(nc.scalar.activation(w1[0:64], w1[0:64], ACT.Exp, scale=-1.0))
                nc.scalar.activation(w1[0:64], w1[0:64], ACT.Ln, bias=1.0).then_inc(f_exp, 1)
                for h in range(MH):
                    act.wait_ge(kq_mm, h + 1)
                    nc.scalar.activation(sw[:, h], ps[:, 4 * (h % 2) * BANK:4 * (h % 2) * BANK + TOK].rearrange("p (c t) -> p c t", c=NT),
                                         ACT.Copy).then_inc(kq_cp, 1)
                for t in range(NT):
                    act.wait_ge(kn_turned, t + 1)
                    nc.scalar.activation(knat[:, t, :], bank(3 + 4 * (t % 2))[:, 0:MW], ACT.Copy).then_inc(kn_cp, 1)
                act.wait_ge(a_rdy, 1)
                nc.scalar.activation(w1[0:64], w1[0:64], ACT.Exp).then_inc(e_rdy, 1)
                nc.scalar.activation(w2[0:64], w2[0:64], ACT.Exp).then_inc(e_rdy, 1)
                nc.scalar.activation(gfT[0:64], mT[0:64], ACT.Exp, scale=-1.0).then_inc(e_rdy, 1)

            @block.vector
            def _(dve):
                st = Steps(dve, ml_gates)
                st.add(nc.vector.memset(m0[0:64], 0.0))
                nc.vector.memset(r1, 0.0).then_inc(r1_zeroed, 1)
                dve.wait_ge(g_turned, 1)
                nc.vector.tensor_copy(giT[0:64], ps[0:64, 0:TOK]).then_inc(g_copied, 1)
                nc.vector.tensor_copy(gfT[0:64], ps[0:64, 4 * BANK:4 * BANK + TOK]).then_inc(g_copied, 1)
                dve.wait_ge(g_copied, 2)
                nc.vector.scalar_tensor_tensor(out=w1[0:64], in0=gfT[0:64], scalar=-1.0, in1=gfT[0:64], op0=ALU.mult, op1=ALU.max).then_inc(f_abs, 1)
                dve.wait_ge(f_exp, 1)
                st.link(nc.vector.scalar_tensor_tensor(out=gfT[0:64], in0=gfT[0:64], scalar=0.0, in1=w1[0:64], op0=ALU.min, op1=ALU.subtract))
                dve.wait_ge(g_in, 64)
                st.add(nc.vector.tensor_tensor_scan(bT[FW], reset[FW], gfT[FW], 0.0, ALU.mult, ALU.add))
                st.add(nc.vector.tensor_tensor_scan(bT[BW][:, ::-1], reset[BW][:, ::-1], gfT[BW][:, ::-1], 0.0, ALU.mult, ALU.add))
                for seg, init in ((slice(0, LAT), True), (slice(LAT, TOK), False)):
                    for rows, way in ((FW, 0), (BW, 1)):
                        o, a, b = (x[rows, seg] for x in (mT, gfT, giT))
                        if way:
                            o, a, b = (x[:, ::-1] for x in (o, a, b))
                        st.add(nc.vector.tensor_tensor_scan(o, a, b, m0[rows, 0:1] if init else 0.0, ALU.add, ALU.max))
                st.settle()
                dve.wait_ge(r1_zeroed, 1)
                st.add(nc.vector.tensor_tensor(r1[0:64], bT[0:64], mT[0:64], ALU.subtract))
                st.add(nc.vector.memset(min_[0:64], 0.0))
                st.link(nc.vector.tensor_tensor(giT[0:64], giT[0:64], bT[0:64], ALU.subtract))
                v3 = lambda x, rows: x[rows].rearrange("p (c t) -> p c t", c=NT)
                st.add(nc.vector.tensor_copy(min_[FW, 0:1], m0[FW]))
                st.add(nc.vector.tensor_copy(min_[FW, 1:8], v3(mT, FW)[:, 0:7, P - 1]))
                st.add(nc.vector.tensor_copy(min_[BW, 7:8], m0[BW]))
                st.add(nc.vector.tensor_copy(min_[BW, 0:7], v3(mT, BW)[:, 1:8, 0]))
                st.add(nc.vector.tensor_copy(r1e[FW], v3(r1, FW)[:, :, P - 1]))
                st.link(nc.vector.tensor_copy(r1e[BW], v3(r1, BW)[:, :, 0]))
                A = slice(0, 64)
                st.add(nc.vector.tensor_tensor(v3(w1, A), v3(r1, A), bc(min_[A, :, None], (64, NT, P)), ALU.add))
                st.settle()
                nc.vector.tensor_tensor(v3(w2, A), v3(giT, A), bc(r1e[A, :, None], (64, NT, P)), ALU.add).then_inc(a_rdy, 1)
                dve.wait_ge(e_rdy, 3)
                st.add(nc.vector.tensor_copy(ewe[FW], v3(w1, FW)[:, :, P - 1]))
                st.settle()
                nc.vector.tensor_copy(ewe[BW], v3(w1, BW)[:, :, 0]).then_inc(a_rdy, 1)
                dve.wait_ge(ew_turned, 1)
                st.add(nc.vector.tensor_copy(cols, ps[:, 0:NT * 256].rearrange("p (t n r) -> p t n r", t=NT, n=4)))
                dve.wait_ge(dec_mm, 1)
                st.add(nc.vector.tensor_copy(decay, bank(6)[:, 0:8 * NT].rearrange("p (r t) -> p r t", r=8)))
        ar.at = keep

        keep_s = ar.at
        cs = ar.take([8, MA])
        c_in = sem("state_in")
        scanmask = ar.take([2, P])
        am = [ar.take([NT, P]) for _ in range(2)]
        ew = [ar.take([NT, P]) for _ in range(2)]
        sm_in, am_rdy, bc_mm, ew_add, ew_exp, sw_rdy = (sem(n) for n in (
            "scanmask_in", "a_masked", "weights_mm", "weights_added", "weights_exp", "sw_ready"))
        row_order = [MH * way + h for h in range(MH) for way in (1, 0)]

        def a_col(t, way, h0=0, n=1):
            return cols[:, t, 0, 32 * way + h0:32 * way + h0 + n]

        with nc.Block() as block:
            @block.sync
            def _(sp):
                sp.dma_start(scanmask, k_scanmask).then_inc(sm_in, 16)
                for way in range(2):
                    sp.dma_start(cs[0:MD, MH * way:MH * way + MH, 0:MD], state_C[way].rearrange("h d e -> d h e")).then_inc(c_in, 16)
                    sp.dma_start(cs[0:MD, MH * way:MH * way + MH, MD], state_n[way].rearrange("h d -> d h")).then_inc(c_in, 16)

            @block.gpsimd
            def _(pool):
                pool.wait_ge(sm_in, 16)
                for n, r in enumerate(row_order):
                    way, h = divmod(r, MH)
                    if n >= 2:
                        pool.wait_ge(ew_add, n - 1)
                    nc.gpsimd.tensor_tensor(am[n % 2], bc(scanmask[:, way:way + 1, :], (P, NT, P)),
                                            bc(cols[:, :, 0, 32 * way + h:32 * way + h + 1], (P, NT, P)), ALU.add).then_inc(am_rdy, 1)

            @block.tensor
            def _(pe):
                for n, r in enumerate(row_order):
                    if n >= 2:
                        pe.wait_ge(ew_add, n - 1)
                    for t0, tn in ((0, 512), (512, 512), (1024, 128)):
                        at = 4 * (n % 2) * BANK + t0
                        last = nc.tensor.matmul(ps[:, at:at + tn], selm[:, r, :], r1[:, t0:t0 + tn], start=True, stop=True)
                    last.then_inc(bc_mm, 1)

            @block.scalar
            def _(act):
                for n in range(8):
                    act.wait_ge(ew_add, n + 1)
                    nc.scalar.activation(ew[n % 2], ew[n % 2], ACT.Exp).then_inc(ew_exp, 1)

            @block.vector
            def _(dve):
                def add(n):
                    dve.wait_ge(bc_mm, n + 1)
                    dve.wait_ge(am_rdy, n + 1)
                    if n >= 2:
                        dve.wait_ge(sw_rdy, n - 1)
                    src = ps[:, 4 * (n % 2) * BANK:4 * (n % 2) * BANK + TOK].rearrange("p (c t) -> p c t", c=NT)
                    nc.vector.tensor_tensor(ew[n % 2], src, am[n % 2], ALU.add).then_inc(ew_add, 1)

                add(0)
                for n, r in enumerate(row_order):
                    if n + 1 < 8:
                        add(n + 1)
                    dve.wait_ge(ew_exp, n + 1)
                    if n:
                        dve.wait_ge(sw_rdy, n)
                    nc.vector.tensor_tensor(sw[:, r], ew[n % 2], sw[:, r % MH], ALU.mult).then_inc(sw_rdy, 1)
        ar.at = keep_s

        ar.at += 8 * MA
        cctx = ar.take([8, MA])
        hn = [ar.take([MH, MA]) for _ in range(2)]
        ct = ar.take([MH, MA])
        dn = ar.take([MH])
        KW_RING = 4
        kw = [ar.take([MW]) for _ in range(KW_RING)]
        sq = ar.take([MD])
        wo_at = max(ar.at + NT * MH * 3, mark_h + 2 * NT * D + 4 * D)
        assert wo_at + KD * BANK <= ar.columns
        wo = [sb[:, wo_at + n * KD * BANK:wo_at + (n + 1) * KD * BANK].rearrange("p (k n) -> p k n", k=KD) for n in range(2)]
        wo_src = w_out.rearrange("(k p) n -> p k n", p=P)
        wo_in = [sem("wo_in0"), sem("wo_in1")]
        ssb, tb = (ar.take([NT * MH]) for _ in range(2))
        sc_mm, sc_used, hb_mean, hb_guess, hb_sq, c_ctx_rdy, kw_rdy = (sem(n) for n in (
            "scan_mm", "scan_used", "hb_mean", "hb_guess", "hb_squares", "ctx_state_ready", "keys_weighted"))
        dve_scan, act_scan, num_rdy = sem("dve_scan"), sem("act_scan"), sem("numerators_ready")
        order = [(CTX_TILE, 0), (CTX_TILE, 1)]
        for c in range(8):
            order += [(c, 0), (7 - c, 1)]
        hb = mix[:, :, AW:AW + MW]

        def whole_after(t):
            return 1 + max(i for i, (u, _) in enumerate(order) if u == t)

        with nc.Block() as block:
            @block.sync
            def _(sp):
                sp.dma_start(wo[0], wo_src[:, :, 0:BANK]).then_inc(wo_in[0], 16)
                sp.wait_ge(c_ctx_rdy, 2)
                for way in range(2):
                    sp.dma_start(out_C[way].rearrange("h d e -> d h e"), cctx[0:MD, MH * way:MH * way + MH, 0:MD]).then_inc(out_stored, 16)
                    sp.dma_start(out_n[way].rearrange("h d -> d h"), cctx[0:MD, MH * way:MH * way + MH, MD]).then_inc(out_stored, 16)
                stored[0] += 64
                sp.wait_ge(out_stored, stored[0])

            @block.gpsimd
            def _(pool):
                for i, (t, way) in enumerate(order):
                    if i >= KW_RING:
                        pool.wait_ge(sc_mm, i - KW_RING + 1)
                    nc.gpsimd.tensor_tensor(kw[i % KW_RING].rearrange("p (h d) -> p h d", h=MH),
                                            knat[:, t, :].rearrange("p (h d) -> p h d", h=MH),
                                            bc(cols[:, t, 3, 32 * way:32 * way + MH][:, :, None], (P, MH, MD)), ALU.mult).then_inc(kw_rdy, 1)

            @block.tensor
            def _(pe):
                pe.wait_ge(c_in, 64)
                for i, (t, way) in enumerate(order):
                    pe.wait_ge(kw_rdy, i + 1)
                    b = 3 * (i % 2)
                    if i >= 2:
                        pe.wait_ge(sc_used, i - 1)
                    for h in range(MH):
                        nc.tensor.matmul(bank(b)[:, h * MA:(h + 1) * MA], sw[:, MH * way + h, t, :], vb[:, t, h, :], start=True, stop=True)
                    for h in range(MH):
                        last = nc.tensor.matmul(bank(b + 2)[0:MD, h * MA:(h + 1) * MA], kw[i % KW_RING][:, h * MD:(h + 1) * MD], vb[:, t, h, :], start=True, stop=True)
                    if t != CTX_TILE:
                        for h in range(MH):
                            last = nc.tensor.matmul(bank(b + 1)[:, h * MA:(h + 1) * MA], qbT[0:MD, h, t * P:(t + 1) * P], cs[0:MD, MH * way + h, :], start=True, stop=True)
                    last.then_inc(sc_mm, 1)

            @block.scalar
            def _(act):
                st = Steps(act, act_scan)

                def squares_of(t):
                    act.wait_ge(sc_used, whole_after(t))
                    for h in range(MH):
                        st.link(nc.scalar.activation(sq, hb[:, t, h * MD:(h + 1) * MD], ACT.Square, accum_out=ssb[:, MH * t + h:MH * t + h + 1]))

                for i, (t, way) in enumerate(order):
                    if t != CTX_TILE:
                        act.wait_ge(sc_mm, i + 1)
                        act.wait_ge(sc_used, i - 1)
                        for h in range(MH):
                            ins = nc.scalar.activation(hn[i % 2][:, h, :], bank(3 * (i % 2) + 1)[:, h * MA:(h + 1) * MA], ACT.Copy,
                                                       scale=cols[:, t, 1, 32 * way + h:32 * way + h + 1])
                        ins.then_inc(num_rdy, 1)
                    for u in range(NT):
                        if whole_after(u) == i:
                            squares_of(u)
                for u in range(NT):
                    if whole_after(u) >= len(order):
                        squares_of(u)
                nc.scalar.activation(sq[:, 0:1], ssb[:, 0:1], ACT.Square).then_inc(hb_sq, 1)
                act.wait_ge(hb_mean, 1)
                nc.scalar.activation(ysb, ssb, ACT.Sqrt).then_inc(hb_guess, 1)

            @block.vector
            def _(dve):
                st = Steps(dve, dve_scan)
                dve.wait_ge(c_in, 64)
                p4 = lambda n, rows=P: bank(n)[0:rows, 0:MH * MA].rearrange("p (h e) -> p h e", h=MH)
                for i, (t, way) in enumerate(order):
                    b = 3 * (i % 2)
                    hs = slice(MH * way, MH * way + MH)
                    dve.wait_ge(sc_mm, i + 1)
                    num = hn[i % 2]
                    w = lambda n: cols[:, t, n, 32 * way:32 * way + MH]
                    if t == CTX_TILE:
                        nc.vector.tensor_copy(cctx[0:MD, hs, :], p4(b + 2, MD)).then_inc(c_ctx_rdy, 1)
                        st.link(nc.vector.tensor_copy(num, p4(b)))
                    else:
                        st.link(nc.vector.tensor_tensor(ct[0:MD], cs[0:MD, hs, :], bc(decay[0:MD, hs, t:t + 1], (MD, MH, MA)), ALU.mult))
                        st.add(nc.vector.tensor_tensor(cs[0:MD, hs, :], ct[0:MD], p4(b + 2, MD), ALU.add))
                        dve.wait_ge(num_rdy, i - 1)
                        st.link(nc.vector.tensor_tensor(num, num, p4(b), ALU.add))
                    st.link(nc.vector.scalar_tensor_tensor(out=dn[:, :, None], in0=num[:, :, MD:MA], scalar=-1.0, in1=num[:, :, MD:MA], op0=ALU.mult, op1=ALU.max))
                    st.link(nc.vector.tensor_tensor(dn, dn, w(2), ALU.max))
                    st.link(nc.vector.reciprocal(dn, dn))
                    dst = hb[:, t, :].rearrange("p (h d) -> p h d", h=MH)
                    first = (way == 0 and t <= 3) or (way == 1 and 4 <= t < 8) or (way == 0 and t == CTX_TILE)
                    if first:
                        nc.vector.tensor_tensor(dst, num[:, :, 0:MD], bc(dn[:, :, None], (P, MH, MD)), ALU.mult).then_inc(sc_used, 1)
                    else:
                        st.link(nc.vector.tensor_tensor(num[:, :, 0:MD], num[:, :, 0:MD], bc(dn[:, :, None], (P, MH, MD)), ALU.mult))
                        nc.vector.tensor_tensor(dst, dst, num[:, :, 0:MD], ALU.add).then_inc(sc_used, 1)
                dve.wait_ge(sc_used, len(order))
                dve.wait_ge(hb_sq, 1)
                nc.vector.tensor_scalar(ssb, ssb, 1.0 / MD, EPS, ALU.mult, ALU.add).then_inc(hb_mean, 1)
                dve.wait_ge(hb_guess, 1)
                newton(st, ysb, tb, ssb)
        ar.at = mark_h
        ar.columns = SB_COLUMNS - NT * MW

        x1 = ar.take([NT, D])
        h2 = ar.take([NT, D])
        after_x1 = ar.at
        n2_rows = (ar.take([2, D]), ar.take([2, D]))
        after_rows = ar.at
        ar.at = wo_at + 2 * KD * BANK
        g1 = ar.take([2, D])
        mt = [ar.take([KD, P]) for _ in range(2)]
        o_in, ox_in, o_turned, o_cp, o_mm, o_add = (sem(n) for n in ("g1_in", "ox_in", "mix_turned", "mix_copied", "out_mm", "out_add"))
        mix_rdy = sem("mix_ready")
        dve_o, act_o = sem("dve_out"), sem("act_out")
        sq_junk = ar.take([D])
        n2_rows_in = sem("n2_rows_in")
        sq2, mean2, guess2 = sem("n2_squares"), sem("n2_mean"), sem("n2_guess")
        with nc.Block() as block:
            @block.sync
            def _(sp):
                sp.dma_start(wo[1], wo_src[:, :, BANK:2 * BANK]).then_inc(wo_in[1], 16)
                sp.dma_start(g1, mod_row(2)).then_inc(o_in, 16)
                sp.wait_ge(wo_in[1], 16)
                for t in range(NT):
                    sp.dma_start(x1[:, t, :], x_all[t * P:(t + 1) * P, :]).then_inc(ox_in, 16)
                load_rows_of(n2_rows, (3, 4), sp, n2_rows_in)

            @block.tensor
            def _(pe):
                def turn(t):
                    if t >= 2:
                        pe.wait_ge(o_cp, t - 1)
                    pe.wait_ge(mix_rdy, t + 1)
                    for k in range(KD):
                        at = 2 * (t % 2) * BANK + k * P
                        last = nc.tensor.transpose(ps[:, at:at + P], mix[:, t, k * P:(k + 1) * P], ident)
                    last.then_inc(o_turned, 1)

                turn(0)
                for t in range(NT):
                    if t + 1 < NT:
                        turn(t + 1)
                    pe.wait_ge(o_cp, t + 1)
                    if t >= 2:
                        pe.wait_ge(o_add, 2 * (t - 1))
                    for half in range(2):
                        if t == 0:
                            pe.wait_ge(wo_in[half], 16)
                        for k in range(KD):
                            last = nc.tensor.matmul(bank(4 + 2 * (t % 2) + half), mt[t % 2][:, k, :], wo[half][:, k, :],
                                                    start=(k == 0), stop=(k == KD - 1))
                    last.then_inc(o_mm, 1)

            @block.scalar
            def _(act):
                st = Steps(act, act_o)

                def square(t):
                    act.wait_ge(o_add, 2 * (t + 1))
                    if t:
                        st.settle()
                    st.add(nc.scalar.activation(sq_junk, x1[:, t, :], ACT.Square, accum_out=ss2[:, t:t + 1]))

                for t in range(NT):
                    act.wait_ge(o_turned, t + 1)
                    if t >= 2:
                        act.wait_ge(o_mm, t - 1)
                    for half in range(2):
                        ins = nc.scalar.activation(mt[t % 2][:, 4 * half:4 * half + 4, :], bank(2 * (t % 2) + half).rearrange("p (k t) -> p k t", k=4), ACT.Copy)
                    ins.then_inc(o_cp, 1)
                    if t:
                        square(t - 1)
                square(NT - 1)
                st.settle()
                nc.scalar.activation(sq_junk[:, 0:1], ss2[:, 0:1], ACT.Square).then_inc(sq2, 1)
                act.wait_ge(mean2, 1)
                nc.scalar.activation(y2, ss2, ACT.Sqrt).then_inc(guess2, 1)

            @block.vector
            def _(dve):
                st = Steps(dve, dve_o)

                def norm_gate(t):
                    h4 = hb[:, t, :].rearrange("p (h d) -> p h d", h=MH)
                    st.link(nc.vector.tensor_tensor(h4, h4, bc(ysb[:, MH * t:MH * t + MH][:, :, None], (P, MH, MD)), ALU.mult))
                    nc.vector.tensor_tensor(hb[:, t, :], hb[:, t, :], og[:, t, :], ALU.mult).then_inc(mix_rdy, 1)

                norm_gate(0)
                norm_gate(1)
                dve.wait_ge(o_in, 16)
                dve.wait_ge(ox_in, 16 * NT)
                for t in range(NT):
                    if t + 2 < NT:
                        norm_gate(t + 2)
                    dve.wait_ge(o_mm, t + 1)
                    for half in range(2):
                        hs = slice(half * BANK, (half + 1) * BANK)
                        st.link(nc.vector.tensor_tensor(h2[:, t, hs], bank(4 + 2 * (t % 2) + half), g1[:, side(t), hs], ALU.mult))
                        nc.vector.tensor_tensor(x1[:, t, hs], x1[:, t, hs], h2[:, t, hs], ALU.add).then_inc(o_add, 1)
                dve.wait_ge(sq2, 1)
                nc.vector.tensor_scalar(ss2, ss2, 1.0 / D, EPS, ALU.mult, ALU.add).then_inc(mean2, 1)
                dve.wait_ge(guess2, 1)
                newton(st, y2, t2, ss2)
        ar.at = after_rows
        
        h2T = mix.rearrange("p t d -> p (t d)").rearrange("p (k t) -> p k t", k=KD)
        wr = ar.take([KD, NE])
        lgT = ar.take([TOK])
        lgT_mm, lgT_cp = sem("logits_mm"), sem("logits_copied")

        def router_dve(dve):
            for n, (t0, t1) in enumerate(((0, 4), (4, 8), (8, 9))):
                dve.wait_ge(lgT_mm, n + 1)
                nc.vector.tensor_copy(lgT[0:NE, t0 * P:t1 * P], bank((2, 3, 6)[n])[0:NE, 0:(t1 - t0) * P]).then_inc(lgT_cp, 1)

        upper, ones = ar.take([P]), ar.take([P])
        brr, cids, tok_f, tok_ids = ar.take([NE]), ar.take([CHUNKS]), ar.take([NT]), ar.take([NT]).bitcast(I32)
        r_in = sem("router_in")
        router_mark = ar.at
        wr_in, r_mm, moe_w = sem("router_weights_in"), sem("router_mm"), SB_COLUMNS - 2 * 3 * KD * DF
        assert moe_w + 3 * KD * DF >= ar.at + 4 * D
        half_cols = 3 * KD * DF
        halves = sb[:, moe_w:moe_w + 2 * half_cols].rearrange("p (s n) -> p s n", s=2)
        w_even, w_odd = halves[:, 1, :], halves[:, 0, :]
        gu_ld, d_ld = [sem(f"gate_up_in{s}") for s in range(2)], [sem(f"down_in{s}") for s in range(2)]

        def load_gate_up(sp, dst, e, s):
            for n, w in enumerate((w_gate, w_up)):
                sp.dma_start(dst[:, n * KD * DF:(n + 1) * KD * DF].rearrange("p (k f) -> p k f", k=KD),
                             w[e].rearrange("(k p) n -> p k n", p=P)).then_inc(gu_ld[s], 16)

        def load_down(sp, dst, e, s):
            for n in range(2):
                sp.dma_start(dst[:, (2 * KD + n * KD // 2) * DF:(2 * KD + (n + 1) * KD // 2) * DF].rearrange("p (k f) -> p k f", k=KF // 2),
                             w_down[e].rearrange("(k p) n -> p k n", p=P)[:, n * KF // 2:(n + 1) * KF // 2]).then_inc(d_ld[s], 16)

        def router_sp(sp):
            sp.dma_start(upper, k_upper).then_inc(r_in, 16)
            sp.dma_start(brr, bass.AP(b_router.tensor, 0, [[0, P], [1, NE]])).then_inc(r_in, 16)
            sp.dma_start(cids, bass.AP(k_chunk_ids.tensor, 0, [[0, P], [1, CHUNKS]])).then_inc(r_in, 16)
            sp.dma_start(tok_f, k_token_ids).then_inc(r_in, 16)
            sp.dma_start(w_odd[:, half_cols - 8:half_cols - 4], k_ident[:, 0:4]).then_inc(gu_ld[1], 16)
            sp.dma_start(w_odd[:, half_cols - 4:half_cols], k_ident[:, 0:4]).then_inc(d_ld[1], 16)
            sp.dma_start(wr, w_router.rearrange("(k p) n -> p k n", p=P)).then_inc(wr_in, 16)
            load_gate_up(sp, w_even, 0, 0)
            load_down(sp, w_even, 0, 0)
            sp.wait_ge(gu_ld[1], 16)
            sp.wait_ge(d_ld[1], 16)

        def router_pe(pe, t, copied):
            if t == 0:
                pe.wait_ge(wr_in, 16)
            for t0, t1 in ((0, 4), (4, 8), (8, 9)):
                if t == min(t1, NT - 1):
                    pe.wait_ge(copied, t1)
                    n = (t1 - t0) * P
                    for k in range(KD):
                        last = nc.tensor.matmul(bank((2, 3, 6)[t0 // 4])[0:NE, 0:n], wr[:, k, :],
                                                h2T[:, k, t0 * P:t1 * P], start=(k == 0), stop=(k == KD - 1))
                    last.then_inc(lgT_mm, 1)
            if t == NT - 1:
                pe.wait_ge(lgT_cp, 3)
                for u in range(NT):
                    last = nc.tensor.transpose(bank(7)[:, u * NE:(u + 1) * NE], lgT[0:NE, u * P:(u + 1) * P], ident[0:NE, 0:NE])
                last.then_inc(r_mm, 1)

        h2_stored = sem("h2_stored")

        def store_h2(pool, nat_ready):
            for t in range(NT):
                pool.wait_ge(nat_ready, t + 1)
                pool.dma_start(h2_rows[t * P:(t + 1) * P, :], h2[:, t, :]).then_inc(h2_stored, 16)

        norm_stage("n2_", x1, y2, (3, 4), h2, h2T, router_sp, router_pe, dve_last=router_dve, pool_more=store_h2,
                   rows=(n2_rows, n2_rows_in))
        ar.at = router_mark

        NEt = NT * NE
        lg, sco, sel, cmpb = ar.take([NEt]), ar.take([NEt]), ar.take([NEt]), ar.take([NEt * EPG])
        rank, oh1, oh2, tmp, both, sl = (ar.take([NEt]) for _ in range(6))
        gs, gr = ar.take([NT * EG]), ar.take([NT * EG])
        gcmp = ar.take([NT * EG * EG])
        base_ = ar.take([NT, NE])
        tot = ar.take([NT, NE])
        cnt, ntl, cum, off = (ar.take([NE]) for _ in range(4))
        s12, rden = ar.take([3, NT]), ar.take([NT])
        nch, cumch, start_ch, tile_base, pair_base = (ar.take([NE]) for _ in range(5))
        ended, begun, picked = (ar.take([CHUNKS, NE]) for _ in range(3))
        cf, ef, valid = (ar.take([CHUNKS]) for _ in range(3))
        assert ar.at <= moe_w + half_cols
        r_exp, both_rdy, pos_mm, slot_rdy, scattered, dve_r = (sem(n) for n in (
            "router_exp", "picked", "position_mm", "slot_ready", "scattered", "dve_router"))
        with nc.Block() as block:
            @block.tensor
            def _(pe):
                pe.wait_ge(r_in, 64)
                pe.wait_ge(both_rdy, 1)
                nc.tensor.matmul(bank(1)[:, 0:NEt], upper, both, start=True, stop=True)
                nc.tensor.matmul(bank(3)[:, 0:NEt], ones, both, start=True, stop=True).then_inc(pos_mm, 1)

            @block.scalar
            def _(act):
                act.wait_ge(r_mm, 1)
                nc.scalar.activation(lg, bank(7)[:, 0:NEt], ACT.Exp, scale=-1.0).then_inc(r_exp, 1)

            @block.gpsimd
            def _(pool):
                pool.wait_ge(slot_rdy, 1)
                for t in range(NT):
                    for n in range(2):
                        pool.indirect_dma_start(slot_token, bass.IndirectOffsetOnAxis(slot[n].bitcast(U32)[:, t:t + 1], 0),
                                                tok_ids[:, t:t + 1], None).then_inc(scattered, 16)
                pool.wait_ge(scattered, 16 * 2 * NT)
                pool.wait_ge(h2_stored, 16 * NT)

            @block.vector
            def _(dve):
                st = Steps(dve, dve_r)
                v = nc.vector
                st.add(v.memset(ones, 1.0))
                st.add(v.memset(cmpb, 0.0))
                st.add(v.memset(gcmp, 0.0))
                st.add(v.memset(base_, 0.0))
                dve.wait_ge(r_in, 64)
                dve.wait_ge(r_exp, 1)
                st.link(v.tensor_scalar(lg, lg, 1.0, None, ALU.add))
                st.link(v.reciprocal(sco, lg))
                st.link(v.tensor_tensor(sel.rearrange("p (t e) -> p t e", t=NT), sco.rearrange("p (t e) -> p t e", t=NT),
                                        bc(brr[:, None, :], (P, NT, NE)), ALU.add))

                def ranks(src, cmp, out, n):
                    s4 = src.rearrange("p (n e) -> p n e", e=4)
                    c4 = cmp.rearrange("p (n e f) -> p n e f", e=4, f=4)
                    for f in range(4):
                        if f < 3:
                            st.add(v.tensor_tensor(c4[:, :, f + 1:4, f], bc(s4[:, :, f:f + 1], (P, n, 3 - f)), s4[:, :, f + 1:4], ALU.is_ge))
                        if f > 0:
                            st.add(v.tensor_tensor(c4[:, :, 0:f, f], bc(s4[:, :, f:f + 1], (P, n, f)), s4[:, :, 0:f], ALU.is_gt))
                    st.settle()
                    st.link(v.tensor_reduce(out.rearrange("p (n e) -> p n e", e=4), c4, AX.X, ALU.add))

                ranks(sel, cmpb, rank, NT * EG)
                st.add(v.tensor_scalar(oh1, rank, 0.0, None, ALU.is_equal))
                st.add(v.tensor_scalar(oh2, rank, 1.0, None, ALU.is_equal))
                st.link(v.scalar_tensor_tensor(out=tmp, in0=rank, scalar=2.0, in1=sel, op0=ALU.is_lt, op1=ALU.mult))
                st.link(v.tensor_reduce(gs, tmp.rearrange("p (n e) -> p n e", e=EPG), AX.X, ALU.add))
                ranks(gs, gcmp, gr, NT)
                st.link(v.tensor_scalar(gs, gr, 0.0, None, ALU.is_equal))
                g4 = bc(gs[:, :, None], (P, NT * EG, EPG))
                for oh in (oh1, oh2):
                    o4 = oh.rearrange("p (n e) -> p n e", e=EPG)
                    st.add(v.tensor_tensor(o4, o4, g4, ALU.mult))
                st.settle()
                v.tensor_tensor(both, oh1, oh2, ALU.add).then_inc(both_rdy, 1)
                dve.wait_ge(pos_mm, 1)
                st.link(v.tensor_copy(tot, bank(3)[:, 0:NEt].rearrange("p (t e) -> p t e", t=NT)))
                for t in range(1, NT):
                    st.link(v.tensor_tensor(base_[:, t, :], base_[:, t - 1, :], tot[:, t - 1, :], ALU.add))
                st.link(v.tensor_tensor(cnt, base_[:, NT - 1, :], tot[:, NT - 1, :], ALU.add))
                st.link(v.tensor_scalar(ntl, cnt, 0.0, None, ALU.is_gt))
                for k in range(1, NT):
                    st.link(v.scalar_tensor_tensor(out=ntl, in0=cnt, scalar=float(P * k), in1=ntl, op0=ALU.is_gt, op1=ALU.add))
                st.link(v.tensor_tensor_scan(cum, ones[:, 0:NE], ntl, 0.0, ALU.mult, ALU.add))
                st.link(v.tensor_tensor(off, cum, ntl, ALU.subtract))
                st.link(v.tensor_scalar(off, off, float(P), None, ALU.mult))
                s3 = sl.rearrange("p (t e) -> p t e", t=NT)
                st.link(v.tensor_tensor(s3, base_, bc(off[:, None, :], (P, NT, NE)), ALU.add))
                st.link(v.tensor_tensor(sl, sl, bank(1)[:, 0:NEt], ALU.add))
                st.add(v.tensor_copy(tok_ids, tok_f))
                for n, oh in enumerate((oh1, oh2)):
                    st.link(v.tensor_tensor(tmp, sl, oh, ALU.mult))
                    st.link(v.tensor_reduce(s12[:, 2, :], tmp.rearrange("p (t e) -> p t e", t=NT), AX.X, ALU.add))
                    st.link(v.tensor_copy(slot[n].bitcast(U32), s12[:, 2, :]))
                nc.vector.memset(ones[:, 0:1], 1.0).then_inc(slot_rdy, 1)
                for n, oh in enumerate((oh1, oh2)):
                    st.link(v.tensor_tensor(tmp, sco, oh, ALU.mult))
                    st.link(v.tensor_reduce(s12[:, n, :], tmp.rearrange("p (t e) -> p t e", t=NT), AX.X, ALU.add))
                st.link(v.tensor_tensor(rden, s12[:, 0, :], s12[:, 1, :], ALU.add))
                st.link(v.reciprocal(rden, rden))
                for n in range(2):
                    st.add(v.tensor_tensor(gate[n], s12[:, n, :], rden, ALU.mult))
                st.link(v.tensor_scalar(nch, cnt, 0.0, None, ALU.is_gt))
                for k in range(1, (TOK + CHUNK - 1) // CHUNK):
                    st.link(v.scalar_tensor_tensor(out=nch, in0=cnt, scalar=float(CHUNK * k), in1=nch, op0=ALU.is_gt, op1=ALU.add))
                dve.wait_ge(slot_rdy, 1)
                st.link(v.tensor_tensor_scan(cumch, ones[:, 0:NE], nch, 0.0, ALU.mult, ALU.add))
                st.link(v.tensor_tensor(start_ch, cumch, nch, ALU.subtract))
                st.link(v.tensor_scalar(tile_base, off, 1.0 / P, None, ALU.mult))
                st.link(v.scalar_tensor_tensor(out=tile_base, in0=start_ch, scalar=-2.0, in1=tile_base, op0=ALU.mult, op1=ALU.add))
                st.link(v.scalar_tensor_tensor(out=pair_base, in0=start_ch, scalar=float(CHUNK), in1=cnt, op0=ALU.mult, op1=ALU.add))
                ce3 = lambda a: bc(a[:, None, :], (P, CHUNKS, NE))
                ids3 = bc(cids[:, :, None], (P, CHUNKS, NE))
                st.add(v.tensor_tensor(ended, ce3(cumch), ids3, ALU.is_le))
                st.link(v.tensor_tensor(begun, ce3(start_ch), ids3, ALU.is_le))
                st.link(v.tensor_tensor(begun, begun, ended, ALU.subtract))
                st.link(v.tensor_reduce(ef, ended, AX.X, ALU.add))
                st.link(v.tensor_scalar(ef, ef, float(NE - 1), None, ALU.min))
                st.link(v.tensor_reduce(valid, begun, AX.X, ALU.add))
                st.link(v.tensor_tensor(valid, valid, cids, ALU.mult))
                for base, slope, out in ((tile_base, 2.0, tile_of), (pair_base, -float(CHUNK), code_of)):
                    st.link(v.tensor_tensor(picked, begun, ce3(base), ALU.mult))
                    st.link(v.tensor_reduce(cf, picked, AX.X, ALU.add))
                    st.link(v.scalar_tensor_tensor(out=cf, in0=valid, scalar=slope, in1=cf, op0=ALU.mult, op1=ALU.add))
                    if out is code_of:
                        st.link(v.scalar_tensor_tensor(out=cf, in0=ef, scalar=float(CODE), in1=cf, op0=ALU.mult, op1=ALU.add))
                    st.link(v.tensor_copy(out, cf))
                st.add(v.tensor_copy(n_chunks, cumch[:, NE - 1:NE]))
                st.add(v.tensor_copy(last_chunk, cumch))
                st.link(v.memset(ps[:, :], 0.0))
        ar.at = after_x1 - NT * D

        ar.at = start_h
        xs = [ar.take([D]) for _ in range(2)]
        xT = ar.take([KD, CHUNK])
        ge = [ar.take([CHUNK]) for _ in range(2)]
        hidT = ar.take([KF, CHUNK])
        yT = ar.take([KD, CHUNK])
        assert ar.at <= mark_h
        ar.at = mark_h + NT * D
        g2 = ar.take([2, D])
        fn = ar.take([D])
        f_in = sem("final_in")
        yo = [ar.take([D]) for _ in range(2)]
        row_ids = ar.take([2]).bitcast(I32)
        assert ar.at <= moe_w
        x_ld, ids_ld = sem("rows_in"), sem("row_ids_in")
        x_turned, x_cp, gu_mm, g_exp, g_dve, hid_rdy, dn_mm, yT_cp, y_turned = (sem(n) for n in (
            "rows_turned", "rows_copied", "gate_up_mm", "gate_exp", "dve_experts", "hid_ready", "down_mm", "out_copied", "out_turned"))
        y_rdy = [sem(f"y_ready{s}") for s in range(2)]
        y_st = [sem(f"y_stored{s}") for s in range(2)]

        def over_chunks(engine, turn):
            used = engine.value_load(n_chunks[0:1, 0:1], min_val=MIN_CHUNKS, max_val=MAX_CHUNKS)
            turn(0, True)
            with engine.Fori(1, MAX_CHUNKS) as i:
                with engine.If(i < used):
                    turn(i, False)
                with engine.Else():
                    engine.nop()
            return used

        with nc.Block() as block:
            @block.sync
            def _(sp):
                sp.wait_ge(x_turned, 1)
                load_gate_up(sp, w_odd, 1, 1)
                load_down(sp, w_odd, 1, 1)
                sp.dma_start(g2, mod_row(5)).then_inc(f_in, 16)
                sp.dma_start(fn, bass.AP(final_norm.tensor, 0, [[0, P], [1, D]])).then_inc(f_in, 16)
                with sp.Fori(1, NE // 2) as i:
                    for s, dst in enumerate((w_even, w_odd)):
                        e = 2 * i + s
                        done = sp.value_load(last_chunk[0:1, bass.ds(e - 2, 1)], min_val=0, max_val=MAX_CHUNKS)
                        sp.wait_ge(gu_ld[s], 32 * i + 16 * s)
                        sp.wait_ge(d_ld[s], 32 * i + 16 * s)
                        sp.wait_ge(gu_mm, 4 * done + 1)
                        load_gate_up(sp, dst, e, s)
                        sp.wait_ge(dn_mm, 4 * done + 1)
                        load_down(sp, dst, e, s)
                for s in range(2):
                    sp.wait_ge(gu_ld[s], 16 * NE + 16 * s)
                    sp.wait_ge(d_ld[s], 16 * NE + 16 * s)

            @block.gpsimd
            def _(pool):
                def load_ids(i, tile):
                    for s in range(2):
                        pool.dma_start(row_ids[:, s:s + 1], slot_token[bass.ds((tile + s) * P, P), :]).then_inc(ids_ld, 16)
                    pool.wait_ge(ids_ld, 32 * i + 32)

                def load_rows():
                    for s in range(2):
                        pool.indirect_dma_start(xs[s], None, h2_rows, bass.IndirectOffsetOnAxis(row_ids[:, s:s + 1].bitcast(U32), 0)).then_inc(x_ld, 16)

                def store_y(n, tile):
                    for s in range(2):
                        pool.wait_ge(y_rdy[s], n)
                        pool.dma_start(slot_y[bass.ds((tile + s) * P, P), :], yo[s]).then_inc(y_st[s], 16)

                def tile_at(i):
                    return pool.value_load(tile_of[0:1, bass.ds(i, 1)], min_val=0, max_val=N_SLOT_TILES - 2)

                def turn(i, first):
                    if not first:
                        tile = tile_at(i - 1)
                    next_tile = tile_at(i + 1)
                    pool.wait_ge(x_turned, i + 1)
                    load_ids(i + 1, next_tile)
                    if not first:
                        store_y(i, tile)
                    load_rows()

                load_ids(0, tile_at(0))
                load_rows()
                used = over_chunks(pool, turn)
                store_y(used, tile_at(used - 1))
                for s in range(2):
                    pool.wait_ge(y_st[s], used * 16)
                pool.wait_ge(x_ld, used * 32 + 32)

            @block.tensor
            def _(pe):
                def turn_x(i, first):
                    pe.wait_ge(x_ld, 32 * i + 32)
                    if not first:
                        for s in range(2):
                            pe.wait_ge(y_rdy[s], i - 1)
                    for s in range(2):
                        for k in range(KD):
                            last = nc.tensor.transpose(ps[:, (4 + 2 * s) * BANK + k * P:(4 + 2 * s) * BANK + (k + 1) * P],
                                                       xs[s][:, k * P:(k + 1) * P], ident)
                    last.then_inc(x_turned, 1)

                def chunk(i, first, w, cols_n, n_even, n_odd):
                    pe.wait_ge(gu_ld[0], n_even * 32)
                    pe.wait_ge(gu_ld[1], n_odd * 32 + 16)
                    pe.wait_ge(x_cp, 2 * i + 2)
                    for f in range(KF):
                        if not (first and f < 2):
                            pe.wait_ge(hid_rdy, 4 * i + f - 1)
                        for n in range(2):
                            for k in range(KD):
                                at = (n * KD + k) * DF + f * P
                                last = nc.tensor.matmul(bank(f % 2)[:, n * CHUNK:n * CHUNK + cols_n], w[:, at:at + P], xT[:, k, 0:cols_n],
                                                        start=(k == 0), stop=(k == KD - 1))
                        last.then_inc(gu_mm, 1)
                    turn_x(i + 1, first)
                    pe.wait_ge(d_ld[0], n_even * 32)
                    pe.wait_ge(d_ld[1], n_odd * 32 + 16)
                    pe.wait_ge(hid_rdy, 4 * i + KF - 1)

                    def down(d, ks):
                        for k in ks:
                            at = 2 * KD * DF + k * D + d * P
                            last = nc.tensor.matmul(bank(2 + d // 2 % 2)[:, (d % 2) * CHUNK:(d % 2) * CHUNK + cols_n], w[:, at:at + P],
                                                    hidT[:, k, 0:cols_n], start=(k == 0), stop=(k == KF - 1))
                        return last

                    for d in (0, 2):
                        if not first:
                            pe.wait_ge(yT_cp, 4 * i + d // 2 - 1)
                        down(d, range(KF - 1))
                    pe.wait_ge(hid_rdy, 4 * i + KF)
                    for d in (0, 2):
                        down(d, (KF - 1,))
                    for d in range(KD):
                        if d in (4, 6):
                            pe.wait_ge(yT_cp, 4 * i + d // 2 - 1)
                        if d not in (0, 2):
                            last = down(d, range(KF))
                        if d % 2:
                            last.then_inc(dn_mm, 1)
                    pe.wait_ge(x_cp, 2 * i + 4)
                    for s in range(2 if cols_n > P else 1):
                        for d in range(KD):
                            if s == 0 and d in (0, 6):
                                pe.wait_ge(yT_cp, 4 * i + 3 + d // 6)
                            last = nc.tensor.transpose(ps[:, (4 + 2 * s) * BANK + d * P:(4 + 2 * s) * BANK + (d + 1) * P],
                                                       yT[:, d, s * P:(s + 1) * P], ident)
                        last.then_inc(y_turned, 1 if cols_n > P else 2)

                def by_width(i, first, w, pairs, n_even, n_odd, widths):
                    if len(widths) == 1:
                        chunk(i, first, w, widths[0], n_even, n_odd)
                        return
                    half = len(widths) // 2
                    with pe.If(pairs < widths[half - 1] + 1):
                        by_width(i, first, w, pairs, n_even, n_odd, widths[:half])
                    with pe.Else():
                        by_width(i, first, w, pairs, n_even, n_odd, widths[half:])

                def turn(i, first):
                    code = pe.value_load(code_of[0:1, bass.ds(i, 1)], min_val=0, max_val=NE * CODE - 1)
                    e, pairs = code // CODE, code % CODE
                    n_even, n_odd = e // 2 + 1, (e + 1) // 2
                    with pe.If(e % 2 < 1):
                        by_width(i, first, w_even, pairs, n_even, n_odd, WIDTHS)
                    with pe.Else():
                        by_width(i, first, w_odd, pairs, n_even, n_odd, WIDTHS)

                pe.sem_inc(gu_mm, 1)
                pe.sem_inc(dn_mm, 1)
                turn_x(0, True)
                over_chunks(pe, turn)

            @block.scalar
            def _(act):
                def copy_x(i):
                    act.wait_ge(x_turned, i + 1)
                    for s in range(2):
                        for half in range(2):
                            ins = nc.scalar.activation(xT[:, 4 * half:4 * half + 4, s * P:(s + 1) * P],
                                                       bank(4 + 2 * s + half).rearrange("p (k t) -> p k t", k=4), ACT.Copy)
                        ins.then_inc(x_cp, 1)

                def turn(i, first):
                    for f in range(KF):
                        act.wait_ge(gu_mm, 4 * i + f + 2)
                        if not (first and f < 2):
                            act.wait_ge(hid_rdy, 4 * i + f - 1)
                        nc.scalar.activation(ge[f % 2], bank(f % 2)[:, 0:CHUNK], ACT.Exp, scale=-1.0).then_inc(g_exp, 1)
                    copy_x(i + 1)
                    act.wait_ge(y_turned, 2 * i + 2)
                    if not first:
                        act.wait_ge(y_st[1], 16 * i)
                    for half in range(2):
                        ins = nc.scalar.activation(yo[1][:, half * BANK:(half + 1) * BANK], bank(6 + half), ACT.Copy)
                    ins.then_inc(y_rdy[1], 1)

                copy_x(0)
                over_chunks(act, turn)

            @block.vector
            def _(dve):
                def silu(i, f, first):
                    j = 4 * i + f
                    g, up = bank(f % 2)[:, 0:CHUNK], bank(f % 2)[:, CHUNK:2 * CHUNK]

                    def link(ins, n):
                        ins.then_inc(g_dve, 1)
                        dve.wait_ge(g_dve, 3 * j + n)

                    dve.wait_ge(g_exp, j + 1)
                    link(nc.vector.tensor_scalar(ge[f % 2], ge[f % 2], 1.0, None, ALU.add), 1)
                    link(nc.vector.reciprocal(ge[f % 2], ge[f % 2]), 2)
                    if not first:
                        dve.wait_ge(dn_mm, 4 * i + 1)
                    link(nc.vector.tensor_tensor(hidT[:, f, :], g, ge[f % 2], ALU.mult), 3)
                    nc.vector.tensor_tensor(hidT[:, f, :], hidT[:, f, :], up, ALU.mult).then_inc(hid_rdy, 1)

                def turn(i, first):
                    for f in range(KF):
                        silu(i, f, first)
                    if not first:
                        dve.wait_ge(y_turned, 2 * i)
                    for d in range(4):
                        dve.wait_ge(dn_mm, 4 * i + d + 2)
                        nc.vector.tensor_copy(yT[:, 2 * d:2 * d + 2, :], bank(2 + d % 2).rearrange("p (a t) -> p a t", a=2)).then_inc(yT_cp, 1)
                    dve.wait_ge(y_turned, 2 * i + 1)
                    if not first:
                        for s in range(2):
                            dve.wait_ge(y_st[s], 16 * i)
                    for half in range(2):
                        ins = nc.vector.tensor_copy(yo[0][:, half * BANK:(half + 1) * BANK], bank(4 + half))
                    ins.then_inc(y_rdy[0], 1)

                over_chunks(dve, turn)

        ar.at = after_x1
        assert mark_h + NT * D + 3 * D <= ar.at
        Y_RING = 6
        BATCH = 3
        ya, yb = ([ar.take([D]) for _ in range(Y_RING)] for _ in range(2))
        yg = [ar.take([D]) for _ in range(2)]
        z = [ar.take([D]) for _ in range(2)]
        junk = ar.take([D])
        fs = ar.take([4, NT])
        gates_rdy, mixed, z_rdy, z_sq, z_mean, z_guess, z_out, dve_f, act_f = (sem(n) for n in (
            "gates_prepared", "rows_mixed", "z_ready", "z_squares", "z_mean", "z_guess", "z_out", "dve_final", "act_final"))
        y_in = [sem(f"rows_in{s}") for s in range(Y_RING)]
        y_stored = [sem("y_out0"), sem("y_out1")]
        diag = [ar.take([2, P]) for _ in range(2)]

        pe_tiles = [t for t in range(NT) if t % 3 != 2]

        def prepare_gates(act, t):
            if t in pe_tiles:
                n_pe = pe_tiles.index(t)
                if n_pe >= 2:
                    act.wait_ge(mixed, n_pe - 1)
                for n in range(2):
                    ins = nc.scalar.activation(diag[n_pe % 2][:, n, :], ident, ACT.Copy, scale=gate[n][:, t:t + 1])
            else:
                act.wait_ge(y_in[t % Y_RING], 32 * (t // Y_RING + 1))
                ins = nc.scalar.activation(ya[t % Y_RING], ya[t % Y_RING], ACT.Copy, scale=gate[0][:, t:t + 1])
            ins.then_inc(gates_rdy, 1)

        with nc.Block() as block:
            @block.tensor
            def _(pe):
                for n_pe, t in enumerate(pe_tiles):
                    pe.wait_ge(gates_rdy, t + 1)
                    pe.wait_ge(y_in[t % Y_RING], 32 * (t // Y_RING + 1))
                    if n_pe >= 2:
                        pe.wait_ge(z_rdy, pe_tiles[n_pe - 2] + 1)
                    for half in range(2):
                        for n, y in enumerate((ya, yb)):
                            last = nc.tensor.matmul(bank(2 * (n_pe % 2) + half), diag[n_pe % 2][:, n, :], y[t % Y_RING][:, half * BANK:(half + 1) * BANK],
                                                    start=(n == 0), stop=(n == 1))
                    last.then_inc(mixed, 1)

            @block.sync
            def _(sp):
                for t in range(NT):
                    sp.wait_ge(z_out, t + 1)
                    sp.dma_start(y_all[t * P:(t + 1) * P, :], z[t % 2]).then_inc(y_stored[t % 2], 16)
                for s in range(2):
                    sp.wait_ge(y_stored[s], 16 * ((NT + 1 - s) // 2))
                sp.wait_ge(out_stored, stored[0])

            @block.gpsimd
            def _(pool):
                for t in range(NT):
                    if t >= Y_RING:
                        pool.wait_ge(z_rdy, t - Y_RING + 1)
                    for n, y in enumerate((ya, yb)):
                        pool.indirect_dma_start(y[t % Y_RING], None, slot_y, bass.IndirectOffsetOnAxis(slot[n].bitcast(U32)[:, t:t + 1], 0)).then_inc(y_in[t % Y_RING], 16)

            @block.scalar
            def _(act):
                st = Steps(act, act_f)

                for t in range(2):
                    prepare_gates(act, t)
                for t in range(NT):
                    if t + 2 < NT:
                        prepare_gates(act, t + 2)
                    act.wait_ge(z_rdy, t + 1)
                    st.link(nc.scalar.activation(junk, x1[:, t, :], ACT.Square, accum_out=fs[:, 0, t:t + 1]))
                    if t % BATCH == BATCH - 1:
                        b = slice(t - BATCH + 1, t + 1)
                        nc.scalar.activation(junk[:, 0:1], fs[:, 0, t:t + 1], ACT.Square).then_inc(z_sq, 1)
                        act.wait_ge(z_mean, t // BATCH + 1)
                        nc.scalar.activation(fs[:, 2, b], fs[:, 0, b], ACT.Sqrt).then_inc(z_guess, 1)

            @block.vector
            def _(dve):
                st = Steps(dve, dve_f)
                v = nc.vector

                def combine(t):
                    y = yg[t % 2]
                    if t >= 2:
                        dve.wait_ge(z_rdy, t - 1)
                    if t in pe_tiles:
                        n_pe = pe_tiles.index(t)
                        dve.wait_ge(mixed, n_pe + 1)
                        rows = ps[:, 2 * (n_pe % 2) * BANK:2 * (n_pe % 2) * BANK + D]
                    else:
                        rows = y
                        dve.wait_ge(gates_rdy, t + 1)
                        dve.wait_ge(y_in[t % Y_RING], 32 * (t // Y_RING + 1))
                        st.link(v.scalar_tensor_tensor(out=y, in0=yb[t % Y_RING], scalar=gate[1][:, t:t + 1], in1=ya[t % Y_RING], op0=ALU.mult, op1=ALU.add))
                    st.link(v.tensor_tensor(y, rows, g2[:, side(t), :], ALU.mult))
                    v.tensor_tensor(x1[:, t, :], y, x1[:, t, :], ALU.add).then_inc(z_rdy, 1)

                def mean(n):
                    b = slice(BATCH * n, BATCH * (n + 1))
                    dve.wait_ge(z_sq, n + 1)
                    v.tensor_scalar(fs[:, 0, b], fs[:, 0, b], 1.0 / D, EPS, ALU.mult, ALU.add).then_inc(z_mean, 1)

                def finish(n):
                    b = slice(BATCH * n, BATCH * (n + 1))
                    dve.wait_ge(z_guess, n + 1)
                    newton(st, fs[:, 2, b], fs[:, 3, b], fs[:, 0, b])
                    for t in range(BATCH * n, BATCH * (n + 1)):
                        if t >= 2:
                            dve.wait_ge(y_stored[t % 2], 16 * (t // 2))
                        v.scalar_tensor_tensor(out=z[t % 2], in0=x1[:, t, :], scalar=fs[:, 2, t:t + 1], in1=fn, op0=ALU.mult, op1=ALU.mult).then_inc(z_out, 1)

                dve.wait_ge(f_in, 32)
                assert NT % BATCH == 0
                for n in range(NT // BATCH):
                    for t in range(BATCH * n, BATCH * (n + 1)):
                        combine(t)
                        if n and t % BATCH == 0:
                            mean(n - 1)
                        if n and t % BATCH == 1:
                            finish(n - 1)
                mean(NT // BATCH - 1)
                finish(NT // BATCH - 1)


def constants():
    f = np.float32
    ident = np.eye(P, dtype=f)
    upper = np.triu(np.ones((P, P), f), 1)
    sel = np.zeros((P, 8, P), f)
    for way in range(2):
        for h in range(MH):
            sel[32 * way + h, MH * way + h, :] = 1
    s, t = np.arange(P)[:, None], np.arange(P)[None, :]
    scanmask = np.stack([np.where(s <= t, 0, NEG), np.where(s >= t, 0, NEG)]).astype(f)
    reset = np.ones((64, TOK), f)
    reset[:32, 0::P] = 0
    reset[32:, P - 1::P] = 0
    q = np.arange(GRID_W)
    start = np.clip(q - KCOLS // 2, 0, GRID_W - KCOLS)[:, None]
    k = np.arange(GRID_W)[None, :]
    window = np.where((k >= start) & (k < start + KCOLS), 0, NEG).astype(f)
    winmask = np.tile(window[None, :, None, :], (2, 1, TAB_SLOTS, 1))
    winmask[0, :, EDGE_SLOTS + 8:, :] = NEG
    winmask[1, :, EDGE_SLOTS, :] = NEG
    winmask[1, :, EDGE_SLOTS + 9, :] = NEG
    winmask = winmask.reshape(P, TAB_SLOTS, GRID_W)
    band = np.zeros((PG, 6, P, P), f)
    for g, w in enumerate(WINDOWS):
        for b, (lo_end, hi_end) in enumerate(((False, False), (True, False), (False, True), (True, True))):
            for tt in range(P):
                lo, hi = tt - w // 2, tt - w // 2 + w
                n_lo, n_hi = max(lo, 0) if lo_end else lo, min(hi, P) if hi_end else hi
                band[g, b, max(lo, 0):min(hi, P), tt] = f(1) / f(n_hi - n_lo)
                band[g, b, tt, tt] -= 1
                if b == 0:
                    if lo < 0:
                        band[g, 4, P + lo:P, tt] = f(1) / f(w)
                    if hi > P:
                        band[g, 5, 0:hi - P, tt] = f(1) / f(w)
    return {"k_ident": ident, "k_upper": upper, "k_sel": sel, "k_scanmask": np.ascontiguousarray(scanmask.transpose(1, 0, 2)), "k_reset": reset,
            "k_winmask": winmask, "k_band": np.ascontiguousarray(band.reshape(PG * 6, P, P).transpose(1, 0, 2)), "k_chunk_ids": np.arange(CHUNKS, dtype=f),
            "k_token_ids": np.arange(TOK, dtype=f).reshape(NT, P).T.copy()}


def kernel(**inputs):
    import concourse.bacc as bacc
    from concourse.bass_utils import run_bass_kernel_spmd as run

    a = {k: np.ascontiguousarray(v) for k, v in inputs.items()}
    ins = {
        "x_all": np.concatenate([a["x_sample"].reshape(LAT, D), a["x_prompt"].reshape(CTX, D)]),
        "cache_k": a["cache_k_attn"].reshape(CTX, AW), "cache_v": a["cache_v_attn"].reshape(CTX, AW),
        "state_C": a["state_mlstm_C"].reshape(2, MH, MD, MD), "state_n": a["state_mlstm_n"].reshape(2, MH, MD),
        "state_m": a["state_mlstm_m"].reshape(2, MH), "c_both": np.stack([a["c"].reshape(D), a["c_ctx"].reshape(D)]),
        "w_ada": a["w_ada"].reshape(D, 6 * D), "b_ada": a["b_ada"].reshape(6 * D), "norm1": a["norm1"].reshape(D),
        "w_in": a["w_in"].reshape(D, -1), "b_in": a["b_in"].reshape(-1),
        "rpb_pad": np.pad(a["rpb"].reshape(HEADS, RPB_R, RPB_C), ((0, 0), (0, 0), (GRID_W - KCOLS, GRID_W - KCOLS))),
        "ml_norm": a["ml_norm"].reshape(MW), "w_pool": a["w_pool"].reshape(PG, PD, PD), "pool_scale": a["pool_scale"].reshape(PW),
        "w_out": a["w_out"].reshape(D, D), "norm2": a["norm2"].reshape(D), "w_router": a["w_router"], "b_router": a["b_router"],
        "w_gate": a["w_gate"].reshape(NE, D, DF), "w_up": a["w_up"].reshape(NE, D, DF), "w_down": a["w_down"].reshape(NE, DF, D),
        "final_norm": a["final_norm"], **constants(),
    }
    outs = {"y_all": (TOK, D), "out_k": (CTX, AW), "out_v": (CTX, AW), "out_C": (2, MH, MD, MD), "out_n": (2, MH, MD), "out_m": (2, MH)}
    nc = bacc.Bacc("TRN2", target_bir_lowering=False, num_devices=1)
    aps = {k: nc.dram_tensor("in_" + k, v.shape, F32, kind="ExternalInput").ap() for k, v in ins.items()}
    aps |= {k: nc.dram_tensor(k, s, F32, kind="ExternalOutput").ap() for k, s in outs.items()}
    program(nc, **aps)
    r = run(nc, [{"in_" + k: v for k, v in ins.items()}], core_ids=[0]).results[0]
    y = r["y_all"]
    return (y[LAT:].reshape(1, CTX, D), y[:LAT].reshape(1, LAT, D),
            r["out_k"].reshape(1, 1, CTX, HEADS, HD), r["out_v"].reshape(1, 1, CTX, HEADS, HD),
            r["out_C"].reshape(1, 1, 2, MH, MD, MD), r["out_n"].reshape(1, 1, 2, MH, MD), r["out_m"].reshape(1, 1, 2, MH))
```
